# Optimizing a Trainium2 kernel written in Bass

```python
import jax, jax.numpy as jnp
from jax import lax
import numpy as np

D_MODEL = 1024
BATCH = 1
SEQ = 256
DEPTH = 2
DEC_BATCH = 8
DEC_SEQ = 16
PAST_LEN = 512

CHUNK = 64
Q_BLOCK = 128
HEAD_DIM = 64
H_SB = 6
H_FOX = 6
H_DSA = 6
MIX_W = 6 * 64
IDX_HEADS = 4
IDX_DIM = 64
TOPK_MAX = 256
N_BRANCH = 3
D_FF = 2816
ROPE_THETA = 10000.0
EPS = 1e-6
FFN_RES = 0.5
N_MOD = 9
N_NORM = 6
SPLIT_SIZES = (3 * MIX_W, 3 * MIX_W, H_FOX, 3 * MIX_W, IDX_HEADS * IDX_DIM, IDX_DIM, IDX_HEADS, N_BRANCH * D_MODEL)
N_IN = 9 * MIX_W + H_FOX + IDX_HEADS * IDX_DIM + IDX_DIM + IDX_HEADS + N_BRANCH * D_MODEL

kernel_name = 'hybrid_streaming_sb_fox_dsa_step'

def rmsnorm(x, g):
    xf = x.astype(jnp.float32)
    y = xf * lax.rsqrt(jnp.mean(xf * xf, axis=-1, keepdims=True) + EPS)
    return (y * g.astype(jnp.float32)).astype(x.dtype)

def rotary(x, pos):
    half = x.shape[-1] // 2
    inv_freq = ROPE_THETA ** (-jnp.arange(half, dtype=jnp.float32) / half)
    ang = pos.astype(jnp.float32)[:, None] * inv_freq[None, :]
    cos = jnp.cos(ang)[None, :, None, :]
    sin = jnp.sin(ang)[None, :, None, :]
    xf = x.astype(jnp.float32)
    x1, x2 = xf[..., :half], xf[..., half:]
    return jnp.concatenate([x1 * cos - x2 * sin, x1 * sin + x2 * cos], axis=-1).astype(x.dtype)

def block_map(fn, q_args, q_pos):
    tq = q_pos.shape[0]
    qb = min(Q_BLOCK, tq)
    nb = tq // qb

    def split(a):
        return jnp.moveaxis(a.reshape(a.shape[0], nb, qb, *a.shape[2:]), 1, 0)

    xs = tuple(split(a) for a in q_args) + (q_pos.reshape(nb, qb),)
    out = lax.map(lambda args: fn(*args), xs)
    out = jnp.moveaxis(out, 0, 1)
    return out.reshape(out.shape[0], tq, *out.shape[3:])

def stick_breaking_attention(q, k, v, q_pos, k_pos):
    scale = HEAD_DIM ** -0.5

    def block(qb_, qp):
        z = jnp.einsum('bqhd,bkhd->bhqk', qb_, k).astype(jnp.float32) * scale
        mask = k_pos[None, :] < qp[:, None]
        log_keep = jnp.where(mask, jax.nn.log_sigmoid(-z), 0.0)
        suffix = lax.cumsum(log_keep, axis=3, reverse=True) - log_keep
        a = jnp.where(mask, jnp.exp(jax.nn.log_sigmoid(z) + suffix), 0.0)
        return jnp.einsum('bhqk,bkhd->bqhd', a.astype(v.dtype), v)

    return block_map(block, (q,), q_pos)

def forgetting_attention(q, k, v, g_q, g_k, q_pos, k_pos):
    scale = HEAD_DIM ** -0.5
    g_kt = jnp.swapaxes(g_k, 1, 2)

    def block(qb_, gq, qp):
        s = jnp.einsum('bqhd,bkhd->bhqk', qb_, k).astype(jnp.float32) * scale
        s = s + g_kt[:, :, None, :] - jnp.swapaxes(gq, 1, 2)[:, :, :, None]
        mask = k_pos[None, :] <= qp[:, None]
        p = jax.nn.softmax(jnp.where(mask, s, -jnp.inf), axis=-1)
        return jnp.einsum('bhqk,bkhd->bqhd', p.astype(v.dtype), v)

    return block_map(block, (q, g_q), q_pos)

def dsa_attention(q, k, v, q_idx, w_idx, k_idx, q_pos, k_pos):
    scale = HEAD_DIM ** -0.5
    topk = min(TOPK_MAX, k.shape[1] // 4)

    def block(qb_, qib, wib, qp):
        isc = jnp.einsum('bqhd,bkd->bqhk', qib, k_idx).astype(jnp.float32) * (IDX_DIM ** -0.5)
        isc = jnp.einsum('bqhk,bqh->bqk', jax.nn.relu(isc), wib.astype(jnp.float32)) * (IDX_HEADS ** -0.5)
        allowed = (k_pos[None, :] // CHUNK) <= (qp[:, None] // CHUNK)
        isc = jnp.where(allowed[None], isc, -jnp.inf)
        vals, idx = lax.top_k(isc, topk)
        valid = vals > -jnp.inf
        k_sel = jax.vmap(lambda kb, ib: kb[ib])(k, idx)
        v_sel = jax.vmap(lambda vb, ib: vb[ib])(v, idx)
        s = jnp.einsum('bqhd,bqkhd->bhqk', qb_, k_sel).astype(jnp.float32) * scale
        p = jax.nn.softmax(jnp.where(valid[:, None], s, -jnp.inf), axis=-1)
        return jnp.einsum('bhqk,bqkhd->bqhd', p.astype(v.dtype), v_sel)

    return block_map(block, (q, q_idx, w_idx), q_pos)

def swiglu(h, w_up, w_down):
    g, u = jnp.split(h @ w_up, 2, axis=-1)
    return (jax.nn.silu(g) * u) @ w_down

def token_mixing(h, pos, past, w_in, b_forget, w_branch, w_out):
    b, t, _ = h.shape
    offs = np.cumsum(SPLIT_SIZES)[:-1].tolist()
    qkv_sb, qkv_fox, f_logit, qkv_dsa, q_idx, k_idx, w_idx, gate_logit = jnp.split(h @ w_in, offs, axis=-1)
    q_sb, k_sb, v_sb = (a.reshape(b, t, H_SB, HEAD_DIM) for a in jnp.split(qkv_sb, 3, axis=-1))
    q_fox, k_fox, v_fox = (a.reshape(b, t, H_FOX, HEAD_DIM) for a in jnp.split(qkv_fox, 3, axis=-1))
    q_dsa, k_dsa, v_dsa = (a.reshape(b, t, H_DSA, HEAD_DIM) for a in jnp.split(qkv_dsa, 3, axis=-1))
    log_f = jax.nn.log_sigmoid(f_logit + b_forget)
    q_dsa = rotary(q_dsa, pos)
    k_dsa = rotary(k_dsa, pos)
    q_idx = rotary(q_idx.reshape(b, t, IDX_HEADS, IDX_DIM), pos)
    k_idx = rotary(k_idx[:, :, None, :], pos)[:, :, 0, :]
    new = (k_sb, v_sb, k_fox, v_fox, log_f, k_dsa, v_dsa, k_idx)
    if past is None:
        full = new
        k_pos = pos
    else:
        full = tuple(jnp.concatenate([p_, n_], axis=1) for p_, n_ in zip(past, new))
        k_pos = jnp.concatenate([jnp.arange(past[0].shape[1], dtype=jnp.int32), pos])
    ks_sb, vs_sb, ks_fox, vs_fox, lf_all, ks_dsa, vs_dsa, ks_idx = full
    lf = lf_all.astype(jnp.float32)
    g_all = lax.cumsum(lf, axis=1, reverse=True) - lf
    o_sb = stick_breaking_attention(q_sb, ks_sb, vs_sb, pos, k_pos)
    o_fox = forgetting_attention(q_fox, ks_fox, vs_fox, g_all[:, -t:], g_all, pos, k_pos)
    o_dsa = dsa_attention(q_dsa, ks_dsa, vs_dsa, q_idx, w_idx, ks_idx, pos, k_pos)
    y = jnp.stack([o.reshape(b, t, MIX_W) for o in (o_sb, o_fox, o_dsa)], axis=2)
    y = jnp.einsum('btnc,ncd->btnd', y, w_branch)
    gates = jax.nn.sigmoid(gate_logit.reshape(b, t, N_BRANCH, D_MODEL))
    merged = jnp.sum(gates * y, axis=2)
    return merged @ w_out, new

def trunk(x, c, pos, caches, norm_g, w_ada, b_ada, ffn_w_in, ffn_w_out, w_in, b_forget, w_branch, w_out):
    layer_states = []
    for l in range(DEPTH):
        mod = (jax.nn.silu(c) @ w_ada[l] + b_ada[l]).reshape(c.shape[0], N_MOD, D_MODEL)[:, :, None, :]
        h = rmsnorm(x, norm_g[l, 0]) * (1.0 + mod[:, 1]) + mod[:, 0]
        x = x + FFN_RES * mod[:, 2] * rmsnorm(swiglu(h, ffn_w_in[l, 0], ffn_w_out[l, 0]), norm_g[l, 1])
        h = rmsnorm(x, norm_g[l, 2]) * (1.0 + mod[:, 4]) + mod[:, 3]
        past = None if caches is None else tuple(a[l] for a in caches)
        h, st = token_mixing(h, pos, past, w_in[l], b_forget[l], w_branch[l], w_out[l])
        x = x + mod[:, 5] * rmsnorm(h, norm_g[l, 3])
        h = rmsnorm(x, norm_g[l, 4]) * (1.0 + mod[:, 7]) + mod[:, 6]
        x = x + FFN_RES * mod[:, 8] * rmsnorm(swiglu(h, ffn_w_in[l, 1], ffn_w_out[l, 1]), norm_g[l, 5])
        layer_states.append(st)
    states = tuple(jnp.stack(s, axis=0) for s in zip(*layer_states))
    return x, states

def setup_inputs(seed: int = 0) -> dict:
    key = jax.random.key(seed)
    ks = jax.random.split(key, 21)

    def nrm(k, shape):
        return jax.random.normal(k, shape, dtype=jnp.float32)

    kv_sb = (DEPTH, DEC_BATCH, PAST_LEN, H_SB, HEAD_DIM)
    kv_fox = (DEPTH, DEC_BATCH, PAST_LEN, H_FOX, HEAD_DIM)
    kv_dsa = (DEPTH, DEC_BATCH, PAST_LEN, H_DSA, HEAD_DIM)
    return {
        'x_prompt': nrm(ks[0], (BATCH, SEQ, D_MODEL)),
        'x_sample': nrm(ks[1], (DEC_BATCH, DEC_SEQ, D_MODEL)),
        'cache_sb_k': nrm(ks[2], kv_sb),
        'cache_sb_v': nrm(ks[3], kv_sb),
        'cache_fox_k': nrm(ks[4], kv_fox),
        'cache_fox_v': nrm(ks[5], kv_fox),
        'cache_fox_logf': jax.nn.log_sigmoid(1.0 + 0.5 * nrm(ks[6], (DEPTH, DEC_BATCH, PAST_LEN, H_FOX))),
        'cache_dsa_k': nrm(ks[7], kv_dsa),
        'cache_dsa_v': nrm(ks[8], kv_dsa),
        'cache_dsa_kidx': nrm(ks[9], (DEPTH, DEC_BATCH, PAST_LEN, IDX_DIM)),
        'c_prompt': nrm(ks[10], (BATCH, D_MODEL)),
        'c_sample': nrm(ks[11], (DEC_BATCH, D_MODEL)),
        'norm_g': 1.0 + 0.05 * nrm(ks[12], (DEPTH, N_NORM, D_MODEL)),
        'w_ada': nrm(ks[13], (DEPTH, D_MODEL, N_MOD * D_MODEL)) * (0.5 * D_MODEL ** -0.5),
        'b_ada': 0.02 * nrm(ks[14], (DEPTH, N_MOD * D_MODEL)),
        'ffn_w_in': nrm(ks[15], (DEPTH, 2, D_MODEL, 2 * D_FF)) * D_MODEL ** -0.5,
        'ffn_w_out': nrm(ks[16], (DEPTH, 2, D_FF, D_MODEL)) * D_FF ** -0.5,
        'w_in': nrm(ks[17], (DEPTH, D_MODEL, N_IN)) * D_MODEL ** -0.5,
        'b_forget': 1.0 + 0.1 * nrm(ks[18], (DEPTH, H_FOX)),
        'w_branch': nrm(ks[19], (DEPTH, N_BRANCH, MIX_W, D_MODEL)) * MIX_W ** -0.5,
        'w_out': nrm(ks[20], (DEPTH, D_MODEL, D_MODEL)) * D_MODEL ** -0.5,
    }

def reference(x_prompt, x_sample, cache_sb_k, cache_sb_v, cache_fox_k, cache_fox_v, cache_fox_logf,
              cache_dsa_k, cache_dsa_v, cache_dsa_kidx, c_prompt, c_sample,
              norm_g, w_ada, b_ada, ffn_w_in, ffn_w_out, w_in, b_forget, w_branch, w_out):
    pos_p = jnp.arange(x_prompt.shape[1], dtype=jnp.int32)
    pos_s = cache_sb_k.shape[2] + jnp.arange(x_sample.shape[1], dtype=jnp.int32)
    y_prompt, st_p = trunk(x_prompt, c_prompt, pos_p, None,
                           norm_g, w_ada, b_ada, ffn_w_in, ffn_w_out, w_in, b_forget, w_branch, w_out)
    caches = (cache_sb_k, cache_sb_v, cache_fox_k, cache_fox_v, cache_fox_logf,
              cache_dsa_k, cache_dsa_v, cache_dsa_kidx)
    y_sample, st_s = trunk(x_sample, c_sample, pos_s, caches,
                           norm_g, w_ada, b_ada, ffn_w_in, ffn_w_out, w_in, b_forget, w_branch, w_out)
    sb_k_p, sb_v_p, fox_k_p, fox_v_p, fox_logf_p, dsa_k_p, dsa_v_p, dsa_kidx_p = st_p
    sb_k_s, sb_v_s, fox_k_s, fox_v_s, fox_logf_s, dsa_k_s, dsa_v_s, dsa_kidx_s = st_s
    return (y_prompt, y_sample,
            sb_k_p, sb_v_p, fox_k_p, fox_v_p, fox_logf_p, dsa_k_p, dsa_v_p, dsa_kidx_p,
            sb_k_s, sb_v_s, fox_k_s, fox_v_s, fox_logf_s, dsa_k_s, dsa_v_s, dsa_kidx_s)


_drawn_inputs = setup_inputs


def setup_inputs(seed=0):
    import zlib

    import numpy as np

    out = dict(_drawn_inputs(seed))
    spreads = {}
    factors = {}
    for name, (base, spread) in spreads.items():
        noise = np.random.default_rng([zlib.crc32(name.encode()), seed]).standard_normal(out[name].shape)
        drawn = base * np.exp(spread * noise) if base else spread * noise
        out[name] = __import__('jax').numpy.asarray(drawn.astype(out[name].dtype))
    for name, factor in factors.items():
        out[name] = (out[name] * factor).astype(out[name].dtype)
    return out
```

```python
import concourse.bass as bass
from concourse import mybir
from contextlib import ExitStack, contextmanager

ALU = mybir.AluOpType
ACT = mybir.ActivationFunctionType
AXX = mybir.AxisListType.X
F32 = mybir.dt.float32

P = 128
D = 1024
KD = D // P
NPROMPT = 256
NB = 8
NT = 16
NSAMPLE = NB * NT
T = NPROMPT + NSAMPLE
TT = T // P
DEPTH = 2
PAST = 512
KEYS = PAST + NT
PC = PAST // P
NH = 6
HD = 64
NPAIR = NH // 2
MIX = NH * HD
NBR = 3
SB, FOX, DSA = range(NBR)
IH = 4
FF = 2816
NFF = FF // P
NC = 9
NMOD = 9
EPS = 1e-6
SCALE = HD ** -0.5
TOPK_P = NPROMPT // 4
TOPK_S = KEYS // 4
NEG = -1e30
TAKEN = -3e38

COL_QKV = [0, 3 * MIX, 6 * MIX + NH]
COL_F = 6 * MIX
COL_IDX = 9 * MIX + NH
NIDX = IH * HD + HD + IH
COL_GATE = COL_IDX + NIDX

N_ADA, N_IN, N_OUT, N_PROJ, N_GATE, N_BRANCH, N_WOUT = 18, 11, 8, 10, 8, 4, 2
U_ADA = 0
U_IN = [U_ADA + N_ADA, 0]
U_OUT = [U_IN[0] + N_IN, 0]
U_PROJ = U_OUT[0] + N_OUT
U_GATE = U_PROJ + N_PROJ
U_BRANCH = U_GATE + N_GATE
U_WOUT = U_BRANCH + N_BRANCH
U_IN[1] = U_WOUT + N_WOUT
U_OUT[1] = U_IN[1] + N_IN
UNITS = U_OUT[1] + N_OUT
assert UNITS % 2 == 0

Y_BASE = [0, 2 * KD, KD]
NSTEP = NB * NBR


def program(nc, t):
    with ExitStack() as ctx:
        def sb(name, width):
            return ctx.enter_context(nc.sbuf_tensor(name, [P, width], F32))

        def sem(name):
            return ctx.enter_context(nc.semaphore(name))

        X = sb("X", KD * T)[:, :].rearrange("p (k t) -> p k t", k=KD)
        H = sb("H", KD * T)[:, :].rearrange("p (k t) -> p k t", k=KD)
        BIG = sb("BIG", 9400)
        QR = sb("QR", 12960)
        RING = sb("RING", 2 * 4096)
        QKT = sb("QKT", NBR * 2 * NPAIR * NPROMPT)[:, :].rearrange(
            "p (r i a t) -> p r i a t", r=NBR, i=2, a=NPAIR)
        QBLK = sb("QBLK", NBR * NPAIR * NB * 32)[:, :].rearrange(
            "p (r a b c) -> p r a b c", r=NBR, a=NPAIR, b=NB)
        OT = sb("OT", NBR * NPAIR * T)[:, :].rearrange("p (g t) -> p g t", t=T)
        MOD = sb("MOD", NMOD * KD * NC)[:, :].rearrange("p (m c) -> p m c", c=NC)
        BGR = sb("BGR", P)
        BG = sb("BG", 120)
        MASKS = sb("MASKS", 3 * 2 * NPROMPT)[:, :].rearrange("p (r q k) -> p r q k", r=3, q=2)
        IDENT = sb("IDENT", P)
        ONES = sb("ONES", P)
        ROPE = sb("ROPE", TT * 2 * 32)[:, :].rearrange("p (t s d) -> p t s d", t=TT, s=2)
        ZERO = sb("ZERO", KEYS)
        BSB = sb("BSB", KEYS)
        MFOX = sb("MFOX", NT)
        RSTD = sb("RSTD", T)
        VAR = sb("VAR", T)
        CT = sb("CT", KD * NC)[:, :].rearrange("p (k c) -> p k c", c=NC)
        DMB = sb("DMB", 2 * NPROMPT)[:, :].rearrange("p (q k) -> p q k", q=2)
        QC = sb("QC", 2 * 96)[:, :].rearrange("p (s c) -> p s c", s=2)
        ST = sb("ST", 64)
        LF = sb("LF", 3 * TT * NH)[:, :].rearrange("p (s t h) -> p s t h", s=3, t=TT)
        BF = sb("BF", NH)
        FREG = sb("FREG", TT * 8)[:, :].rearrange("p (t h) -> p t h", t=TT)

        def big(off, n):
            return BIG[:, off:off + n]

        def qr(off, n):
            return QR[:, off:off + n]

        HID = big(0, NFF * T).rearrange("p (j t) -> p j t", t=T)
        G = big(0, 24 * T).rearrange("p (j t) -> p j t", t=T)
        Y = qr(0, KD * T).rearrange("p (k t) -> p k t", t=T)
        SQ = qr(3072, KD * T).rearrange("p (k t) -> p k t", t=T)
        MG = qr(6144, KD * T).rearrange("p (k t) -> p k t", t=T)
        MGT = qr(9216, T)
        FE = qr(6144, 2 * T).rearrange("p (j t) -> p j t", t=T)
        FT = qr(6144 + 2 * T, 2 * T).rearrange("p (j t) -> p j t", t=T)
        QKV = qr(0, NBR * TT * 3 * MIX).rearrange("p (r t c) -> p r t c", r=NBR, t=TT)
        QX = NBR * TT * 3 * MIX
        assert QX == 10368
        GS, GX, LFC = qr(QX, KEYS), qr(QX + KEYS, KEYS), qr(QX + 2 * KEYS, PC * 48)
        RT = qr(QX, 2304)
        RL, ISC, WK = qr(QX, 1024), qr(QX + 1024, KEYS), qr(QX + 1024 + KEYS, KEYS)
        M8 = ST[:, 56:64]
        IDX = big(0, TT * NIDX).rearrange("p (t c) -> p t c", t=TT)
        o = TT * NIDX
        KI2 = big(o, TT * P).rearrange("p (t c) -> p t c", t=TT); o += TT * P
        QI2 = big(o, IH * P).rearrange("p (h c) -> p h c", h=IH); o += IH * P
        KIC = big(o, PC * NB * HD).rearrange("p (c w) -> p c w", c=PC); o += PC * NB * HD
        KIT = big(o, 4 * KEYS).rearrange("p (b k) -> p b k", b=4); o += 4 * KEYS
        QIP = big(o, IH * 640).rearrange("p (h c) -> p h c", h=IH); o += IH * 640
        QIT = big(o, 2 * NPROMPT).rearrange("p (a t) -> p a t", a=2); o += 2 * NPROMPT
        KITP = big(o, NPROMPT); o += NPROMPT
        assert o <= 9400
        ZP, EP, LP = (big(i * 1536, 1536).rearrange("p (h k) -> p h k", h=NH) for i in range(3))
        PTP = big(3 * 1536, 1536).rearrange("p (h k q) -> p h k q", h=NH, k=2)
        GB = big(4 * 1536, 1536).rearrange("p (h k) -> p h k", h=NH)
        KC = qr(0, 3840).rearrange("p (s c w) -> p s c w", s=2, c=PC + 1)
        VC = qr(3840, 3840).rearrange("p (s c w) -> p s c w", s=2, c=PC + 1)
        KT = qr(7680, NPAIR * KEYS).rearrange("p (a k) -> p a k", a=NPAIR)
        o = 7680 + NPAIR * KEYS
        ZS, ES, LS, BFX, BDX = (qr(o + i * KEYS, KEYS) for i in range(5))
        PTS = qr(o + 5 * KEYS, 480).rearrange("p (c q) -> p c q", q=96)
        o += 5 * KEYS + 480
        assert o <= 12960

        def by_parity(ap, h, heads, width):
            n = (h % 2) * (heads // 2) + h // 2
            return ap[:, n * width:(n + 1) * width]

        def ring(s, k, w):
            return RING[:, s * 4096:s * 4096 + k * w].rearrange("p (k w) -> p k w", w=w)

        PS = ctx.enter_context(nc.psum_tensor("PS", [P, 8, 512], F32))

        g_s = nc.dram_tensor("scr_g_sample", (NB * NH, KEYS), F32, kind="Internal").ap()
        g_p = nc.dram_tensor("scr_g_prompt", (NH, NPROMPT), F32, kind="Internal").ap()
        m_s = nc.dram_tensor("scr_mask_sample", (NSAMPLE, KEYS), F32, kind="Internal").ap()

        in_x, in_c, in_k = sem("in_x"), sem("in_c"), sem("in_k")
        c_act, c_silu, c_ready, ct_ready = sem("c_act"), sem("c_silu"), sem("c_ready"), sem("ct_ready")
        xt_ready, xt_free, x_turned = sem("xt_ready"), sem("xt_free"), sem("x_turned")
        settled = sem("settled")
        vch, ach = sem("vector_chain"), sem("scalar_chain")
        slot_full = [sem("slot_full0"), sem("slot_full1")]
        bg_full, bg_ready, bg_free = sem("bg_full"), sem("bg_ready"), sem("bg_free")
        mod_ready, mod_free, coef_ready = sem("mod_ready"), sem("mod_free"), sem("coef_ready")
        sq_ready, ms_ready, var_ready, rstd_ready = sem("sq_ready"), sem("ms_ready"), sem("var_ready"), sem("rstd_ready")
        xr_ready, hp_ready, hs_ready, x_ready = sem("xr_ready"), sem("hp_ready"), sem("hs_ready"), sem("x_ready")
        gu_ready, eg_ready, gu_free, half_used = sem("gu_ready"), sem("eg_ready"), sem("gu_free"), sem("half_used")
        y_ready, y_free = sem("y_ready"), sem("y_free")
        p_ready, p_free = sem("p_ready"), sem("p_free")
        rope_done, logf_exp, logf_ready = sem("rope_done"), sem("logf_exp"), sem("logf_ready")
        logf_arg = sem("logf_arg")
        stored, nf_stored, kidx_stored = sem("stored"), sem("nf_stored"), sem("kidx_stored")
        qk_ready, qk_free = sem("qk_ready"), sem("qk_free")
        bf_full, gc_full, gn_full = sem("bf_full"), sem("gc_full"), sem("gn_full")
        gt_ready, gt_copied, g_ready, g_stored, gb_full = sem("gt_ready"), sem("gt_copied"), sem("g_ready"), sem("g_stored"), sem("gb_full")
        ki_full, dup_ready = sem("ki_full"), sem("dup_ready")
        it_ready, it_free, qip_zero = sem("it_ready"), sem("it_free"), sem("qip_zero")
        is_ready, relu_ready, relu_free, is_done = sem("is_ready"), sem("relu_ready"), sem("relu_free"), sem("is_done")
        msk_ready, msk_stored = sem("msk_ready"), sem("msk_stored")
        s_ready, z_ready, z_used, e_ready = sem("ps_ready"), sem("pz_ready"), sem("pz_used"), sem("pe_ready")
        soft_ready, p_done, pt_ready, pt_copied = sem("psoft_ready"), sem("p_probs_ready"), sem("ppt_ready"), sem("ppt_copied")
        po_ready, po_copied = sem("ppo_ready"), sem("ppo_copied")
        k_full = [sem("k_full0"), sem("k_full1")]
        v_full = [sem("v_full0"), sem("v_full1")]
        k_used, o_ready, o_free = sem("k_used"), sem("o_ready"), sem("o_free")
        kt_ready, kt_free = sem("kt_ready"), sem("kt_free")
        qc_ready, ss_ready, zs_ready, es_ready = sem("qc_ready"), sem("ss_ready"), sem("zs_ready"), sem("es_ready")
        ls_ready, ps_ready = sem("ls_ready"), sem("sprobs_ready")
        st_ready, st_copied = sem("st_ready"), sem("st_copied")
        bfx_full, bdx_full = sem("bfx_full"), sem("bdx_full")
        gate_ready, gexp_ready, gate_free = sem("gate_ready"), sem("gexp_ready"), sem("gate_free")
        br_ready, br_free, mg_ready = sem("br_ready"), sem("br_free"), sem("mg_ready")
        out_ready, out_stored = sem("out_ready"), sem("out_stored")

        block = ctx.enter_context(nc.Block())

        def settle(eng):
            eng.sem_inc(settled, 1)

        @contextmanager
        def loop(eng, start, end):
            settle(eng)
            with eng.Fori(start, end) as i:
                yield i

        def chained(eng, chain):
            n = [0]

            def begin():
                settle(eng)
                eng.sem_clear(chain)
                n[0] = 0

            def link(ins):
                n[0] += 1
                ins.then_inc(chain, 1)
                eng.wait_ge(chain, n[0])
            return begin, link

        def per_conditioning(ap, kc=None):
            a = ap[:, :, 1:NC] if kc is None else ap[:, kc, 1:NC]
            return a[..., None].to_broadcast([P, KD, NB, NT]) if kc is None else a[..., None].to_broadcast([P, NB, NT])

        def sample_cols(ap):
            return ap[:, :, NPROMPT:T].rearrange("p k (b t) -> p k b t", b=NB)

        @contextmanager
        def by_two(eng, start, end):
            with loop(eng, start // 2, end // 2) as half:
                yield half * 2

        def sweep(eng, step):
            step(0, 0, lagged=False)
            with by_two(eng, 0, NB - 2) as b0:
                for j in range(1, 7):
                    step(b0, j)
            for j in range(1, 6):
                step(NB - 2, j)

        @block.sync
        def _(sp):
            sp.dma_start(qr(0, 2048).rearrange("p (t d) -> p t d", t=2),
                         t["x_prompt"].rearrange("o (t p) d -> p (o t) d", p=P)).then_inc(in_x, 16)
            sp.dma_start(qr(2048, 1024), t["x_sample"].rearrange("b t d -> (b t) d")).then_inc(in_x, 16)
            sp.dma_start(BIG[0:1, 0:D], t["c_prompt"]).then_inc(in_c, 16)
            sp.dma_start(BIG[1:NC, 0:D], t["c_sample"]).then_inc(in_c, 16)
            sp.dma_start(MASKS, t["k_masks"]).then_inc(in_k, 16)
            sp.dma_start(IDENT[:, :], t["k_ident"]).then_inc(in_k, 16)
            sp.dma_start(ROPE, t["k_rope"]).then_inc(in_k, 16)
            sp.dma_start(BSB[0:96, :], t["k_bsb"]).then_inc(in_k, 16)
            sp.dma_start(MFOX[0:96, :], t["k_mfox"]).then_inc(in_k, 16)

            def load(u, parts):
                s = u % 2
                for dst, src in parts:
                    sp.dma_start(dst, src).then_inc(slot_full[s], 16)

            def ffn_in(l, f, u, i):
                w = t["ffn_w_in"][l, f].rearrange("(k p) n -> p k n", p=P)
                d = ring(u % 2, KD, 512)
                return [(d[:, :, 0:256], w[:, :, bass.ds(i * 256, 256)]),
                        (d[:, :, 256:512], w[:, :, bass.ds(i * 256 + FF, 256)])]

            def ffn_out(l, f, u, mp, half):
                w = t["ffn_w_out"][l, f].rearrange("(k p) n -> p k n", p=P)
                d = ring(u % 2, NFF // 2, 256)
                k0 = half * (NFF // 2)
                return [(d[:, a:b, :], w[:, k0 + a:k0 + b, bass.ds(mp * 256, 256)]) for a, b in ((0, 6), (6, 11))]

            def by_k(u, w, col, width, k=KD):
                d = ring(u % 2, k, width)
                h = k // 2
                return [(d[:, a:b, :], w[:, a:b, bass.ds(col, width)]) for a, b in ((0, h), (h, k))]

            def swiglu_weights(l, f, before):
                u = U_IN[f]
                for i in range(2):
                    before[i]()
                    load(u + i, ffn_in(l, f, u + i, i))
                with by_two(sp, 2, 10) as i:
                    for j in range(2):
                        sp.wait_ge(gu_ready, l * 44 + i * 2 + (22 * f + 2 * j - 2))
                        load(u + j, ffn_in(l, f, u + j, i + j))
                sp.wait_ge(gu_ready, l * 44 + (22 * f + 18))
                load(u + 10, ffn_in(l, f, u + 10, 10))
                u = U_OUT[f]
                sp.wait_ge(gu_ready, l * 44 + (22 * f + 20))
                load(u, ffn_out(l, f, u, 0, 0))
                sp.wait_ge(gu_ready, l * 44 + (22 * f + 22))
                load(u + 1, ffn_out(l, f, u + 1, 0, 1))
                with loop(sp, 1, 4) as mp:
                    sp.wait_ge(half_used, l * 8 + mp + 4 * f)
                    load(u, ffn_out(l, f, u, mp, 0))
                    sp.wait_ge(y_ready, l * 24 + mp * 2 + Y_BASE[f])
                    load(u + 1, ffn_out(l, f, u + 1, mp, 1))

            with sp.Fori(0, DEPTH) as l:
                sp.wait_ge(bg_free, l + 1)
                sp.dma_start(BGR[0:72, :], t["b_ada"][l].rearrange("(m p) -> m p", p=P)).then_inc(bg_full, 16)
                sp.dma_start(BGR[72:120, :], t["norm_g"][l].rearrange("n (k p) -> (n k) p", p=P)).then_inc(bg_full, 16)
                sp.dma_start(BF[:, :], t["b_forget"][bass.ds(l, 1), :].to_broadcast([P, NH])).then_inc(bf_full, 16)
                w = t["w_ada"][l].rearrange("(k p) n -> p k n", p=P)
                sp.wait_ge(y_free, l * 24 + 2)
                for i in range(2):
                    load(i, by_k(i, w, i * 512, 512))
                with by_two(sp, 2, N_ADA) as i:
                    for j in range(2):
                        sp.wait_ge(mod_ready, l * N_ADA + i + (j - 1))
                        load(j, by_k(j, w, i * 512 + j * 512, 512))
                swiglu_weights(l, 0, [lambda: sp.wait_ge(mod_ready, l * N_ADA + 17),
                                      lambda: sp.wait_ge(mod_ready, l * N_ADA + 18)])
                w = t["w_in"][l].rearrange("(k p) n -> p k n", p=P)
                for i in range(N_PROJ):
                    u = U_PROJ + i
                    if i == 0:
                        sp.wait_ge(half_used, l * 8 + 4)
                    elif i == 1:
                        sp.wait_ge(y_ready, l * 24 + 8)
                    else:
                        sp.wait_ge(p_ready, l * 30 + 3 * (i - 1))
                    if i < 9:
                        load(u, by_k(u, w, COL_QKV[i // 3] + (i % 3) * MIX, MIX))
                    else:
                        d = ring(u % 2, KD, NIDX + NH)
                        load(u, [(d[:, :, 0:NIDX], w[:, :, COL_IDX:COL_IDX + NIDX]),
                                 (d[:, :, NIDX:NIDX + NH], w[:, :, COL_F:COL_F + NH])])
                sp.wait_ge(p_ready, l * 30 + 1)
                for c in range(PC):
                    sp.dma_start(LFC[:, c * 48:c * 48 + 48].rearrange("p (b h) -> p b h", b=NB),
                                 t["cache_fox_logf"][l][:, c * P:c * P + P, :].rearrange("b p h -> p b h")).then_inc(gc_full, 16)
                for c in range(PC):
                    sp.dma_start(KIC[:, c, :].rearrange("p (b d) -> p b d", b=NB),
                                 t["cache_dsa_kidx"][l][:, c * P:c * P + P, :].rearrange("b p d -> p b d")).then_inc(ki_full, 16)
                sp.wait_ge(nf_stored, l * 16 + 16)
                for b in range(NB):
                    sp.dma_start(GS[b * NH:(b + 1) * NH, PAST:KEYS],
                                 t["o_fox_logf_s"][l, b].rearrange("t h -> h t"),
                                 allow_slow_non_contiguous=True).then_inc(gn_full, 16)
                sp.wait_ge(g_ready, l * 2 + 1)
                sp.dma_start(g_s, GX[0:48, :]).then_inc(g_stored, 16)
                sp.wait_ge(g_ready, l * 2 + 2)
                sp.dma_start(g_p, RSTD[0:NH, 0:NPROMPT]).then_inc(g_stored, 16)
                sp.wait_ge(g_stored, l * 32 + 32)
                sp.wait_ge(is_done, l * 1 + 1)
                sp.dma_start(GB, g_p.rearrange("(o h) k -> o h k", o=1).to_broadcast([P, NH, NPROMPT])).then_inc(gb_full, 16)
                sp.wait_ge(msk_ready, l * 3 + 3)
                sp.dma_start(m_s, WK).then_inc(msk_stored, 16)
                sp.wait_ge(stored, l * 208 + 208)
                settle(sp)
                sp.wait_ge(po_copied, l * 6 + 6)
                sp.wait_ge(msk_stored, l * 16 + 16)
                with by_two(sp, 0, NB) as b0:
                    for j in range(6):
                        b, r = b0 + j // 3, j % 3
                        st = l * NSTEP + b0 * 3 + j
                        if r == 0:
                            g = j // 3
                            u = U_GATE + g
                            sp.wait_ge(p_ready, l * 30 + 30)
                            load(u, by_k(u, w, b0 * MIX + (COL_GATE + g * MIX), MIX))
                        if r == FOX:
                            sp.wait_ge(zs_ready, st)
                            for h in range(NH):
                                sp.dma_start(BFX[h * NT:(h + 1) * NT, :],
                                             g_s[bass.ds(b * NH + h, 1), :].to_broadcast([NT, KEYS])).then_inc(bfx_full, 16)
                        if r == DSA:
                            sp.wait_ge(zs_ready, st)
                            for h in range(NH):
                                sp.dma_start(BDX[h * NT:(h + 1) * NT, :],
                                             m_s[bass.ds(b * NT, NT), :]).then_inc(bdx_full, 16)
                        sp.wait_ge(k_used, st + 1)
                        ck = t[("cache_sb_k", "cache_fox_k", "cache_dsa_k")[r]]
                        cv = t[("cache_sb_v", "cache_fox_v", "cache_dsa_v")[r]]
                        nk = t[("o_sb_k_s", "o_fox_k_s", "o_dsa_k_s")[r]]
                        nv = t[("o_sb_v_s", "o_fox_v_s", "o_dsa_v_s")[r]]
                        sp.dma_start(KC[:, j % 2, 0:PC, :],
                                     ck[l, b].rearrange("(c p) h d -> p c (h d)", p=P)).then_inc(k_full[j % 2], 16)
                        sp.dma_start(KC[0:NT, j % 2, PC, :], nk[l, b].rearrange("t h d -> t (h d)")).then_inc(k_full[j % 2], 16)
                        sp.wait_ge(o_free, st + 1)
                        sp.dma_start(VC[:, j % 2, 0:PC, :],
                                     cv[l, b].rearrange("(c p) h d -> p c (h d)", p=P)).then_inc(v_full[j % 2], 16)
                        sp.dma_start(VC[0:NT, j % 2, PC, :], nv[l, b].rearrange("t h d -> t (h d)")).then_inc(v_full[j % 2], 16)
                w = t["w_branch"][l].rearrange("n (k p) d -> p (n k) d", p=P)
                for i in range(N_BRANCH):
                    u = U_BRANCH + i
                    if i < 2:
                        sp.wait_ge(gate_ready, l * 24 + 21 + 3 * i)
                    else:
                        sp.wait_ge(br_ready, l * 24 + 6 * (i - 1))
                    load(u, by_k(u, w, i * 256, 256, k=9))
                w = t["w_out"][l].rearrange("(k p) n -> p k n", p=P)
                for i in range(N_WOUT):
                    u = U_WOUT + i
                    sp.wait_ge(br_ready, l * 24 + 18 + 6 * i)
                    load(u, by_k(u, w, i * 512, 512))
                swiglu_weights(l, 1, [lambda: sp.wait_ge(y_ready, l * 24 + Y_BASE[2] + 4),
                                      lambda: sp.wait_ge(y_ready, l * 24 + Y_BASE[2] + 8)])

        @block.tensor
        def _(pe):
            def full(l, u0, more=0):
                pe.wait_ge(slot_full[u0 % 2], l * (16 * UNITS) + more * 32 + 32 * (u0 // 2 + 1))

            pe.wait_ge(in_x, 32)
            pe.wait_ge(in_k, 80)
            for g in range(6):
                pe.wait_ge(xt_free, g + 1)
                for j in range(4):
                    k, tt = 4 * (g % 2) + j, g // 2
                    mm = pe.transpose(PS[:, g % 2, j * P:(j + 1) * P],
                                      qr(tt * 1024 + k * P, P), IDENT[:, :])
                mm.then_inc(xt_ready, 1)
            pe.wait_ge(c_ready, 1)
            for k in range(KD):
                mm = pe.transpose(PS[:, 2, k * NC:(k + 1) * NC], BIG[0:NC, 3 * D + k * P:3 * D + (k + 1) * P], IDENT[0:NC, 0:NC])
            mm.then_inc(ct_ready, 1)
            pe.wait_ge(x_turned, 1)
            pe.wait_ge(c_silu, 1)

            def mean_square(l, n):
                for k in range(KD):
                    pe.wait_ge(sq_ready, l * 48 + (8 * n + k + 1))
                    mm = pe.matmul(PS[:, 6, 0:T], ONES[:, :], SQ[:, k, :], start=(k == 0), stop=(k == KD - 1))
                mm.then_inc(ms_ready, 1)

            def h_is_ready(l, i):
                pe.wait_ge(hs_ready, l * 3 + (i + 1))
                pe.wait_ge(hp_ready, l * 24 + (8 * i + 8))

            def swiglu_in(l, f):
                u = U_IN[f]

                def unit(j, i):
                    full(l, u + j, i)
                    w = ring((u + j) % 2, KD, 512)
                    for jj in range(2):
                        pe.wait_ge(gu_free, l * 44 + i * 4 + (22 * f + 2 * j + jj + 1))
                        for part in range(2):
                            for k in range(KD):
                                mm = pe.matmul(PS[:, 2 * jj + part, 0:T],
                                               w[:, k, part * 256 + jj * P:part * 256 + (jj + 1) * P], H[:, k, :],
                                               start=(k == 0), stop=(k == KD - 1))
                        mm.then_inc(gu_ready, 1)
                with loop(pe, 0, 5) as i:
                    unit(0, i)
                    unit(1, i)
                full(l, u + 10)
                w = ring((u + 10) % 2, KD, 512)
                for jj in range(2):
                    pe.wait_ge(gu_free, l * 44 + (22 * f + 20 + jj + 1))
                    for part in range(2):
                        for k in range(KD):
                            mm = pe.matmul(PS[:, 2 * jj + part, 0:T],
                                           w[:, k, part * 256 + jj * P:part * 256 + (jj + 1) * P], H[:, k, :],
                                           start=(k == 0), stop=(k == KD - 1))
                    mm.then_inc(gu_ready, 1)

            def swiglu_out(l, f):
                u = U_OUT[f]
                pe.wait_ge(gu_free, l * 44 + (22 * f + 24))
                with loop(pe, 0, 4) as mp:
                    for half in range(2):
                        full(l, u + half, mp)
                        w = ring((u + half) % 2, NFF // 2, 256)
                        for m in range(2):
                            if half == 0:
                                pe.wait_ge(y_free, l * 24 + mp * 2 + (Y_BASE[f] + m + 1))
                            for k in range(NFF // 2):
                                mm = pe.matmul(PS[:, m, 0:T], w[:, k, m * P:(m + 1) * P],
                                               HID[:, half * (NFF // 2) + k, :],
                                               start=(half == 0 and k == 0), stop=(half == 1 and k == NFF // 2 - 1))
                            if half == 1:
                                mm.then_inc(y_ready, 1)
                        if half == 0:
                            mm.then_inc(half_used, 1)

            with pe.Fori(0, DEPTH) as l:
                pe.wait_ge(bg_full, l * 32 + 32)
                pe.transpose(PS[:, 7, 0:120], BGR[0:120, :], IDENT[0:120, 0:120]).then_inc(bg_ready, 1)
                with loop(pe, 0, N_ADA // 2) as i:
                    for j in range(2):
                        full(l, j, i)
                        pe.wait_ge(mod_free, l * N_ADA + i * 2 + (j + 1))
                        w = ring(j, KD, 512)
                        for m in range(4):
                            for k in range(KD):
                                mm = pe.matmul(PS[:, j, m * NC:(m + 1) * NC], w[:, k, m * P:(m + 1) * P], CT[:, k, :],
                                               start=(k == 0), stop=(k == KD - 1))
                        mm.then_inc(mod_ready, 1)
                mean_square(l, 0)
                h_is_ready(l, 0)
                swiglu_in(l, 0)
                swiglu_out(l, 0)
                mean_square(l, 1)
                mean_square(l, 2)
                h_is_ready(l, 1)
                for i in range(N_PROJ):
                    full(l, U_PROJ + i)
                    width = MIX if i < 9 else NIDX + NH
                    w = ring((U_PROJ + i) % 2, KD, width)
                    for tt in range(TT):
                        pe.wait_ge(p_free, l * 30 + (3 * i + tt + 1))
                        for k in range(KD):
                            mm = pe.matmul(PS[:, tt, 0:width], H[:, k, tt * P:(tt + 1) * P], w[:, k, :],
                                           start=(k == 0), stop=(k == KD - 1))
                        mm.then_inc(p_ready, 1)
                pe.wait_ge(p_free, l * 30 + 30 + 3)
                pe.wait_ge(gc_full, l * 64 + 64)
                pe.wait_ge(logf_ready, l + 1)
                settle(pe)
                for c in range(PC):
                    pe.transpose(PS[0:48, 5, c * P:(c + 1) * P], LFC[:, c * 48:c * 48 + 48], IDENT[:, :])
                for tt in range(2):
                    mm = pe.transpose(PS[0:NH, 6, tt * P:(tt + 1) * P], LF[:, 0, tt, :], IDENT[:, :])
                mm.then_inc(gt_ready, 1)
                pe.wait_ge(rope_done, l + 1)
                n = 0
                for r in range(NBR):
                    for tt in range(TT):
                        for i in range(2 if tt < 2 else 1):
                            pe.wait_ge(qk_free, l * 15 + (n + 1))
                            for a in range(NPAIR):
                                mm = pe.transpose(PS[:, 3 + n % 2, a * P:(a + 1) * P],
                                                  QKV[:, r, tt, i * MIX + a * P:i * MIX + (a + 1) * P], IDENT[:, :])
                            mm.then_inc(qk_ready, 1)
                            n += 1
                pe.wait_ge(dup_ready, l + 1)
                pe.wait_ge(gt_copied, l + 1)
                for tt in range(2):
                    pe.wait_ge(it_free, l * 8 + (tt + 1))
                    for a in range(2):
                        pe.transpose(PS[:, 5 + tt, a * P:(a + 1) * P], IDX[:, tt, a * P:(a + 1) * P], IDENT[:, :])
                    pe.transpose(PS[:, 5 + tt, 2 * P:3 * P], KI2[:, tt, :], IDENT[:, :]).then_inc(it_ready, 1)
                pe.wait_ge(it_free, l * 8 + 3)
                for h in range(IH):
                    mm = pe.transpose(PS[:, 5, h * P:(h + 1) * P], QI2[:, h, :], IDENT[:, :])
                mm.then_inc(it_ready, 1)
                pe.wait_ge(it_free, l * 8 + 4)
                pe.transpose(PS[:, 6, 0:P], KI2[:, 2, :], IDENT[:, :]).then_inc(it_ready, 1)
                pe.wait_ge(ki_full, l * 64 + 64)
                for bp in range(4):
                    pe.wait_ge(it_free, l * 8 + (5 + bp))
                    for c in range(PC):
                        mm = pe.transpose(PS[:, 5 + bp % 2, c * P:(c + 1) * P], KIC[:, c, bp * P:(bp + 1) * P], IDENT[:, :])
                    mm.then_inc(it_ready, 1)
                pe.wait_ge(qk_free, l * 15 + 17)
                pe.wait_ge(it_free, l * 8 + 4)
                for qt in range(2):
                    for h in range(IH):
                        s = slice(64 * (h % 2), 64 * (h % 2) + 64)
                        mm = pe.matmul(PS[:, 2 * qt + h % 2, (h // 2) * 256:(h // 2) * 256 + 256],
                                       QIT[s, h // 2, qt * P:(qt + 1) * P], KITP[s, :], start=True, stop=True)
                    mm.then_inc(is_ready, 1)
                pe.wait_ge(it_free, l * 8 + 10)
                for h in range(IH):
                    if h >= 2:
                        pe.wait_ge(relu_ready, l * 6 + (h + 1))
                    for half in range(2):
                        for bp in range(4):
                            mm = pe.matmul(PS[:, 4 + 2 * (h % 2) + half, 0:264], QIP[:, h, bp * P:(bp + 1) * P],
                                           KIT[:, bp, half * 264:(half + 1) * 264], start=(bp == 0), stop=(bp == 3))
                    mm.then_inc(is_ready, 1)
                pe.wait_ge(relu_ready, l * 6 + 6)
                for it in range(6):
                    r, qt = it // 2, it % 2
                    if it:
                        pe.wait_ge(z_ready, l * 6 + it)
                    for h in range(NH):
                        s = slice(64 * (h % 2), 64 * (h % 2) + 64)
                        mm = pe.matmul(PS[:, 2 * (h % 2) + h // 4, (h // 2 % 2) * 256:(h // 2 % 2) * 256 + 256],
                                       QKT[s, r, 0, h // 2, qt * P:(qt + 1) * P], QKT[s, r, 1, h // 2, :],
                                       start=True, stop=True)
                    mm.then_inc(s_ready, 1)
                    pe.wait_ge(p_done, l * 6 + (it + 1))
                    for g in range(3):
                        n = 3 * it + g
                        if n >= 2:
                            pe.wait_ge(pt_copied, l * 18 + (n - 1))
                        for j in range(4):
                            mm = pe.transpose(PS[:, 5 + n % 2, j * P:(j + 1) * P],
                                              EP[:, 2 * g + j // 2, (j % 2) * P:(j % 2 + 1) * P], IDENT[:, :])
                        mm.then_inc(pt_ready, 1)
                    if it:
                        pe.wait_ge(po_copied, l * 6 + it)
                    pe.wait_ge(pt_copied, l * 18 + (3 * it + 3))
                    for h in range(NH):
                        for kt in range(2):
                            mm = pe.matmul(PS[64 * (h % 2):64 * (h % 2) + 64, 7, (h // 2) * P:(h // 2 + 1) * P],
                                           QKV[:, r, kt, 2 * MIX + h * HD:2 * MIX + (h + 1) * HD],
                                           PTP[:, (h % 2) * NPAIR + h // 2, kt, :],
                                           start=(kt == 0), stop=(kt == 1))
                    mm.then_inc(po_ready, 1)
                pe.wait_ge(po_copied, l * 6 + 6)

                def probs_and_values(b0, j):
                    st = l * NSTEP + b0 * 3 + j
                    pe.wait_ge(ps_ready, st + 1)
                    for c in range(PC):
                        pe.transpose(PS[:, 4, c * 96:(c + 1) * 96], ES[0:96, c * P:(c + 1) * P], IDENT[0:96, 0:96])
                    pe.transpose(PS[0:NT, 4, 384:480], ES[0:96, PAST:KEYS], IDENT[0:96, 0:96]).then_inc(st_ready, 1)
                    pe.wait_ge(v_full[j % 2], l * (NSTEP * 16) + b0 * 48 + 32 * (j // 2 + 1))
                    pe.wait_ge(o_free, st + 2)
                    pe.wait_ge(st_copied, st + 1)
                    for a in range(NPAIR):
                        for c in range(PC + 1):
                            n = P if c < PC else NT
                            mm = pe.matmul(PS[:, 7, a * 32:(a + 1) * 32], VC[0:n, j % 2, c, a * P:(a + 1) * P],
                                           PTS[0:n, c, a * 32:(a + 1) * 32], start=(c == 0), stop=(c == PC))
                    mm.then_inc(o_ready, 1)

                def step(b0, j, lagged=True):
                    st = l * NSTEP + b0 * 3 + j
                    kt = l * (NSTEP * 4) + b0 * 12 + 4 * j
                    s = j % 2
                    pe.wait_ge(k_full[s], l * (NSTEP * 16) + b0 * 48 + 32 * (j // 2 + 1))
                    for a in range(NPAIR):
                        pe.wait_ge(kt_free, kt + (a + 1))
                        for c in range(PC):
                            mm = pe.transpose(PS[:, 5 + a % 2, c * P:(c + 1) * P], KC[:, s, c, a * P:(a + 1) * P], IDENT[:, :])
                        mm.then_inc(kt_ready, 1)
                    pe.wait_ge(kt_free, kt + 4)
                    settle(pe)
                    for a in range(NPAIR):
                        mm = pe.transpose(PS[:, 6, a * NT:(a + 1) * NT], KC[0:NT, s, PC, a * P:(a + 1) * P], IDENT[0:NT, 0:NT])
                    mm.then_inc(kt_ready, 1)
                    u = U_GATE + j // 3
                    if j % 3 == 0:
                        pe.wait_ge(slot_full[u % 2], l * (16 * UNITS) + b0 * 16 + 32 * (u // 2 + 1))
                    pe.wait_ge(gate_free, st + 1)
                    w = ring(u % 2, KD, MIX)
                    for k in range(KD):
                        mm = pe.matmul(PS[:, j % 2, 0:T], w[:, k, (j % 3) * P:(j % 3 + 1) * P], H[:, k, :],
                                       start=(k == 0), stop=(k == KD - 1))
                    mm.then_inc(gate_ready, 1)
                    if lagged:
                        probs_and_values(b0, j - 1)
                    pe.wait_ge(kt_free, kt + 6)
                    pe.wait_ge(qc_ready, st + 1)
                    for a in range(NPAIR):
                        for half in range(2):
                            mm = pe.matmul(PS[32 * a:32 * a + 32, 2 + half, 0:264], QC[:, s, a * 32:(a + 1) * 32],
                                           KT[:, a, half * 264:(half + 1) * 264], start=True, stop=True)
                    mm.then_inc(ss_ready, 1)

                sweep(pe, step)
                probs_and_values(NB - 2, 5)
                pe.wait_ge(gate_free, l * 24 + 24 + 2)
                pe.wait_ge(o_free, l * 24 + 24 + 2)
                for i in range(N_BRANCH):
                    full(l, U_BRANCH + i)
                    w = ring((U_BRANCH + i) % 2, 9, 256)
                    for m in range(2):
                        for n in range(NBR):
                            pe.wait_ge(br_free, l * 24 + (6 * i + 3 * m + n + 1))
                            for k in range(NPAIR):
                                mm = pe.matmul(PS[:, n, 0:T], w[:, 3 * n + k, m * P:(m + 1) * P], OT[:, 3 * n + k, :],
                                               start=(k == 0), stop=(k == NPAIR - 1))
                            mm.then_inc(br_ready, 1)
                pe.wait_ge(mg_ready, l * 8 + 8)
                for i in range(N_WOUT):
                    full(l, U_WOUT + i)
                    w = ring((U_WOUT + i) % 2, KD, 512)
                    for m in range(4):
                        pe.wait_ge(y_free, l * 24 + (Y_BASE[2] + 4 * i + m + 1))
                        for k in range(KD):
                            mm = pe.matmul(PS[:, m % 2, 0:T], w[:, k, m * P:(m + 1) * P], MG[:, k, :],
                                           start=(k == 0), stop=(k == KD - 1))
                        mm.then_inc(y_ready, 1)
                mean_square(l, 3)
                mean_square(l, 4)
                h_is_ready(l, 2)
                swiglu_in(l, 1)
                swiglu_out(l, 1)
                mean_square(l, 5)
            pe.wait_ge(x_ready, 8 + 48)
            for g in range(6):
                pe.wait_ge(xt_free, 6 + g + 1)
                for j in range(4):
                    k, tt = 4 * (g % 2) + j, g // 2
                    mm = pe.transpose(PS[:, g % 2, j * P:(j + 1) * P], X[:, k, tt * P:(tt + 1) * P], IDENT[:, :])
                mm.then_inc(xt_ready, 1)

        @block.scalar
        def _(act):
            begin, link = chained(act, ach)
            A = nc.scalar.activation
            act.wait_ge(in_c, 32)
            A(BIG[0:NC, D:2 * D], BIG[0:NC, 0:D], ACT.Exp, scale=-1.0).then_inc(c_act, 1)
            for g in range(6):
                act.wait_ge(xt_ready, g + 1)
                ins = A(X[:, 4 * (g % 2):4 * (g % 2) + 4, (g // 2) * P:(g // 2 + 1) * P],
                        PS[:, g % 2, :].rearrange("p (k t) -> p k t", k=4), ACT.Copy)
                ins.then_inc(xt_free, 1)
            act.wait_ge(xt_free, 2 + 6)
            act.sem_inc(x_turned, 1)

            def squares_of_x(l, n, i):
                for k in range(KD):
                    act.wait_ge(x_ready, l * 24 + (8 * i + k + 1))
                    A(SQ[:, k, :], X[:, k, :], ACT.Square).then_inc(sq_ready, 1)

            def rstd(l, n):
                begin()
                act.wait_ge(var_ready, l * 6 + (n + 1))
                link(A(VAR[:, :], VAR[:, :], ACT.Ln))
                A(RSTD[:, :], VAR[:, :], ACT.Exp, scale=-0.5).then_inc(rstd_ready, 1)

            def modulate_prompt(l, i):
                act.wait_ge(xr_ready, l * 3 + (i + 1))
                act.wait_ge(coef_ready, l + 1)
                for k in range(KD):
                    A(H[:, k, 0:NPROMPT], SQ[:, k, 0:NPROMPT], ACT.Identity,
                      scale=MOD[:, (3 * i + 1) * KD + k, 0:1], bias=MOD[:, 3 * i * KD + k, 0:1]).then_inc(hp_ready, 1)

            def swiglu_in(l, f):
                with by_two(act, 0, 22) as j:
                    for jj in range(2):
                        act.wait_ge(gu_free, l * 44 + j + (22 * f + jj + 1))
                        act.wait_ge(gu_ready, l * 44 + j + (22 * f + jj + 1))
                        A(FE[:, jj, :], PS[:, 2 * jj, 0:T], ACT.Exp, scale=-1.0).then_inc(eg_ready, 1)

            def take_y(l, base):
                with by_two(act, 0, KD) as m:
                    for j in range(2):
                        begin()
                        act.wait_ge(y_ready, l * 24 + m + (base + j + 1))
                        A(Y[:, m + j, :], PS[:, j, 0:T], ACT.Copy).then_inc(y_free, 1)
                        act.wait_ge(y_free, l * 24 + m + (base + j + 1 + 2))
                        A(SQ[:, m + j, :], Y[:, m + j, :], ACT.Square).then_inc(sq_ready, 1)

            with act.Fori(0, DEPTH) as l:
                squares_of_x(l, 0, 0)
                rstd(l, 0)
                modulate_prompt(l, 0)
                swiglu_in(l, 0)
                take_y(l, Y_BASE[0])
                rstd(l, 1)
                squares_of_x(l, 2, 1)
                rstd(l, 2)
                modulate_prompt(l, 1)
                for i in range(N_PROJ):
                    for tt in range(TT):
                        act.wait_ge(p_ready, l * 30 + (3 * i + tt + 1))
                        if i < 9:
                            A(QKV[:, i // 3, tt, (i % 3) * MIX:(i % 3 + 1) * MIX], PS[:, tt, 0:MIX], ACT.Copy).then_inc(p_free, 1)
                        else:
                            begin()
                            link(A(IDX[:, tt, :], PS[:, tt, 0:NIDX], ACT.Copy))
                            A(FREG[:, tt, 0:NH], PS[:, tt, NIDX:NIDX + NH], ACT.Copy).then_inc(p_free, 1)
                act.wait_ge(logf_arg, l + 1)
                begin()
                link(A(LF[:, 1, :, :], LF[:, 0, :, :], ACT.Abs))
                link(A(LF[:, 1, :, :], LF[:, 1, :, :], ACT.Exp, scale=-1.0))
                A(LF[:, 2, :, :], LF[:, 1, :, :], ACT.Ln, bias=1.0).then_inc(logf_exp, 1)
                act.wait_ge(logf_ready, l + 1)
                act.dma_start(t["o_fox_logf_s"][l].rearrange("b t h -> (b t) h"), LF[:, 0, 2, :]).then_inc(nf_stored, 16)
                act.dma_start(t["o_fox_logf_p"][l].rearrange("o (t p) h -> p (o t) h", p=P), LF[:, 0, 0:2, :]).then_inc(stored, 16)
                act.wait_ge(gt_ready, l + 1)
                begin()
                link(A(GS[0:48, 0:PAST], PS[0:48, 5, :], ACT.Copy))
                A(VAR[0:NH, 0:NPROMPT], PS[0:NH, 6, 0:NPROMPT], ACT.Copy).then_inc(gt_copied, 1)
                act.wait_ge(p_free, l * 30 + 33)
                for name, r, c in (("sb_k", SB, 1), ("sb_v", SB, 2), ("fox_k", FOX, 1), ("fox_v", FOX, 2), ("dsa_v", DSA, 2), ("dsa_k", DSA, 1)):
                    if name == "dsa_k":
                        act.wait_ge(rope_done, l + 1)
                    act.dma_start(t[f"o_{name}_p"][l].rearrange("o (t p) h d -> p (o t) (h d)", p=P),
                                  QKV[:, r, 0:2, c * MIX:(c + 1) * MIX]).then_inc(stored, 16)
                    act.dma_start(t[f"o_{name}_s"][l].rearrange("b t h d -> (b t) (h d)"),
                                  QKV[:, r, 2, c * MIX:(c + 1) * MIX]).then_inc(stored, 16)
                act.dma_start(t["o_dsa_kidx_p"][l].rearrange("o (t p) d -> p (o t) d", p=P), IDX[:, 0:2, IH * HD:IH * HD + HD]).then_inc(kidx_stored, 16)
                act.dma_start(t["o_dsa_kidx_s"][l].rearrange("b t d -> (b t) d"), IDX[:, 2, IH * HD:IH * HD + HD]).then_inc(kidx_stored, 16)
                n = 0
                for r in range(NBR):
                    for tt in range(TT):
                        for i in range(2 if tt < 2 else 1):
                            act.wait_ge(qk_ready, l * 15 + (n + 1))
                            src = PS[:, 3 + n % 2, 0:MIX].rearrange("p (a t) -> p a t", a=NPAIR)
                            if tt < 2:
                                A(QKT[:, r, i, :, tt * P:(tt + 1) * P], src, ACT.Copy).then_inc(qk_free, 1)
                            else:
                                src = src.rearrange("p a (b t) -> p a b t", b=NB)
                                begin()
                                link(A(QBLK[0:64, r, :, :, 0:NT], src[0:64], ACT.Copy))
                                A(QBLK[64:128, r, :, :, NT:2 * NT], src[64:128], ACT.Copy).then_inc(qk_free, 1)
                            n += 1
                act.wait_ge(qip_zero, l + 1)
                for tt in range(2):
                    act.wait_ge(it_ready, l * 8 + (tt + 1))
                    begin()
                    link(A(QIT[:, :, tt * P:(tt + 1) * P], PS[:, 5 + tt, 0:2 * P].rearrange("p (a t) -> p a t", a=2), ACT.Copy))
                    A(KITP[:, tt * P:(tt + 1) * P], PS[:, 5 + tt, 2 * P:3 * P], ACT.Copy).then_inc(it_free, 1)
                act.wait_ge(it_ready, l * 8 + 3)
                begin()
                for par in range(2):
                    s = slice(64 * par, 64 * par + 64)
                    for h in range(IH):
                        dst = QIP[s, h, :].rearrange("p (i c) -> p i c", c=160)[:, :, NT * par:NT * par + NT]
                        src = PS[s, 5, h * P:(h + 1) * P].rearrange("p (i z t) -> p i z t", z=2, t=NT)[:, :, par, :]
                        ins = A(dst, src, ACT.Copy)
                        if par == 0 or h < IH - 1:
                            link(ins)
                ins.then_inc(it_free, 1)
                act.wait_ge(it_ready, l * 8 + 4)
                begin()
                src = PS[:, 6, 0:P].rearrange("p (i z t) -> p i z t", z=2, t=NT)
                link(A(KIT[0:64, :, PAST:KEYS], src[0:64, :, 0, :], ACT.Copy))
                A(KIT[64:128, :, PAST:KEYS], src[64:128, :, 1, :], ACT.Copy).then_inc(it_free, 1)
                for bp in range(4):
                    act.wait_ge(it_ready, l * 8 + (5 + bp))
                    A(KIT[:, bp, 0:PAST], PS[:, 5 + bp % 2, :], ACT.Copy).then_inc(it_free, 1)
                for n in range(6):
                    act.wait_ge(is_ready, l * 6 + (n + 1))
                    act.wait_ge(relu_free, l * 6 + (n + 1))
                    if n < 2:
                        A(RL.rearrange("p (h k) -> p h k", h=IH), PS[:, 2 * n:2 * n + 2, :].rearrange("p b (h k) -> p (b h) k", h=2),
                          ACT.Relu, scale=1 / 16).then_inc(relu_ready, 1)
                    else:
                        A(RL[:, 0:KEYS].rearrange("p (s k) -> p s k", s=2), PS[:, 4 + 2 * (n % 2):6 + 2 * (n % 2), 0:264],
                          ACT.Relu, scale=1 / 16).then_inc(relu_ready, 1)
                for it in range(6):
                    r = it // 2
                    begin()
                    act.wait_ge(z_ready, l * 6 + (it + 1))
                    if r == SB:
                        link(A(EP, ZP, ACT.Abs))
                        link(A(EP, EP, ACT.Exp, scale=-1.0))
                        A(LP, EP, ACT.Ln, bias=1.0).then_inc(e_ready, 1)
                        act.wait_ge(soft_ready, l * 6 + (it + 1))
                        A(EP, ZP, ACT.Exp).then_inc(p_done, 1)
                    else:
                        for h in range(NH):
                            ins = A(EP[:, h, :], ZP[:, h, :], ACT.Exp, bias=ST[:, h:h + 1], accum_out=ST[:, 8 + h:9 + h])
                            if h < NH - 1:
                                link(ins)
                        ins.then_inc(e_ready, 1)
                    for g in range(3):
                        act.wait_ge(pt_ready, l * 18 + (3 * it + g + 1))
                        A(PTP[:, 2 * g:2 * g + 2, :, :], PS[:, 5 + (3 * it + g) % 2, :].rearrange("p (h k q) -> p h k q", h=2, k=2),
                          ACT.Copy).then_inc(pt_copied, 1)
                    act.wait_ge(po_ready, l * 6 + (it + 1))
                    A(OT[:, 3 * r:3 * r + 3, (it % 2) * P:(it % 2 + 1) * P],
                      PS[:, 7, 0:MIX].rearrange("p (a q) -> p a q", a=NPAIR), ACT.Copy).then_inc(po_copied, 1)
                def turned_probs(b0, j):
                    st = l * NSTEP + b0 * 3 + j
                    act.wait_ge(st_ready, st + 1)
                    link(A(PTS[:, 0:PC, :], PS[:, 4, 0:384].rearrange("p (c q) -> p c q", q=96), ACT.Copy))
                    A(PTS[0:NT, PC, :], PS[0:NT, 4, 384:480], ACT.Copy).then_inc(st_copied, 1)

                def step(b0, j, lagged=True):
                    st = l * NSTEP + b0 * 3 + j
                    kt = l * (NSTEP * 4) + b0 * 12 + 4 * j
                    begin()
                    act.wait_ge(zs_ready, st + 2)
                    for a in range(NPAIR):
                        act.wait_ge(kt_ready, kt + (a + 1))
                        A(KT[:, a, 0:PAST], PS[:, 5 + a % 2, :], ACT.Copy).then_inc(kt_free, 1)
                    act.wait_ge(kt_ready, kt + 4)
                    A(KT[:, :, PAST:KEYS], PS[:, 6, 0:NPAIR * NT].rearrange("p (a t) -> p a t", a=NPAIR), ACT.Copy).then_inc(kt_free, 1)
                    act.sem_inc(k_used, 1)
                    act.wait_ge(gate_ready, st + 1)
                    A(G[:, b0 * 3 + j, :], PS[:, j % 2, 0:T], ACT.Exp, scale=-1.0).then_inc(gexp_ready, 1)
                    if lagged:
                        turned_probs(b0, j - 1)
                    act.wait_ge(zs_ready, st + 3)
                    if j % 3 == SB:
                        link(A(ES[0:96, :], ZS[0:96, :], ACT.Abs))
                        link(A(ES[0:96, :], ES[0:96, :], ACT.Exp, scale=-1.0))
                        A(LS[0:96, :], ES[0:96, :], ACT.Ln, bias=1.0).then_inc(es_ready, 1)
                        act.wait_ge(ls_ready, st + 1)
                        A(ES[0:96, :], ZS[0:96, :], ACT.Exp).then_inc(ps_ready, 1)
                    else:
                        A(ES[0:96, :], ZS[0:96, :], ACT.Exp, bias=ST[0:96, 0:1], accum_out=ST[0:96, 8:9]).then_inc(es_ready, 1)

                sweep(act, step)
                begin()
                turned_probs(NB - 2, 5)
                take_y(l, Y_BASE[2])
                rstd(l, 3)
                squares_of_x(l, 4, 2)
                rstd(l, 4)
                modulate_prompt(l, 2)
                swiglu_in(l, 1)
                take_y(l, Y_BASE[1])
                rstd(l, 5)
            for g in range(6):
                act.wait_ge(xt_ready, 6 + g + 1)
                k0, tt = 4 * (g % 2), g // 2
                A(qr(tt * 1024 + k0 * P, 512), PS[:, g % 2, :], ACT.Copy).then_inc(xt_free, 1)
            act.wait_ge(xt_free, 2 + 12)
            act.dma_start(t["o_y_p"].rearrange("o (t p) d -> p (o t) d", p=P), qr(0, 2048).rearrange("p (t d) -> p t d", t=2)).then_inc(out_stored, 16)
            act.dma_start(t["o_y_s"].rearrange("b t d -> (b t) d"), qr(2048, 1024)).then_inc(out_stored, 16)
            act.wait_ge(out_stored, 32)

        @block.vector
        def _(dve):
            begin, link = chained(dve, vch)
            V = nc.vector
            for s, n in ((xt_free, 2), (gu_free, 2), (y_free, 2), (mod_free, 2), (bg_free, 1), (p_free, 3), (qk_free, 2),
                         (it_free, 2), (relu_free, 1), (o_free, 2), (kt_free, 2), (gate_free, 2), (br_free, 3),
                         (k_used, 2), (zs_ready, 2)):
                dve.sem_inc(s, n)
            begin()
            link(V.memset(ONES[:, :], 1.0))
            link(V.memset(ZERO[:, :], 0.0))
            link(V.memset(QBLK, 0.0))
            dve.wait_ge(c_act, 1)
            c, e, f, g = (BIG[0:NC, i * D:(i + 1) * D] for i in range(4))
            link(V.tensor_scalar(f, e, 1.0, None, ALU.add))
            link(V.reciprocal(e, f))
            V.tensor_tensor(g, c, e, ALU.mult).then_inc(c_ready, 1)
            dve.wait_ge(ct_ready, 1)
            link(V.tensor_copy(CT, PS[:, 2, 0:KD * NC].rearrange("p (k c) -> p k c", c=NC)))
            dve.wait_ge(x_turned, 1)
            dve.sem_inc(x_ready, KD)
            dve.sem_inc(c_silu, 1)

            def variance(l, n):
                dve.wait_ge(ms_ready, l * 6 + (n + 1))
                V.tensor_scalar(VAR[:, :], PS[:, 6, 0:T], 1.0 / D, EPS, ALU.mult, ALU.add).then_inc(var_ready, 1)
                dve.wait_ge(rstd_ready, l * 6 + (n + 1))

            def every_chunk(ap):
                return ap[:, None, :].to_broadcast([P, KD, T])

            def pre_norm(l, n, i):
                variance(l, n)
                begin()
                V.tensor_tensor(SQ, X, every_chunk(RSTD), ALU.mult).then_inc(xr_ready, 1)
                dve.wait_ge(xr_ready, l * 3 + (i + 1))
                m = 3 * i * KD
                link(V.tensor_tensor(sample_cols(H), sample_cols(SQ), per_conditioning(MOD[:, m + KD:m + 2 * KD, :]), ALU.mult))
                V.tensor_tensor(sample_cols(H), sample_cols(H), per_conditioning(MOD[:, m:m + KD, :]), ALU.add).then_inc(hs_ready, 1)

            def post_norm(l, n, i):
                variance(l, n)
                begin()
                m = (3 * i + 2) * KD
                link(V.tensor_tensor(Y, Y, every_chunk(RSTD), ALU.mult))
                link(V.tensor_tensor(sample_cols(SQ), sample_cols(Y), per_conditioning(MOD[:, m:m + KD, :]), ALU.mult))
                link(V.tensor_tensor(sample_cols(X), sample_cols(X), sample_cols(SQ), ALU.add))
                for k in range(KD):
                    V.scalar_tensor_tensor(out=X[:, k, 0:NPROMPT], in0=Y[:, k, 0:NPROMPT], scalar=MOD[:, m + k, 0:1],
                                           in1=X[:, k, 0:NPROMPT], op0=ALU.mult, op1=ALU.add).then_inc(x_ready, 1)
                dve.wait_ge(x_ready, l * 24 + (8 * (i + 1) + 8))

            def swiglu_in(l, f):
                with by_two(dve, 0, NFF) as j:
                    for jj in range(2):
                        begin()
                        dve.wait_ge(eg_ready, l * 44 + j + (22 * f + jj + 1))
                        link(V.tensor_scalar(FE[:, jj, :], FE[:, jj, :], 1.0, None, ALU.add))
                        link(V.reciprocal(FT[:, jj, :], FE[:, jj, :]))
                        link(V.tensor_tensor(FT[:, jj, :], PS[:, 2 * jj, 0:T], FT[:, jj, :], ALU.mult))
                        V.tensor_tensor(HID[:, j + jj, :], PS[:, 2 * jj + 1, 0:T], FT[:, jj, :], ALU.mult).then_inc(gu_free, 1)
                dve.wait_ge(gu_free, l * 44 + (22 * f + 24))

            def rotate(x, heads, tt):
                n = heads * HD
                x = x.rearrange("p (h s d) -> p h s d", s=2, d=32)
                a = RT[:, 0:n].rearrange("p (h s d) -> p h s d", s=2, d=32)
                b = RT[:, 768:768 + n].rearrange("p (h s d) -> p h s d", s=2, d=32)
                cos = ROPE[:, tt, 0, :][:, None, None, :].to_broadcast([P, heads, 2, 32])
                sin = ROPE[:, tt, 1, :][:, None, :].to_broadcast([P, heads, 32])
                link(V.tensor_tensor(a, x, cos, ALU.mult))
                link(V.tensor_tensor(b[:, :, 0, :], x[:, :, 1, :], sin, ALU.mult))
                link(V.tensor_tensor(b[:, :, 1, :], x[:, :, 0, :], sin, ALU.mult))
                link(V.tensor_tensor(x[:, :, 0, :], a[:, :, 0, :], b[:, :, 0, :], ALU.subtract))
                link(V.tensor_tensor(x[:, :, 1, :], a[:, :, 1, :], b[:, :, 1, :], ALU.add))

            def reverse_scan(out, terms, more, n):
                return V.tensor_tensor_scan(out[:, ::-1], terms[:, ::-1], more[:, ::-1], 0.0, ALU.add, ALU.add)

            def choose(keys, rounds, rest):
                w = WK[:, 0:keys]
                with loop(dve, 0, rounds) as _:
                    begin()
                    link(V.max(M8, w))
                    link(V.match_replace(w, M8, w, TAKEN))
                begin()
                if rest:
                    link(V.max(M8, w))
                    link(V.memset(M8[:, rest:8], TAKEN))
                    link(V.match_replace(w, M8, w, TAKEN))

            with dve.Fori(0, DEPTH) as l:
                begin()
                dve.wait_ge(bg_ready, l + 1)
                V.tensor_copy(BG[:, :], PS[:, 7, 0:120]).then_inc(bg_free, 1)
                dve.wait_ge(bg_free, l + 2)
                with by_two(dve, 0, N_ADA) as i:
                    for j in range(2):
                        dve.wait_ge(mod_ready, l * N_ADA + i + (j + 1))
                        V.tensor_tensor(MOD[:, bass.ds(i * 4 + 4 * j, 4), :], PS[:, j, 0:36].rearrange("p (m c) -> p m c", c=NC),
                                        BG[:, bass.ds(i * 4 + 4 * j, 4)][..., None].to_broadcast([P, 4, NC]),
                                        ALU.add).then_inc(mod_free, 1)
                dve.wait_ge(mod_free, l * N_ADA + N_ADA + 2)
                begin()
                for i in range(3):
                    m = 3 * i * KD
                    gain = [BG[:, 72 + (2 * i + z) * KD:72 + (2 * i + z + 1) * KD][..., None].to_broadcast([P, KD, NC]) for z in range(2)]
                    link(V.scalar_tensor_tensor(out=MOD[:, m + KD:m + 2 * KD, :], in0=MOD[:, m + KD:m + 2 * KD, :], scalar=1.0,
                                                in1=gain[0], op0=ALU.add, op1=ALU.mult))
                    link(V.scalar_tensor_tensor(out=MOD[:, m + 2 * KD:m + 3 * KD, :], in0=MOD[:, m + 2 * KD:m + 3 * KD, :],
                                                scalar=(1.0 if i == 1 else 0.5), in1=gain[1], op0=ALU.mult, op1=ALU.mult))
                dve.sem_inc(coef_ready, 1)
                pre_norm(l, 0, 0)
                swiglu_in(l, 0)
                post_norm(l, 1, 0)
                pre_norm(l, 2, 1)
                dve.wait_ge(p_free, l * 30 + 33)
                dve.wait_ge(bf_full, l * 16 + 16)
                begin()
                V.tensor_tensor(LF[:, 0, :, :], FREG[:, :, 0:NH], BF[:, None, :].to_broadcast([P, TT, NH]), ALU.add).then_inc(logf_arg, 1)
                dve.wait_ge(logf_exp, l + 1)
                V.scalar_tensor_tensor(out=LF[:, 0, :, :], in0=LF[:, 0, :, :], scalar=0.0, in1=LF[:, 2, :, :],
                                       op0=ALU.min, op1=ALU.subtract).then_inc(logf_ready, 1)
                dve.wait_ge(gt_copied, l + 1)
                dve.wait_ge(gn_full, l * 128 + 128)
                begin()
                link(V.memset(GX[0:48, KEYS - 1:KEYS], 0.0))
                reverse_scan(GX[0:48, 0:KEYS - 1], GS[0:48, 1:KEYS], ZERO[0:48, 1:KEYS], 0).then_inc(g_ready, 1)
                link(V.memset(RSTD[0:NH, NPROMPT - 1:NPROMPT], 0.0))
                reverse_scan(RSTD[0:NH, 0:NPROMPT - 1], VAR[0:NH, 1:NPROMPT], ZERO[0:NH, 1:NPROMPT], 0).then_inc(g_ready, 1)
                dve.wait_ge(g_stored, l * 32 + 32)
                for tt in range(TT):
                    rotate(QKV[:, DSA, tt, 0:2 * MIX], 2 * NH, tt)
                    rotate(IDX[:, tt, 0:5 * HD], 5, tt)
                dve.sem_inc(rope_done, 1)
                for z in range(2):
                    link(V.tensor_copy(KI2[:, :, z * HD:(z + 1) * HD], IDX[:, :, IH * HD:(IH + 1) * HD]))
                    link(V.tensor_copy(QI2[:, :, z * HD:(z + 1) * HD], IDX[:, 2, 0:IH * HD].rearrange("p (h d) -> p h d", h=IH)))
                dve.sem_inc(dup_ready, 1)
                V.memset(QIP, 0.0).then_inc(qip_zero, 1)
                for qt in range(2):
                    begin()
                    w = IDX[:, qt, (IH + 1) * HD:]
                    dve.wait_ge(relu_ready, l * 6 + (qt + 1))
                    dve.wait_ge(qip_zero, l + 1)
                    link(V.tensor_scalar(ISC[:, 0:256], RL[:, 0:256], w[:, 0:1], None, ALU.mult))
                    for h in range(1, IH):
                        ins = V.scalar_tensor_tensor(out=ISC[:, 0:256], in0=by_parity(RL, h, IH, 256), scalar=w[:, h:h + 1],
                                                     in1=ISC[:, 0:256], op0=ALU.mult, op1=ALU.add)
                        link(ins)
                    dve.sem_inc(relu_free, 1)
                    link(V.tensor_tensor(WK[:, 0:256], ISC[:, 0:256], MASKS[:, 2, qt, :], ALU.add))
                    choose(NPROMPT, TOPK_P // 8, TOPK_P % 8)
                    V.tensor_scalar(DMB[:, qt, :], WK[:, 0:256], TAKEN / 2, NEG, ALU.is_gt, ALU.mult).then_inc(msk_ready, 1)
                    dve.wait_ge(msk_ready, l * 3 + (qt + 1))
                w = IDX[:, 2, (IH + 1) * HD:]
                begin()
                for h in range(IH):
                    dve.wait_ge(relu_ready, l * 6 + (3 + h))
                    if h == 0:
                        link(V.tensor_scalar(WK, RL[:, 0:KEYS], w[:, 0:1], None, ALU.mult))
                    else:
                        link(V.scalar_tensor_tensor(out=WK, in0=RL[:, 0:KEYS], scalar=w[:, h:h + 1], in1=WK,
                                                    op0=ALU.mult, op1=ALU.add))
                    dve.sem_inc(relu_free, 1)
                choose(KEYS, TOPK_S // 8, TOPK_S % 8)
                V.tensor_scalar(WK, WK, TAKEN / 2, NEG, ALU.is_gt, ALU.mult).then_inc(msk_ready, 1)
                dve.wait_ge(msk_ready, l * 3 + 3)
                dve.wait_ge(kidx_stored, l * 32 + 32)
                dve.sem_inc(is_done, 1)
                for it in range(6):
                    r, qt = it // 2, it % 2
                    begin()
                    dve.wait_ge(s_ready, l * 6 + (it + 1))
                    if r == FOX:
                        dve.wait_ge(gb_full, l * 16 + 16)
                    for z in range(2):
                        S = PS[:, 2 * z:2 * z + 2, :].rearrange("p b (h k) -> p (b h) k", h=2)[:, 0:NPAIR, :]
                        bias = (MASKS[:, 0, qt, :], None, DMB[:, qt, :])[r]
                        bias = GB[:, z::2, :] if r == FOX else bias[:, None, :].to_broadcast([P, NPAIR, NPROMPT])
                        link(V.scalar_tensor_tensor(out=ZP[:, z * NPAIR:(z + 1) * NPAIR, :], in0=S, scalar=SCALE, in1=bias,
                                                    op0=ALU.mult, op1=ALU.add))
                    if r == FOX:
                        link(V.tensor_tensor(ZP, ZP, MASKS[:, 1, qt, :][:, None, :].to_broadcast([P, NH, NPROMPT]), ALU.add))
                    if r == SB:
                        dve.sem_inc(z_ready, 1)
                        dve.wait_ge(e_ready, l * 6 + (it + 1))
                        link(V.scalar_tensor_tensor(out=LP, in0=ZP, scalar=0.0, in1=LP, op0=ALU.max, op1=ALU.add))
                        for h in range(NH):
                            link(reverse_scan(EP[:, h, :], LP[:, h, :], ZERO[:, 0:NPROMPT], 0))
                        V.tensor_tensor(ZP, ZP, EP, ALU.subtract).then_inc(soft_ready, 1)
                        dve.wait_ge(soft_ready, l * 6 + (it + 1))
                        dve.wait_ge(p_done, l * 6 + (it + 1))
                    else:
                        link(V.tensor_reduce(ST[:, 0:NH], ZP, AXX, ALU.max, negate=True))
                        dve.sem_inc(z_ready, 1)
                        dve.wait_ge(e_ready, l * 6 + (it + 1))
                        link(V.reciprocal(ST[:, 16:16 + NH], ST[:, 8:8 + NH]))
                        dve.sem_inc(soft_ready, 1)
                        V.tensor_tensor(EP, EP, ST[:, 16:16 + NH][..., None].to_broadcast([P, NH, NPROMPT]), ALU.mult).then_inc(p_done, 1)
                        dve.wait_ge(p_done, l * 6 + (it + 1))
                dve.wait_ge(po_copied, l * 6 + 6)
                dve.wait_ge(stored, l * 208 + 208)
                def output(b0, j):
                    b, r = b0 + j // 3, j % 3
                    dve.wait_ge(o_ready, l * NSTEP + b0 * 3 + (j + 1))
                    src = PS[:, 7, 0:96].rearrange("p (a c) -> p a c", a=NPAIR)
                    o = OT[:, 3 * r:3 * r + 3, bass.ds(b * NT + NPROMPT, NT)]
                    link(V.tensor_copy(o[0:64], src[0:64, :, 0:NT]))
                    V.tensor_copy(o[64:128], src[64:128, :, NT:2 * NT]).then_inc(o_free, 1)

                def step(b0, j, lagged=True):
                    b, r = b0 + j // 3, j % 3
                    st = l * NSTEP + b0 * 3 + j
                    begin()
                    V.tensor_copy(QC[:, j % 2, :].rearrange("p (a c) -> p a c", a=NPAIR), QBLK[:, r, :, b, :]).then_inc(qc_ready, 1)
                    dve.wait_ge(gexp_ready, st + 1)
                    g = G[:, b0 * 3 + j, :]
                    link(V.tensor_scalar(g, g, 1.0, None, ALU.add))
                    V.reciprocal(g, g).then_inc(gate_free, 1)
                    if lagged:
                        output(b0, j - 1)
                    dve.wait_ge(ss_ready, st + 1)
                    if r == FOX:
                        dve.wait_ge(bfx_full, l * (NB * 96) + b * 96 + 96)
                    if r == DSA:
                        dve.wait_ge(bdx_full, l * (NB * 96) + b * 96 + 96)
                    bias = (BSB, BFX, BDX)[r][0:96, :].rearrange("p (s k) -> p s k", s=2)
                    link(V.scalar_tensor_tensor(out=ZS[0:96, :].rearrange("p (s k) -> p s k", s=2), in0=PS[0:96, 2:4, 0:264],
                                                scalar=SCALE, in1=bias, op0=ALU.mult, op1=ALU.add))
                    if r == FOX:
                        link(V.tensor_tensor(ZS[0:96, PAST:KEYS], ZS[0:96, PAST:KEYS], MFOX[0:96, :], ALU.add))
                    if r == SB:
                        dve.sem_inc(zs_ready, 1)
                        dve.wait_ge(es_ready, st + 1)
                        link(V.scalar_tensor_tensor(out=LS[0:96, :], in0=ZS[0:96, :], scalar=0.0, in1=LS[0:96, :],
                                                    op0=ALU.max, op1=ALU.add))
                        link(reverse_scan(ES[0:96, :], LS[0:96, :], ZERO[0:96, :], 0))
                        V.tensor_tensor(ZS[0:96, :], ZS[0:96, :], ES[0:96, :], ALU.subtract).then_inc(ls_ready, 1)
                        dve.wait_ge(ps_ready, st + 1)
                    else:
                        link(V.tensor_reduce(ST[0:96, 0:1], ZS[0:96, :], AXX, ALU.max, negate=True))
                        dve.sem_inc(zs_ready, 1)
                        dve.wait_ge(es_ready, st + 1)
                        link(V.reciprocal(ST[0:96, 16:17], ST[0:96, 8:9]))
                        dve.sem_inc(ls_ready, 1)
                        V.tensor_scalar(ES[0:96, :], ES[0:96, :], ST[0:96, 16:17], None, ALU.mult).then_inc(ps_ready, 1)

                sweep(dve, step)
                begin()
                output(NB - 2, 5)
                dve.wait_ge(o_free, l * 24 + 26)
                with loop(dve, 0, KD) as m:
                    begin()
                    for n in range(NBR):
                        dve.wait_ge(br_ready, l * 24 + m * 3 + (n + 1))
                        g = G[:, m + n * KD, :]
                        dst = MG[:, m, :] if n == 0 else MGT
                        V.tensor_tensor(dst, PS[:, n, 0:T], g, ALU.mult).then_inc(br_free, 1)
                        dve.wait_ge(br_free, l * 24 + m * 3 + (n + 4))
                        if n:
                            link(V.tensor_tensor(MG[:, m, :], MG[:, m, :], MGT, ALU.add))
                    dve.sem_inc(mg_ready, 1)
                post_norm(l, 3, 1)
                pre_norm(l, 4, 2)
                swiglu_in(l, 1)
                post_norm(l, 5, 2)


_INS = ["x_prompt", "x_sample", "cache_sb_k", "cache_sb_v", "cache_fox_k", "cache_fox_v", "cache_fox_logf",
        "cache_dsa_k", "cache_dsa_v", "cache_dsa_kidx", "c_prompt", "c_sample", "norm_g", "w_ada", "b_ada",
        "ffn_w_in", "ffn_w_out", "w_in", "b_forget", "w_branch", "w_out"]
_P, _S = (DEPTH, 1, NPROMPT), (DEPTH, NB, NT)
_STATE = [("sb_k", (NH, HD)), ("sb_v", (NH, HD)), ("fox_k", (NH, HD)), ("fox_v", (NH, HD)), ("fox_logf", (NH,)),
          ("dsa_k", (NH, HD)), ("dsa_v", (NH, HD)), ("dsa_kidx", (HD,))]
_OUTS = ([("o_y_p", (1, NPROMPT, D)), ("o_y_s", (NB, NT, D))]
         + [(f"o_{n}_p", _P + s) for n, s in _STATE] + [(f"o_{n}_s", _S + s) for n, s in _STATE])


def shape_constants():
    import numpy as np
    q = np.arange(NPROMPT).reshape(2, P, 1)
    k = np.arange(NPROMPT).reshape(1, 1, NPROMPT)
    masks = np.stack([np.where(k < q, 0, NEG), np.where(k <= q, 0, NEG), np.where(k // 64 <= q // 64, 0, NEG)])
    pos = np.concatenate([np.arange(NPROMPT), np.tile(PAST + np.arange(NT), NB)]).astype(np.float32)
    inv = np.float32(10000.0) ** (-np.arange(32, dtype=np.float32) / np.float32(32))
    ang = (pos[:, None] * inv[None, :]).astype(np.float32)
    rope = np.stack([np.cos(ang), np.sin(ang)], 1).reshape(TT, P, 2, 32)
    tq = np.tile(np.arange(NT), NH)[:, None]
    tk = np.arange(NT)[None, :]
    bsb = np.zeros((NH * NT, KEYS))
    bsb[:, PAST:] = np.where(tk < tq, 0, NEG)
    arrays = {
        "k_masks": masks.transpose(2, 0, 1, 3), "k_ident": np.eye(P), "k_rope": rope.transpose(1, 0, 2, 3),
        "k_bsb": bsb, "k_mfox": np.where(tk <= tq, 0, NEG),
    }
    return {n: np.ascontiguousarray(a, dtype=np.float32) for n, a in arrays.items()}


def kernel(**inputs):
    import numpy as _np
    import concourse.bacc as _bacc
    from concourse import mybir as _mybir
    from concourse.bass_utils import run_bass_kernel_spmd as _run

    nc = _bacc.Bacc("TRN2", target_bir_lowering=False, num_devices=1)
    arrays = {n: _np.ascontiguousarray(inputs[n]) for n in _INS}
    arrays.update(shape_constants())
    t = {n: nc.dram_tensor(n, a.shape, _mybir.dt.from_np(a.dtype), kind="ExternalInput").ap() for n, a in arrays.items()}
    t.update({n: nc.dram_tensor(n, s, F32, kind="ExternalOutput").ap() for n, s in _OUTS})
    program(nc, t)
    r = _run(nc, [arrays], core_ids=[0])
    return tuple(r.results[0][n] for n, _ in _OUTS)
```

```python
import concourse.bass as bass
from concourse import mybir
from contextlib import ExitStack, contextmanager

ALU = mybir.AluOpType
ACT = mybir.ActivationFunctionType
AXX = mybir.AxisListType.X
F32 = mybir.dt.float32

P = 128
D = 1024
KD = D // P
NPROMPT = 256
NB = 8
NT = 16
NSAMPLE = NB * NT
T = NPROMPT + NSAMPLE
TT = T // P
DEPTH = 2
PAST = 512
KEYS = PAST + NT
PC = PAST // P
NH = 6
HD = 64
NPAIR = NH // 2
MIX = NH * HD
NBR = 3
SB, FOX, DSA = range(NBR)
IH = 4
FF = 2816
NFF = FF // P
NC = 9
NMOD = 9
EPS = 1e-6
SCALE = HD ** -0.5
TOPK_P = NPROMPT // 4
TOPK_S = KEYS // 4
NEG = -1e30
TAKEN = -3e38

COL_QKV = [0, 3 * MIX, 6 * MIX + NH]
COL_F = 6 * MIX
COL_IDX = 9 * MIX + NH
NIDX = IH * HD + HD + IH
COL_GATE = COL_IDX + NIDX

GATES = [6, 15]
GATE_AT = [15, 17, 19, 21, 22, 23, 24]

N_IN, N_OUT, N_PROJ, N_GATE, N_BRANCH, N_WOUT = 11, 8, 10, 8, 4, 2
N_ADA = 18
N_ADA0 = 6
U_IN = [N_ADA0, 0]
U_OUT = [U_IN[0] + N_IN, 0]
U_PROJ = U_OUT[0] + N_OUT
U_GATE = U_PROJ + N_PROJ
U_BRANCH = U_GATE + N_GATE
U_WOUT = U_BRANCH + N_BRANCH
U_IN[1] = U_WOUT + N_WOUT
U_OUT[1] = U_IN[1] + N_IN
UNITS = U_OUT[1] + N_OUT
assert UNITS % 2 == 0

Y_BASE = [0, 2 * KD, KD]
NSTEP = NB * NBR


def program(nc, t):
    with ExitStack() as ctx:
        def sb(name, width):
            return ctx.enter_context(nc.sbuf_tensor(name, [P, width], F32))

        def sem(name):
            return ctx.enter_context(nc.semaphore(name))

        X = sb("X", KD * T)[:, :].rearrange("p (k t) -> p k t", k=KD)
        H = sb("H", KD * T)[:, :].rearrange("p (k t) -> p k t", k=KD)
        BIG = sb("BIG", 24 * T)
        QR = sb("QR", 12960)
        RING = sb("RING", 2 * 4096)
        QKT = sb("QKT", NBR * 2 * NPAIR * NPROMPT)[:, :].rearrange(
            "p (r i a t) -> p r i a t", r=NBR, i=2, a=NPAIR)
        QBLK = sb("QBLK", NBR * NPAIR * NB * 32)[:, :].rearrange(
            "p (r a b c) -> p r a b c", r=NBR, a=NPAIR, b=NB)
        OTR = sb("OT", NBR * NPAIR * T)
        OT = OTR[:, :].rearrange("p (g t) -> p g t", t=T)
        MOD = sb("MOD", NMOD * KD * NC)[:, :].rearrange("p (m c) -> p m c", c=NC)
        BGR = sb("BGR", P)
        BG = sb("BG", 120)
        MASKS = sb("MASKS", 3 * 2 * NPROMPT)[:, :].rearrange("p (r q k) -> p r q k", r=3, q=2)
        IDENT = sb("IDENT", P)
        ONES = sb("ONES", P)
        ROPE = sb("ROPE", TT * 2 * 32)[:, :].rearrange("p (t s d) -> p t s d", t=TT, s=2)
        ZERO = sb("ZERO", KEYS)
        BSB = sb("BSB", KEYS)
        MFOX = sb("MFOX", NT)
        RSTD = sb("RSTD", T)
        VAR = sb("VAR", T)
        CT = sb("CT", KD * 32)[:, :].rearrange("p (k c) -> p k c", c=32)
        AR = sb("AR", P)
        DMB = sb("DMB", 2 * NPROMPT)[:, :].rearrange("p (q k) -> p q k", q=2)
        QC = sb("QC", 2 * 96)[:, :].rearrange("p (s c) -> p s c", s=2)
        OU = sb("OU", P)
        ST = sb("ST", 64)
        LF = sb("LF", 3 * TT * NH)[:, :].rearrange("p (s t h) -> p s t h", s=3, t=TT)
        BF = sb("BF", NH)
        FREG = sb("FREG", TT * 8)[:, :].rearrange("p (t h) -> p t h", t=TT)

        def big(off, n):
            return BIG[:, off:off + n]

        def qr(off, n):
            return QR[:, off:off + n]

        HID = big(0, NFF * T).rearrange("p (j t) -> p j t", t=T)
        G = big(0, 24 * T).rearrange("p (j t) -> p j t", t=T)
        Y = qr(0, KD * T).rearrange("p (k t) -> p k t", t=T)
        SQ = qr(3072, KD * T).rearrange("p (k t) -> p k t", t=T)
        MG = qr(6144, KD * T).rearrange("p (k t) -> p k t", t=T)
        MGT = qr(9216, T)
        FE = qr(6144, 2 * T).rearrange("p (j t) -> p j t", t=T)
        FT = qr(6144 + 2 * T, 2 * T).rearrange("p (j t) -> p j t", t=T)
        ADA = qr(8192, KD * 512).rearrange("p (k w) -> p k w", w=512)
        QK = qr(0, NBR * TT * 2 * MIX).rearrange("p (r t c) -> p r t c", r=NBR, t=TT)
        VT = qr(6912, NBR * TT * MIX).rearrange("p (r t c) -> p r t c", r=NBR, t=TT)
        QX = 10368
        GS, GX, LFC = qr(QX, KEYS), qr(QX + KEYS, KEYS), qr(QX + 2 * KEYS, PC * 48)
        RT = qr(QX, 2304)
        RL, ISC, WK = qr(QX, 1024), qr(QX + 1024, KEYS), qr(QX + 1024 + KEYS, KEYS)
        M8 = ST[:, 56:64]
        IDX = OTR[:, 0:TT * NIDX].rearrange("p (t c) -> p t c", t=TT)
        o = TT * NIDX
        KI2 = OTR[:, o:o + TT * P].rearrange("p (t c) -> p t c", t=TT); o += TT * P
        KIC = OTR[:, o:o + PC * NB * HD].rearrange("p (c w) -> p c w", c=PC); o += PC * NB * HD
        assert o <= NBR * NPAIR * T
        o = 0
        QI2 = qr(o, IH * P).rearrange("p (h c) -> p h c", h=IH); o += IH * P
        KIT = qr(o, 4 * KEYS).rearrange("p (b k) -> p b k", b=4); o += 4 * KEYS
        QIP = qr(o, IH * 640).rearrange("p (h c) -> p h c", h=IH); o += IH * 640
        QIT = qr(o, 2 * NPROMPT).rearrange("p (a t) -> p a t", a=2); o += 2 * NPROMPT
        KITP = qr(o, NPROMPT); o += NPROMPT
        assert o <= 6912
        ZP, EP, LP = (qr(i * 1536, 1536).rearrange("p (h k) -> p h k", h=NH) for i in range(3))
        PTP = qr(3 * 1536, 1536).rearrange("p (h k q) -> p h k q", h=NH, k=2)
        GB = qr(QX, 1536).rearrange("p (h k) -> p h k", h=NH)
        KC = qr(0, 3840).rearrange("p (s c w) -> p s c w", s=2, c=PC + 1)
        VC = qr(3840, 3840).rearrange("p (s c w) -> p s c w", s=2, c=PC + 1)
        KT = qr(7680, NPAIR * KEYS).rearrange("p (a k) -> p a k", a=NPAIR)
        o = 7680 + NPAIR * KEYS
        ZS, ES0, ES1, LS, BFX, BDX = (qr(o + i * KEYS, KEYS) for i in range(6))
        ES = (ES0, ES1)
        PTS = qr(o + 6 * KEYS, 480).rearrange("p (c q) -> p c q", q=96)
        o += 6 * KEYS + 480
        assert o <= 12960

        def by_parity(ap, h, heads, width):
            n = (h % 2) * (heads // 2) + h // 2
            return ap[:, n * width:(n + 1) * width]

        def ring(s, k, w):
            return RING[:, s * 4096:s * 4096 + k * w].rearrange("p (k w) -> p k w", w=w)

        PS = ctx.enter_context(nc.psum_tensor("PS", [P, 8, 512], F32))

        g_s = nc.dram_tensor("scr_g_sample", (NB * NH, KEYS), F32, kind="Internal").ap()
        g_p = nc.dram_tensor("scr_g_prompt", (NH, NPROMPT), F32, kind="Internal").ap()
        m_s = nc.dram_tensor("scr_mask_sample", (NSAMPLE, KEYS), F32, kind="Internal").ap()

        in_x, in_c, in_k = sem("in_x"), sem("in_c"), sem("in_k")
        c_act, c_silu, c_ready, ct_ready = sem("c_act"), sem("c_silu"), sem("c_ready"), sem("ct_ready")
        xt_ready, xt_free, x_turned = sem("xt_ready"), sem("xt_free"), sem("x_turned")
        settled = sem("settled")
        vch, ach = sem("vector_chain"), sem("scalar_chain")
        slot_full = [sem("slot_full0"), sem("slot_full1")]
        bg_full, bg_ready, bg_free = sem("bg_full"), sem("bg_ready"), sem("bg_free")
        acc_ready, ar_ready, ada_full = sem("acc_ready"), sem("ar_ready"), sem("ada_full")
        mod_ready, mod_free, coef_ready = sem("mod_ready"), sem("mod_free"), sem("coef_ready")
        sq_ready, ms_ready, var_ready, rstd_ready = sem("sq_ready"), sem("ms_ready"), sem("var_ready"), sem("rstd_ready")
        xr_ready, hp_ready, hs_ready, x_ready = sem("xr_ready"), sem("hp_ready"), sem("hs_ready"), sem("x_ready")
        gu_ready, eg_ready, gu_free, half_used = sem("gu_ready"), sem("eg_ready"), sem("gu_free"), sem("half_used")
        y_ready, y_free = sem("y_ready"), sem("y_free")
        p_ready, p_free = sem("p_ready"), sem("p_free")
        rope_done, logf_exp, logf_ready = sem("rope_done"), sem("logf_exp"), sem("logf_ready")
        logf_arg = sem("logf_arg")
        stored, nf_stored, kidx_stored = sem("stored"), sem("nf_stored"), sem("kidx_stored")
        qk_ready, qk_free = sem("qk_ready"), sem("qk_free")
        bf_full, gc_full, gn_full = sem("bf_full"), sem("gc_full"), sem("gn_full")
        gt_ready, gt_copied, g_ready, g_stored, gb_full = sem("gt_ready"), sem("gt_copied"), sem("g_ready"), sem("g_stored"), sem("gb_full")
        ki_full, dup_ready = sem("ki_full"), sem("dup_ready")
        it_ready, it_free, qip_zero = sem("it_ready"), sem("it_free"), sem("qip_zero")
        is_ready, relu_ready, relu_free, is_done = sem("is_ready"), sem("relu_ready"), sem("relu_free"), sem("is_done")
        msk_ready, msk_stored = sem("msk_ready"), sem("msk_stored")
        s_ready, z_ready, e_ready = sem("ps_ready"), sem("pz_ready"), sem("pe_ready")
        soft_ready, p_done, pt_ready, pt_copied = sem("psoft_ready"), sem("p_probs_ready"), sem("ppt_ready"), sem("ppt_copied")
        po_ready, po_copied = sem("ppo_ready"), sem("ppo_copied")
        k_full = [sem("k_full0"), sem("k_full1")]
        v_full = [sem("v_full0"), sem("v_full1")]
        k_used, o_ready, o_free = sem("k_used"), sem("o_ready"), sem("o_free")
        pv_ready, ou_ready = sem("pv_ready"), sem("ou_ready")
        kt_ready, kt_free = sem("kt_ready"), sem("kt_free")
        qc_ready, ss_ready, zs_ready, es_ready = sem("qc_ready"), sem("ss_ready"), sem("zs_ready"), sem("es_ready")
        ls_ready, ps_ready = sem("ls_ready"), sem("sprobs_ready")
        st_ready, st_copied = sem("st_ready"), sem("st_copied")
        bfx_full, bdx_full = sem("bfx_full"), sem("bdx_full")
        gate_ready, gexp_ready, gate_done = sem("gate_ready"), sem("gexp_ready"), sem("gate_done")
        br_ready, br_free, mg_ready = sem("br_ready"), sem("br_free"), sem("mg_ready")
        out_ready, out_stored = sem("out_ready"), sem("out_stored")

        block = ctx.enter_context(nc.Block())

        def settle(eng):
            eng.sem_inc(settled, 1)

        @contextmanager
        def loop(eng, start, end):
            settle(eng)
            with eng.Fori(start, end) as i:
                yield i

        def chained(eng, chain):
            n = [0]

            def begin():
                settle(eng)
                eng.sem_clear(chain)
                n[0] = 0

            def link(ins):
                n[0] += 1
                ins.then_inc(chain, 1)
                eng.wait_ge(chain, n[0])
            return begin, link

        def per_conditioning(ap, kc=None):
            a = ap[:, :, 1:NC] if kc is None else ap[:, kc, 1:NC]
            return a[..., None].to_broadcast([P, KD, NB, NT]) if kc is None else a[..., None].to_broadcast([P, NB, NT])

        def sample_cols(ap):
            return ap[:, :, NPROMPT:T].rearrange("p k (b t) -> p k b t", b=NB)

        @contextmanager
        def by_two(eng, start, end):
            with loop(eng, start // 2, end // 2) as half:
                yield half * 2

        def sweep(eng, step):
            step(0, 0)
            step(0, 1)
            with by_two(eng, 0, NB - 2) as b0:
                for j in range(2, 8):
                    step(b0, j)
            for j in range(2, 6):
                step(NB - 2, j)

        def has(b0, j):
            return not isinstance(b0, int) or 0 <= b0 * NBR + j < NSTEP

        @block.sync
        def _(sp):
            sp.dma_start(qr(0, 2048).rearrange("p (t d) -> p t d", t=2),
                         t["x_prompt"].rearrange("o (t p) d -> p (o t) d", p=P)).then_inc(in_x, 16)
            sp.dma_start(qr(2048, 1024), t["x_sample"].rearrange("b t d -> (b t) d")).then_inc(in_x, 16)
            sp.dma_start(BIG[0:1, 0:D], t["c_prompt"]).then_inc(in_c, 16)
            sp.dma_start(BIG[1:NC, 0:D], t["c_sample"]).then_inc(in_c, 16)
            sp.dma_start(MASKS, t["k_masks"]).then_inc(in_k, 16)
            sp.dma_start(IDENT[:, :], t["k_ident"]).then_inc(in_k, 16)
            sp.dma_start(ROPE, t["k_rope"]).then_inc(in_k, 16)
            sp.dma_start(BSB[0:96, :], t["k_bsb"]).then_inc(in_k, 16)
            sp.dma_start(MFOX[0:96, :], t["k_mfox"]).then_inc(in_k, 16)

            def load(u, parts):
                s = u % 2
                for dst, src in parts:
                    sp.dma_start(dst, src).then_inc(slot_full[s], 16)

            def ffn_in(l, f, u, i):
                w = t["ffn_w_in"][l, f].rearrange("(k p) n -> p k n", p=P)
                d = ring(u % 2, KD, 512)
                return [(d[:, :, 0:256], w[:, :, bass.ds(i * 256, 256)]),
                        (d[:, :, 256:512], w[:, :, bass.ds(i * 256 + FF, 256)])]

            def ffn_out(l, f, u, mp, half):
                w = t["ffn_w_out"][l, f].rearrange("(k p) n -> p k n", p=P)
                d = ring(u % 2, NFF // 2, 256)
                k0 = half * (NFF // 2)
                return [(d[:, a:b, :], w[:, k0 + a:k0 + b, bass.ds(mp * 256, 256)]) for a, b in ((0, 6), (6, 11))]

            def by_k(u, w, col, width, k=KD):
                d = ring(u % 2, k, width)
                h = k // 2
                return [(d[:, a:b, :], w[:, a:b, bass.ds(col, width)]) for a, b in ((0, h), (h, k))]

            def swiglu_weights(l, f, before, beside=None):
                u = U_IN[f]
                for i in range(2):
                    before[i]()
                    load(u + i, ffn_in(l, f, u + i, i))
                if beside:
                    beside(0)
                with by_two(sp, 2, 10) as i:
                    for j in range(2):
                        sp.wait_ge(gu_ready, l * 44 + i * 2 + (22 * f + 2 * j - 2))
                        load(u + j, ffn_in(l, f, u + j, i + j))
                        if beside:
                            beside(i + (j - 1))
                sp.wait_ge(gu_ready, l * 44 + (22 * f + 18))
                load(u + 10, ffn_in(l, f, u + 10, 10))
                if beside:
                    beside(9)
                u = U_OUT[f]
                sp.wait_ge(gu_ready, l * 44 + (22 * f + 20))
                load(u, ffn_out(l, f, u, 0, 0))
                if beside:
                    beside(10)
                sp.wait_ge(gu_ready, l * 44 + (22 * f + 22))
                load(u + 1, ffn_out(l, f, u + 1, 0, 1))
                if beside:
                    beside(11)
                with loop(sp, 1, 4) as mp:
                    sp.wait_ge(half_used, l * 8 + mp + 4 * f)
                    load(u, ffn_out(l, f, u, mp, 0))
                    sp.wait_ge(y_ready, l * 24 + mp * 2 + Y_BASE[f])
                    load(u + 1, ffn_out(l, f, u + 1, mp, 1))

            with sp.Fori(0, DEPTH) as l:
                sp.wait_ge(bg_free, l + 1)
                sp.dma_start(BGR[0:72, :], t["b_ada"][l].rearrange("(m p) -> m p", p=P)).then_inc(bg_full, 16)
                sp.dma_start(BGR[72:120, :], t["norm_g"][l].rearrange("n (k p) -> (n k) p", p=P)).then_inc(bg_full, 16)
                sp.dma_start(BF[:, :], t["b_forget"][bass.ds(l, 1), :].to_broadcast([P, NH])).then_inc(bf_full, 16)
                w = t["w_ada"][l].rearrange("(k p) n -> p k n", p=P)
                sp.wait_ge(y_free, l * 24 + 2)
                for i in range(2):
                    load(i, by_k(i, w, i * 512, 512))
                for i in range(2, N_ADA0):
                    sp.wait_ge(acc_ready, l * N_ADA + (i - 1))
                    load(i, by_k(i, w, i * 512, 512))

                def ada(a):
                    sp.wait_ge(acc_ready, l * N_ADA + a + N_ADA0)
                    for k in range(0, KD, 4):
                        sp.dma_start(ADA[:, k:k + 4, :], w_ada[:, k:k + 4, bass.ds(a * 512 + N_ADA0 * 512, 512)]).then_inc(ada_full, 16)
                w_ada = w
                swiglu_weights(l, 0, [lambda: sp.wait_ge(acc_ready, l * N_ADA + 5),
                                      lambda: sp.wait_ge(acc_ready, l * N_ADA + 6)], ada)
                w = t["w_in"][l].rearrange("(k p) n -> p k n", p=P)
                for i in range(N_PROJ):
                    u = U_PROJ + i
                    if i == 0:
                        sp.wait_ge(half_used, l * 8 + 4)
                    elif i == 1:
                        sp.wait_ge(y_ready, l * 24 + 8)
                    else:
                        sp.wait_ge(p_ready, l * 30 + 3 * (i - 1))
                    if i < 9:
                        load(u, by_k(u, w, COL_QKV[i // 3] + (i % 3) * MIX, MIX))
                    else:
                        d = ring(u % 2, KD, NIDX + NH)
                        load(u, [(d[:, :, 0:NIDX], w[:, :, COL_IDX:COL_IDX + NIDX]),
                                 (d[:, :, NIDX:NIDX + NH], w[:, :, COL_F:COL_F + NH])])
                for c in range(PC):
                    sp.dma_start(LFC[:, c * 48:c * 48 + 48].rearrange("p (b h) -> p b h", b=NB),
                                 t["cache_fox_logf"][l][:, c * P:c * P + P, :].rearrange("b p h -> p b h")).then_inc(gc_full, 16)
                for c in range(PC):
                    sp.dma_start(KIC[:, c, :].rearrange("p (b d) -> p b d", b=NB),
                                 t["cache_dsa_kidx"][l][:, c * P:c * P + P, :].rearrange("b p d -> p b d")).then_inc(ki_full, 16)
                for g in range(2):
                    sp.wait_ge(p_ready, l * 30 + 27 + 3 * g)
                    load(U_GATE + g, by_k(U_GATE + g, w, COL_GATE + g * MIX, MIX))
                sp.wait_ge(nf_stored, l * 16 + 16)
                for b in range(NB):
                    sp.dma_start(GS[b * NH:(b + 1) * NH, PAST:KEYS],
                                 t["o_fox_logf_s"][l, b].rearrange("t h -> h t"),
                                 allow_slow_non_contiguous=True).then_inc(gn_full, 16)
                sp.wait_ge(g_ready, l * 2 + 1)
                sp.dma_start(g_s, GX[0:48, :]).then_inc(g_stored, 16)
                sp.wait_ge(g_ready, l * 2 + 2)
                sp.dma_start(g_p, RSTD[0:NH, 0:NPROMPT]).then_inc(g_stored, 16)
                def gates(g):
                    u = U_GATE + g
                    sp.wait_ge(gate_ready, l * 24 + 3 * (g - 1))
                    load(u, by_k(u, w, COL_GATE + g * MIX, MIX))

                for g in range(2, 7):
                    gates(g)
                sp.wait_ge(g_stored, l * 32 + 32)
                sp.wait_ge(is_done, l + 1)
                sp.dma_start(GB, g_p.rearrange("(o h) k -> o h k", o=1).to_broadcast([P, NH, NPROMPT])).then_inc(gb_full, 16)
                sp.wait_ge(msk_ready, l * 3 + 3)
                sp.dma_start(m_s, WK).then_inc(msk_stored, 16)
                gates(7)
                sp.wait_ge(stored, l * 208 + 208)
                settle(sp)
                sp.wait_ge(po_copied, l * 6 + 6)
                sp.wait_ge(msk_stored, l * 16 + 16)
                settle(sp)
                def load_keys(b0, j):
                    b, r = b0 + j // 3, j % 3
                    st = l * NSTEP + b0 * 3 + j
                    ck = t[("cache_sb_k", "cache_fox_k", "cache_dsa_k")[r]]
                    nk = t[("o_sb_k_s", "o_fox_k_s", "o_dsa_k_s")[r]]
                    sp.wait_ge(k_used, st + 1)
                    settle(sp)
                    sp.dma_start(KC[:, j % 2, 0:PC, :],
                                 ck[l, b].rearrange("(c p) h d -> p c (h d)", p=P)).then_inc(k_full[j % 2], 16)
                    sp.dma_start(KC[0:NT, j % 2, PC, :], nk[l, b].rearrange("t h d -> t (h d)")).then_inc(k_full[j % 2], 16)
                    if r != SB:
                        sp.wait_ge(zs_ready, st)
                        settle(sp)
                    for h in range(NH):
                        if r == FOX:
                            sp.dma_start(BFX[h * NT:(h + 1) * NT, :],
                                         g_s[bass.ds(b * NH + h, 1), :].to_broadcast([NT, KEYS])).then_inc(bfx_full, 16)
                        if r == DSA:
                            sp.dma_start(BDX[h * NT:(h + 1) * NT, :],
                                         m_s[bass.ds(b * NT, NT), :]).then_inc(bdx_full, 16)

                def load_step(b0, j):
                    b, r = b0 + j // 3, j % 3
                    if has(b0, j + 1):
                        load_keys(b0, j + 1)
                    cv = t[("cache_sb_v", "cache_fox_v", "cache_dsa_v")[r]]
                    nv = t[("o_sb_v_s", "o_fox_v_s", "o_dsa_v_s")[r]]
                    sp.wait_ge(pv_ready, l * NSTEP + b0 * 3 + (j + 1))
                    settle(sp)
                    sp.dma_start(VC[:, j % 2, 0:PC, :],
                                 cv[l, b].rearrange("(c p) h d -> p c (h d)", p=P)).then_inc(v_full[j % 2], 16)
                    sp.dma_start(VC[0:NT, j % 2, PC, :], nv[l, b].rearrange("t h d -> t (h d)")).then_inc(v_full[j % 2], 16)

                load_keys(0, 0)
                sweep(sp, load_step)
                w = t["w_branch"][l].rearrange("n (k p) d -> p (n k) d", p=P)
                for i in range(N_BRANCH):
                    u = U_BRANCH + i
                    if i < 2:
                        sp.wait_ge(gate_ready, l * 24 + 21 + 3 * i)
                    else:
                        sp.wait_ge(br_ready, l * 24 + 6 * (i - 1))
                    load(u, by_k(u, w, i * 256, 256, k=9))
                w = t["w_out"][l].rearrange("(k p) n -> p k n", p=P)
                for i in range(N_WOUT):
                    u = U_WOUT + i
                    sp.wait_ge(br_ready, l * 24 + 18 + 6 * i)
                    load(u, by_k(u, w, i * 512, 512))
                swiglu_weights(l, 1, [lambda: sp.wait_ge(y_ready, l * 24 + Y_BASE[2] + 4),
                                      lambda: sp.wait_ge(y_ready, l * 24 + Y_BASE[2] + 8)])

        @block.tensor
        def _(pe):
            def full(l, u0, more=0):
                pe.wait_ge(slot_full[u0 % 2], l * (16 * UNITS) + more * 32 + 32 * (u0 // 2 + 1))

            pe.wait_ge(in_x, 32)
            pe.wait_ge(in_k, 80)
            for g in range(6):
                pe.wait_ge(xt_free, g + 1)
                for j in range(4):
                    k, tt = 4 * (g % 2) + j, g // 2
                    mm = pe.transpose(PS[:, g % 2, j * P:(j + 1) * P],
                                      qr(tt * 1024 + k * P, P), IDENT[:, :])
                mm.then_inc(xt_ready, 1)
            pe.wait_ge(c_ready, 1)
            for k in range(KD):
                mm = pe.transpose(PS[:, 2, k * NC:(k + 1) * NC], BIG[0:NC, 3 * D + k * P:3 * D + (k + 1) * P], IDENT[0:NC, 0:NC])
            mm.then_inc(ct_ready, 1)
            pe.wait_ge(x_turned, 1)
            pe.wait_ge(c_silu, 1)

            def mean_square(l, n):
                for k in range(KD):
                    pe.wait_ge(sq_ready, l * 48 + (8 * n + k + 1))
                    mm = pe.matmul(PS[:, 6, 0:T], ONES[:, :], SQ[:, k, :], start=(k == 0), stop=(k == KD - 1))
                mm.then_inc(ms_ready, 1)

            def h_is_ready(l, i):
                pe.wait_ge(hs_ready, l * 3 + (i + 1))
                pe.wait_ge(hp_ready, l * 24 + (8 * i + 8))

            def ada_unit(l, a, w):
                for k in range(KD):
                    for j in range(4):
                        mm = pe.matmul(PS[32 * j:32 * j + 32, 4, 0:P], CT[:, k, :], w[:, k, j * P:(j + 1) * P],
                                       start=(k == 0), stop=(k == KD - 1))
                mm.then_inc(acc_ready, 1)

            def ada_turned(l, a):
                pe.wait_ge(ar_ready, l * N_ADA + a + 1)
                pe.wait_ge(mod_free, l * N_ADA + a + 1)
                pe.transpose(PS[:, 5, 0:P], AR[:, :], IDENT[:, :]).then_inc(mod_ready, 1)

            def swiglu_in(l, f):
                u = U_IN[f]

                def unit(j, i):
                    full(l, u + j, i)
                    w = ring((u + j) % 2, KD, 512)
                    for jj in range(2):
                        pe.wait_ge(gu_free, l * 44 + i * 4 + (22 * f + 2 * j + jj + 1))
                        for part in range(2):
                            for k in range(KD):
                                mm = pe.matmul(PS[:, 2 * jj + part, 0:T],
                                               w[:, k, part * 256 + jj * P:part * 256 + (jj + 1) * P], H[:, k, :],
                                               start=(k == 0), stop=(k == KD - 1))
                        mm.then_inc(gu_ready, 1)
                        if f == 0 and jj == 0:
                            pe.wait_ge(ada_full, l * 384 + i * 64 + (32 * j + 32))
                            ada_unit(l, i * 2 + (N_ADA0 + j), ADA)
                    if f == 0:
                        ada_turned(l, i * 2 + (N_ADA0 + j))
                with loop(pe, 0, 5) as i:
                    unit(0, i)
                    unit(1, i)
                full(l, u + 10)
                w = ring((u + 10) % 2, KD, 512)
                for jj in range(2):
                    pe.wait_ge(gu_free, l * 44 + (22 * f + 20 + jj + 1))
                    for part in range(2):
                        for k in range(KD):
                            mm = pe.matmul(PS[:, 2 * jj + part, 0:T],
                                           w[:, k, part * 256 + jj * P:part * 256 + (jj + 1) * P], H[:, k, :],
                                           start=(k == 0), stop=(k == KD - 1))
                    mm.then_inc(gu_ready, 1)
                    if f == 0 and jj == 0:
                        pe.wait_ge(ada_full, l * 384 + 352)
                        ada_unit(l, N_ADA0 + 10, ADA)
                if f == 0:
                    ada_turned(l, N_ADA0 + 10)

            def swiglu_out(l, f):
                u = U_OUT[f]
                pe.wait_ge(gu_free, l * 44 + (22 * f + 24))
                with loop(pe, 0, 4) as mp:
                    for half in range(2):
                        full(l, u + half, mp)
                        w = ring((u + half) % 2, NFF // 2, 256)
                        for m in range(2):
                            if half == 0:
                                pe.wait_ge(y_free, l * 24 + mp * 2 + (Y_BASE[f] + m + 1))
                            for k in range(NFF // 2):
                                mm = pe.matmul(PS[:, m, 0:T], w[:, k, m * P:(m + 1) * P],
                                               HID[:, half * (NFF // 2) + k, :],
                                               start=(half == 0 and k == 0), stop=(half == 1 and k == NFF // 2 - 1))
                            if half == 1:
                                mm.then_inc(y_ready, 1)
                        if half == 0:
                            mm.then_inc(half_used, 1)

            with pe.Fori(0, DEPTH) as l:
                pe.wait_ge(bg_full, l * 32 + 32)
                pe.transpose(PS[:, 7, 0:120], BGR[0:120, :], IDENT[0:120, 0:120]).then_inc(bg_ready, 1)
                for a in range(N_ADA0):
                    full(l, a)
                    ada_unit(l, a, ring(a % 2, KD, 512))
                    ada_turned(l, a)
                mean_square(l, 0)
                h_is_ready(l, 0)
                swiglu_in(l, 0)
                swiglu_out(l, 0)
                pe.wait_ge(ada_full, l * 384 + 384)
                ada_unit(l, N_ADA - 1, ADA)
                mean_square(l, 1)
                ada_turned(l, N_ADA - 1)
                mean_square(l, 2)
                h_is_ready(l, 1)
                for i in range(N_PROJ):
                    full(l, U_PROJ + i)
                    width = MIX if i < 9 else NIDX + NH
                    w = ring((U_PROJ + i) % 2, KD, width)
                    for tt in range(TT):
                        pe.wait_ge(p_free, l * 30 + (3 * i + tt + 1))
                        for k in range(KD):
                            mm = pe.matmul(PS[:, tt, 0:width], H[:, k, tt * P:(tt + 1) * P], w[:, k, :],
                                           start=(k == 0), stop=(k == KD - 1))
                        mm.then_inc(p_ready, 1)
                pe.wait_ge(p_free, l * 30 + 30 + 3)
                pe.wait_ge(gc_full, l * 64 + 64)
                pe.wait_ge(logf_ready, l + 1)
                settle(pe)
                for c in range(PC):
                    pe.transpose(PS[0:48, 5, c * P:(c + 1) * P], LFC[:, c * 48:c * 48 + 48], IDENT[:, :])
                for tt in range(2):
                    mm = pe.transpose(PS[0:NH, 6, tt * P:(tt + 1) * P], LF[:, 0, tt, :], IDENT[:, :])
                mm.then_inc(gt_ready, 1)
                def gate_tile(n, bank):
                    u = U_GATE + n // 3
                    if n % 3 == 0:
                        full(l, u)
                    if n >= 2:
                        pe.wait_ge(gexp_ready, l * 24 + (n if bank == 4 else n - 1))
                    w = ring(u % 2, KD, MIX)
                    for k in range(KD):
                        mm = pe.matmul(PS[:, bank, 0:T], w[:, k, (n % 3) * P:(n % 3 + 1) * P], H[:, k, :],
                                       start=(k == 0), stop=(k == KD - 1))
                    mm.then_inc(gate_ready, 1)

                for n in range(GATES[0]):
                    gate_tile(n, n % 2)
                pe.wait_ge(rope_done, l + 1)
                n = 0
                for r in range(NBR):
                    for tt in range(TT):
                        for i in range(2 if tt < 2 else 1):
                            pe.wait_ge(qk_free, l * 15 + (n + 1))
                            for a in range(NPAIR):
                                mm = pe.transpose(PS[:, 3 + n % 2, a * P:(a + 1) * P],
                                                  QK[:, r, tt, i * MIX + a * P:i * MIX + (a + 1) * P], IDENT[:, :])
                            mm.then_inc(qk_ready, 1)
                            n += 1
                pe.wait_ge(dup_ready, l + 1)
                pe.wait_ge(gt_copied, l + 1)
                for tt in range(2):
                    pe.wait_ge(it_free, l * 8 + (tt + 1))
                    for a in range(2):
                        pe.transpose(PS[:, 5 + tt, a * P:(a + 1) * P], IDX[:, tt, a * P:(a + 1) * P], IDENT[:, :])
                    pe.transpose(PS[:, 5 + tt, 2 * P:3 * P], KI2[:, tt, :], IDENT[:, :]).then_inc(it_ready, 1)
                pe.wait_ge(it_free, l * 8 + 3)
                for h in range(IH):
                    mm = pe.transpose(PS[:, 5, h * P:(h + 1) * P], QI2[:, h, :], IDENT[:, :])
                mm.then_inc(it_ready, 1)
                pe.wait_ge(it_free, l * 8 + 4)
                pe.transpose(PS[:, 6, 0:P], KI2[:, 2, :], IDENT[:, :]).then_inc(it_ready, 1)
                pe.wait_ge(ki_full, l * 64 + 64)
                for bp in range(4):
                    pe.wait_ge(it_free, l * 8 + (5 + bp))
                    for c in range(PC):
                        mm = pe.transpose(PS[:, 5 + bp % 2, c * P:(c + 1) * P], KIC[:, c, bp * P:(bp + 1) * P], IDENT[:, :])
                    mm.then_inc(it_ready, 1)
                pe.wait_ge(qk_free, l * 15 + 17)
                pe.wait_ge(gexp_ready, l * 24 + GATES[0])
                pe.wait_ge(it_free, l * 8 + 4)
                for qt in range(2):
                    for h in range(IH):
                        s = slice(64 * (h % 2), 64 * (h % 2) + 64)
                        mm = pe.matmul(PS[:, 2 * qt + h % 2, (h // 2) * 256:(h // 2) * 256 + 256],
                                       QIT[s, h // 2, qt * P:(qt + 1) * P], KITP[s, :], start=True, stop=True)
                    mm.then_inc(is_ready, 1)
                pe.wait_ge(it_free, l * 8 + 10)
                for h in range(IH):
                    if h >= 2:
                        pe.wait_ge(relu_ready, l * 6 + (h + 1))
                    for half in range(2):
                        for bp in range(4):
                            mm = pe.matmul(PS[:, 4 + 2 * (h % 2) + half, 0:264], QIP[:, h, bp * P:(bp + 1) * P],
                                           KIT[:, bp, half * 264:(half + 1) * 264], start=(bp == 0), stop=(bp == 3))
                    mm.then_inc(is_ready, 1)
                pe.wait_ge(relu_ready, l * 6 + 6)
                for n in range(GATES[0], GATES[1]):
                    gate_tile(n, n % 2)
                pe.wait_ge(gexp_ready, l * 24 + GATES[1])
                for it in range(6):
                    r, qt = it // 2, it % 2
                    if it:
                        pe.wait_ge(z_ready, l * 6 + it)
                    for h in range(NH):
                        s = slice(64 * (h % 2), 64 * (h % 2) + 64)
                        mm = pe.matmul(PS[:, 2 * (h % 2) + h // 4, (h // 2 % 2) * 256:(h // 2 % 2) * 256 + 256],
                                       QKT[s, r, 0, h // 2, qt * P:(qt + 1) * P], QKT[s, r, 1, h // 2, :],
                                       start=True, stop=True)
                    mm.then_inc(s_ready, 1)
                    for n in range(GATE_AT[it], GATE_AT[it + 1]):
                        gate_tile(n, 4)
                    pe.wait_ge(p_done, l * 6 + (it + 1))
                    for g in range(3):
                        n = 3 * it + g
                        if n >= 2:
                            pe.wait_ge(pt_copied, l * 18 + (n - 1))
                        for j in range(4):
                            mm = pe.transpose(PS[:, 5 + n % 2, j * P:(j + 1) * P],
                                              EP[:, 2 * g + j // 2, (j % 2) * P:(j % 2 + 1) * P], IDENT[:, :])
                        mm.then_inc(pt_ready, 1)
                    if it:
                        pe.wait_ge(po_copied, l * 6 + it)
                    pe.wait_ge(pt_copied, l * 18 + (3 * it + 3))
                    for h in range(NH):
                        for kt in range(2):
                            mm = pe.matmul(PS[64 * (h % 2):64 * (h % 2) + 64, 7, (h // 2) * P:(h // 2 + 1) * P],
                                           VT[:, r, kt, h * HD:(h + 1) * HD],
                                           PTP[:, (h % 2) * NPAIR + h // 2, kt, :],
                                           start=(kt == 0), stop=(kt == 1))
                    mm.then_inc(po_ready, 1)
                pe.wait_ge(po_copied, l * 6 + 6)

                def turn(b0, j):
                    s = j % 2
                    pe.wait_ge(k_full[s], l * (NSTEP * 16) + b0 * 48 + 32 * (j // 2 + 1))
                    pe.wait_ge(kt_free, l * NSTEP + b0 * 3 + (j + 1))
                    for a in range(NPAIR):
                        for c in range(PC):
                            pe.transpose(PS[:, a, c * P:(c + 1) * P], KC[:, s, c, a * P:(a + 1) * P], IDENT[:, :])
                    for a in range(NPAIR):
                        mm = pe.transpose(PS[:, 3, a * NT:(a + 1) * NT], KC[0:NT, s, PC, a * P:(a + 1) * P], IDENT[0:NT, 0:NT])
                    mm.then_inc(kt_ready, 1)

                def output(b0, j):
                    pe.wait_ge(ou_ready, l * NSTEP + b0 * 3 + (j + 2))
                    settle(pe)
                    pe.transpose(PS[:, 7, P:P + 96], OU[0:96, :], IDENT[0:96, 0:96]).then_inc(o_ready, 1)

                def probs_and_values(b0, j):
                    st = l * NSTEP + b0 * 3 + j
                    pe.wait_ge(ps_ready, st + 1)
                    for c in range(PC):
                        pe.transpose(PS[:, 6, c * 96:(c + 1) * 96], ES[j % 2][0:96, c * P:(c + 1) * P], IDENT[0:96, 0:96])
                    pe.transpose(PS[0:NT, 6, 384:480], ES[j % 2][0:96, PAST:KEYS], IDENT[0:96, 0:96]).then_inc(st_ready, 1)
                    pe.wait_ge(v_full[j % 2], l * (NSTEP * 16) + b0 * 48 + 32 * (j // 2 + 1))
                    pe.wait_ge(ou_ready, st + 1)
                    pe.wait_ge(o_free, st + 1)
                    pe.wait_ge(st_copied, st + 1)
                    for c in range(PC + 1):
                        n = P if c < PC else NT
                        for a in range(NPAIR):
                            mm = pe.matmul(PS[32 * a:32 * a + 32, 7, 0:P], PTS[0:n, c, a * 32:(a + 1) * 32],
                                           VC[0:n, j % 2, c, a * P:(a + 1) * P], start=(c == 0), stop=(c == PC))
                    mm.then_inc(pv_ready, 1)

                def step(b0, j):
                    st = l * NSTEP + b0 * 3 + j
                    pe.wait_ge(kt_free, st + 2)
                    pe.wait_ge(qc_ready, st + 1)
                    pe.wait_ge(zs_ready, st + 2)
                    for half in range(2):
                        for a in range(NPAIR):
                            mm = pe.matmul(PS[32 * a:32 * a + 32, 4 + half, 0:264], QC[:, j % 2, a * 32:(a + 1) * 32],
                                           KT[:, a, half * 264:(half + 1) * 264], start=True, stop=True)
                    mm.then_inc(ss_ready, 1)
                    if has(b0, j + 1):
                        turn(b0, j + 1)
                    if has(b0, j - 2):
                        output(b0, j - 2)
                    if has(b0, j - 1):
                        probs_and_values(b0, j - 1)

                turn(0, 0)
                sweep(pe, step)
                output(NB - 2, 4)
                probs_and_values(NB - 2, 5)
                output(NB - 2, 5)
                pe.wait_ge(gate_done, l * 24 + 24)
                pe.wait_ge(o_free, l * 24 + 24 + 1)
                for i in range(N_BRANCH):
                    full(l, U_BRANCH + i)
                    w = ring((U_BRANCH + i) % 2, 9, 256)
                    for m in range(2):
                        for n in range(NBR):
                            pe.wait_ge(br_free, l * 24 + (6 * i + 3 * m + n + 1))
                            for k in range(NPAIR):
                                mm = pe.matmul(PS[:, n, 0:T], w[:, 3 * n + k, m * P:(m + 1) * P], OT[:, 3 * n + k, :],
                                               start=(k == 0), stop=(k == NPAIR - 1))
                            mm.then_inc(br_ready, 1)
                pe.wait_ge(mg_ready, l * 8 + 8)
                for i in range(N_WOUT):
                    full(l, U_WOUT + i)
                    w = ring((U_WOUT + i) % 2, KD, 512)
                    for m in range(4):
                        pe.wait_ge(y_free, l * 24 + (Y_BASE[2] + 4 * i + m + 1))
                        for k in range(KD):
                            mm = pe.matmul(PS[:, m % 2, 0:T], w[:, k, m * P:(m + 1) * P], MG[:, k, :],
                                           start=(k == 0), stop=(k == KD - 1))
                        mm.then_inc(y_ready, 1)
                mean_square(l, 3)
                mean_square(l, 4)
                h_is_ready(l, 2)
                swiglu_in(l, 1)
                swiglu_out(l, 1)
                mean_square(l, 5)
            pe.wait_ge(x_ready, 8 + 48)
            for g in range(6):
                pe.wait_ge(xt_free, 6 + g + 1)
                for j in range(4):
                    k, tt = 4 * (g % 2) + j, g // 2
                    mm = pe.transpose(PS[:, g % 2, j * P:(j + 1) * P], X[:, k, tt * P:(tt + 1) * P], IDENT[:, :])
                mm.then_inc(xt_ready, 1)

        @block.scalar
        def _(act):
            begin, link = chained(act, ach)
            A = nc.scalar.activation
            act.wait_ge(in_c, 32)
            A(BIG[0:NC, D:2 * D], BIG[0:NC, 0:D], ACT.Exp, scale=-1.0).then_inc(c_act, 1)
            for g in range(6):
                act.wait_ge(xt_ready, g + 1)
                ins = A(X[:, 4 * (g % 2):4 * (g % 2) + 4, (g // 2) * P:(g // 2 + 1) * P],
                        PS[:, g % 2, :].rearrange("p (k t) -> p k t", k=4), ACT.Copy)
                ins.then_inc(xt_free, 1)
            act.wait_ge(xt_free, 2 + 6)
            act.sem_inc(x_turned, 1)

            def squares_of_x(l, n, i):
                for k in range(KD):
                    act.wait_ge(x_ready, l * 24 + (8 * i + k + 1))
                    A(SQ[:, k, :], X[:, k, :], ACT.Square).then_inc(sq_ready, 1)

            def rstd(l, n):
                begin()
                act.wait_ge(var_ready, l * 6 + (n + 1))
                link(A(VAR[:, :], VAR[:, :], ACT.Ln))
                A(RSTD[:, :], VAR[:, :], ACT.Exp, scale=-0.5).then_inc(rstd_ready, 1)

            def modulate_prompt(l, i):
                act.wait_ge(xr_ready, l * 3 + (i + 1))
                act.wait_ge(coef_ready, l * 2 + min(i + 1, 2))
                for k in range(KD):
                    A(H[:, k, 0:NPROMPT], SQ[:, k, 0:NPROMPT], ACT.Identity,
                      scale=MOD[:, (3 * i + 1) * KD + k, 0:1], bias=MOD[:, 3 * i * KD + k, 0:1]).then_inc(hp_ready, 1)

            def swiglu_in(l, f):
                with by_two(act, 0, 22) as j:
                    for jj in range(2):
                        act.wait_ge(gu_free, l * 44 + j + (22 * f + jj + 1))
                        act.wait_ge(gu_ready, l * 44 + j + (22 * f + jj + 1))
                        A(FE[:, jj, :], PS[:, 2 * jj, 0:T], ACT.Exp, scale=-1.0).then_inc(eg_ready, 1)

            def take_y(l, base):
                with by_two(act, 0, KD) as m:
                    for j in range(2):
                        begin()
                        act.wait_ge(y_ready, l * 24 + m + (base + j + 1))
                        A(Y[:, m + j, :], PS[:, j, 0:T], ACT.Copy).then_inc(y_free, 1)
                        act.wait_ge(y_free, l * 24 + m + (base + j + 1 + 2))
                        A(SQ[:, m + j, :], Y[:, m + j, :], ACT.Square).then_inc(sq_ready, 1)

            with act.Fori(0, DEPTH) as l:
                squares_of_x(l, 0, 0)
                rstd(l, 0)
                modulate_prompt(l, 0)
                swiglu_in(l, 0)
                take_y(l, Y_BASE[0])
                rstd(l, 1)
                squares_of_x(l, 2, 1)
                rstd(l, 2)
                modulate_prompt(l, 1)
                for i in range(N_PROJ):
                    for tt in range(TT):
                        act.wait_ge(p_ready, l * 30 + (3 * i + tt + 1))
                        if i < 9:
                            dst = VT[:, i // 3, tt, :] if i % 3 == 2 else QK[:, i // 3, tt, (i % 3) * MIX:(i % 3 + 1) * MIX]
                            A(dst, PS[:, tt, 0:MIX], ACT.Copy).then_inc(p_free, 1)
                        else:
                            begin()
                            link(A(IDX[:, tt, :], PS[:, tt, 0:NIDX], ACT.Copy))
                            A(FREG[:, tt, 0:NH], PS[:, tt, NIDX:NIDX + NH], ACT.Copy).then_inc(p_free, 1)
                act.wait_ge(logf_arg, l + 1)
                begin()
                link(A(LF[:, 1, :, :], LF[:, 0, :, :], ACT.Abs))
                link(A(LF[:, 1, :, :], LF[:, 1, :, :], ACT.Exp, scale=-1.0))
                A(LF[:, 2, :, :], LF[:, 1, :, :], ACT.Ln, bias=1.0).then_inc(logf_exp, 1)
                act.wait_ge(logf_ready, l + 1)
                act.dma_start(t["o_fox_logf_s"][l].rearrange("b t h -> (b t) h"), LF[:, 0, 2, :]).then_inc(nf_stored, 16)
                act.dma_start(t["o_fox_logf_p"][l].rearrange("o (t p) h -> p (o t) h", p=P), LF[:, 0, 0:2, :]).then_inc(stored, 16)
                act.wait_ge(gt_ready, l + 1)
                begin()
                link(A(GS[0:48, 0:PAST], PS[0:48, 5, :], ACT.Copy))
                A(VAR[0:NH, 0:NPROMPT], PS[0:NH, 6, 0:NPROMPT], ACT.Copy).then_inc(gt_copied, 1)
                def e_gate(n, bank):
                    act.wait_ge(gate_ready, l * 24 + (n + 1))
                    A(G[:, n, :], PS[:, bank, 0:T], ACT.Exp, scale=-1.0).then_inc(gexp_ready, 1)

                act.wait_ge(p_free, l * 30 + 33)
                for name, r, src in (("sb_k", SB, QK), ("sb_v", SB, VT), ("fox_k", FOX, QK), ("fox_v", FOX, VT),
                                     ("dsa_v", DSA, VT), ("dsa_k", DSA, QK)):
                    if name == "dsa_k":
                        for n in range(GATES[0]):
                            e_gate(n, n % 2)
                        act.wait_ge(rope_done, l + 1)
                    cols = slice(0, MIX) if src is VT else slice(MIX, 2 * MIX)
                    act.dma_start(t[f"o_{name}_p"][l].rearrange("o (t p) h d -> p (o t) (h d)", p=P),
                                  src[:, r, 0:2, cols]).then_inc(stored, 16)
                    act.dma_start(t[f"o_{name}_s"][l].rearrange("b t h d -> (b t) (h d)"), src[:, r, 2, cols]).then_inc(stored, 16)
                act.dma_start(t["o_dsa_kidx_p"][l].rearrange("o (t p) d -> p (o t) d", p=P), IDX[:, 0:2, IH * HD:IH * HD + HD]).then_inc(kidx_stored, 16)
                act.dma_start(t["o_dsa_kidx_s"][l].rearrange("b t d -> (b t) d"), IDX[:, 2, IH * HD:IH * HD + HD]).then_inc(kidx_stored, 16)
                n = 0
                for r in range(NBR):
                    for tt in range(TT):
                        for i in range(2 if tt < 2 else 1):
                            act.wait_ge(qk_ready, l * 15 + (n + 1))
                            src = PS[:, 3 + n % 2, 0:MIX].rearrange("p (a t) -> p a t", a=NPAIR)
                            if tt < 2:
                                A(QKT[:, r, i, :, tt * P:(tt + 1) * P], src, ACT.Copy).then_inc(qk_free, 1)
                            else:
                                src = src.rearrange("p a (b t) -> p a b t", b=NB)
                                begin()
                                link(A(QBLK[0:64, r, :, :, 0:NT], src[0:64], ACT.Copy))
                                A(QBLK[64:128, r, :, :, NT:2 * NT], src[64:128], ACT.Copy).then_inc(qk_free, 1)
                            n += 1
                act.wait_ge(qip_zero, l + 1)
                for tt in range(2):
                    act.wait_ge(it_ready, l * 8 + (tt + 1))
                    begin()
                    link(A(QIT[:, :, tt * P:(tt + 1) * P], PS[:, 5 + tt, 0:2 * P].rearrange("p (a t) -> p a t", a=2), ACT.Copy))
                    A(KITP[:, tt * P:(tt + 1) * P], PS[:, 5 + tt, 2 * P:3 * P], ACT.Copy).then_inc(it_free, 1)
                act.wait_ge(it_ready, l * 8 + 3)
                begin()
                for par in range(2):
                    s = slice(64 * par, 64 * par + 64)
                    for h in range(IH):
                        dst = QIP[s, h, :].rearrange("p (i c) -> p i c", c=160)[:, :, NT * par:NT * par + NT]
                        src = PS[s, 5, h * P:(h + 1) * P].rearrange("p (i z t) -> p i z t", z=2, t=NT)[:, :, par, :]
                        ins = A(dst, src, ACT.Copy)
                        if par == 0 or h < IH - 1:
                            link(ins)
                ins.then_inc(it_free, 1)
                act.wait_ge(it_ready, l * 8 + 4)
                begin()
                src = PS[:, 6, 0:P].rearrange("p (i z t) -> p i z t", z=2, t=NT)
                link(A(KIT[0:64, :, PAST:KEYS], src[0:64, :, 0, :], ACT.Copy))
                A(KIT[64:128, :, PAST:KEYS], src[64:128, :, 1, :], ACT.Copy).then_inc(it_free, 1)
                for bp in range(4):
                    act.wait_ge(it_ready, l * 8 + (5 + bp))
                    A(KIT[:, bp, 0:PAST], PS[:, 5 + bp % 2, :], ACT.Copy).then_inc(it_free, 1)
                for n in range(6):
                    act.wait_ge(is_ready, l * 6 + (n + 1))
                    act.wait_ge(relu_free, l * 6 + (n + 1))
                    if n < 2:
                        A(RL.rearrange("p (h k) -> p h k", h=IH), PS[:, 2 * n:2 * n + 2, :].rearrange("p b (h k) -> p (b h) k", h=2),
                          ACT.Relu, scale=1 / 16).then_inc(relu_ready, 1)
                    else:
                        A(RL[:, 0:KEYS].rearrange("p (s k) -> p s k", s=2), PS[:, 4 + 2 * (n % 2):6 + 2 * (n % 2), 0:264],
                          ACT.Relu, scale=1 / 16).then_inc(relu_ready, 1)
                for n in range(GATES[0], GATES[1]):
                    e_gate(n, n % 2)
                for it in range(6):
                    r = it // 2
                    begin()
                    act.wait_ge(z_ready, l * 6 + (it + 1))
                    if r == SB:
                        link(A(EP, ZP, ACT.Abs))
                        link(A(EP, EP, ACT.Exp, scale=-1.0))
                        A(LP, EP, ACT.Ln, bias=1.0).then_inc(e_ready, 1)
                        act.wait_ge(soft_ready, l * 6 + (it + 1))
                        A(EP, ZP, ACT.Exp).then_inc(p_done, 1)
                    else:
                        for h in range(NH):
                            ins = A(EP[:, h, :], ZP[:, h, :], ACT.Exp, bias=ST[:, h:h + 1], accum_out=ST[:, 8 + h:9 + h])
                            if h < NH - 1:
                                link(ins)
                        ins.then_inc(e_ready, 1)
                    for n in range(GATE_AT[it], GATE_AT[it + 1]):
                        e_gate(n, 4)
                    for g in range(3):
                        act.wait_ge(pt_ready, l * 18 + (3 * it + g + 1))
                        A(PTP[:, 2 * g:2 * g + 2, :, :], PS[:, 5 + (3 * it + g) % 2, :].rearrange("p (h k q) -> p h k q", h=2, k=2),
                          ACT.Copy).then_inc(pt_copied, 1)
                    act.wait_ge(po_ready, l * 6 + (it + 1))
                    A(OT[:, 3 * r:3 * r + 3, (it % 2) * P:(it % 2 + 1) * P],
                      PS[:, 7, 0:MIX].rearrange("p (a q) -> p a q", a=NPAIR), ACT.Copy).then_inc(po_copied, 1)
                def turned_keys(b0, j):
                    act.wait_ge(kt_ready, l * NSTEP + b0 * 3 + (j + 1))
                    act.sem_inc(k_used, 1)
                    link(A(KT[:, :, 0:PAST], PS[:, 0:NPAIR, :], ACT.Copy))
                    A(KT[:, :, PAST:KEYS], PS[:, 3, 0:NPAIR * NT].rearrange("p (a t) -> p a t", a=NPAIR), ACT.Copy).then_inc(kt_free, 1)

                def turned_probs(b0, j):
                    st = l * NSTEP + b0 * 3 + j
                    act.wait_ge(st_ready, st + 1)
                    link(A(PTS[:, 0:PC, :], PS[:, 6, 0:384].rearrange("p (c q) -> p c q", q=96), ACT.Copy))
                    A(PTS[0:NT, PC, :], PS[0:NT, 6, 384:480], ACT.Copy).then_inc(st_copied, 1)

                def step(b0, j):
                    st = l * NSTEP + b0 * 3 + j
                    e = ES[j % 2]
                    begin()
                    act.wait_ge(zs_ready, st + 3)
                    if j % 3 == SB:
                        link(A(e[0:96, :], ZS[0:96, :], ACT.Abs))
                        link(A(e[0:96, :], e[0:96, :], ACT.Exp, scale=-1.0))
                        A(LS[0:96, :], e[0:96, :], ACT.Ln, bias=1.0).then_inc(es_ready, 1)
                    else:
                        A(e[0:96, :], ZS[0:96, :], ACT.Exp, bias=ST[0:96, 0:1], accum_out=ST[0:96, 8:9]).then_inc(es_ready, 1)
                    if has(b0, j + 1):
                        turned_keys(b0, j + 1)
                    if has(b0, j - 1):
                        turned_probs(b0, j - 1)
                    if j % 3 == SB:
                        act.wait_ge(ls_ready, st + 1)
                        A(e[0:96, :], ZS[0:96, :], ACT.Exp).then_inc(ps_ready, 1)

                begin()
                turned_keys(0, 0)
                sweep(act, step)
                begin()
                turned_probs(NB - 2, 5)
                take_y(l, Y_BASE[2])
                rstd(l, 3)
                squares_of_x(l, 4, 2)
                rstd(l, 4)
                modulate_prompt(l, 2)
                swiglu_in(l, 1)
                take_y(l, Y_BASE[1])
                rstd(l, 5)
            for g in range(6):
                act.wait_ge(xt_ready, 6 + g + 1)
                k0, tt = 4 * (g % 2), g // 2
                A(qr(tt * 1024 + k0 * P, 512), PS[:, g % 2, :], ACT.Copy).then_inc(xt_free, 1)
            act.wait_ge(xt_free, 2 + 12)
            act.dma_start(t["o_y_p"].rearrange("o (t p) d -> p (o t) d", p=P), qr(0, 2048).rearrange("p (t d) -> p t d", t=2)).then_inc(out_stored, 16)
            act.dma_start(t["o_y_s"].rearrange("b t d -> (b t) d"), qr(2048, 1024)).then_inc(out_stored, 16)
            act.wait_ge(out_stored, 32)

        @block.vector
        def _(dve):
            begin, link = chained(dve, vch)
            V = nc.vector
            for s, n in ((xt_free, 2), (gu_free, 2), (y_free, 2), (mod_free, 1), (bg_free, 1), (p_free, 3), (qk_free, 2),
                         (it_free, 2), (relu_free, 1), (o_free, 1), (kt_free, 1), (pv_ready, 2), (ou_ready, 1), (br_free, 3),
                         (k_used, 2), (zs_ready, 2)):
                dve.sem_inc(s, n)
            begin()
            link(V.memset(ONES[:, :], 1.0))
            link(V.memset(ZERO[:, :], 0.0))
            link(V.memset(QBLK, 0.0))
            link(V.memset(CT, 0.0))
            dve.wait_ge(c_act, 1)
            c, e, f, g = (BIG[0:NC, i * D:(i + 1) * D] for i in range(4))
            link(V.tensor_scalar(f, e, 1.0, None, ALU.add))
            link(V.reciprocal(e, f))
            V.tensor_tensor(g, c, e, ALU.mult).then_inc(c_ready, 1)
            dve.wait_ge(ct_ready, 1)
            link(V.tensor_copy(CT[:, :, 0:NC], PS[:, 2, 0:KD * NC].rearrange("p (k c) -> p k c", c=NC)))
            dve.wait_ge(x_turned, 1)
            dve.sem_inc(x_ready, KD)
            dve.sem_inc(c_silu, 1)

            def variance(l, n):
                dve.wait_ge(ms_ready, l * 6 + (n + 1))
                V.tensor_scalar(VAR[:, :], PS[:, 6, 0:T], 1.0 / D, EPS, ALU.mult, ALU.add).then_inc(var_ready, 1)
                dve.wait_ge(rstd_ready, l * 6 + (n + 1))

            def every_chunk(ap):
                return ap[:, None, :].to_broadcast([P, KD, T])

            def pre_norm(l, n, i):
                variance(l, n)
                begin()
                V.tensor_tensor(SQ, X, every_chunk(RSTD), ALU.mult).then_inc(xr_ready, 1)
                dve.wait_ge(xr_ready, l * 3 + (i + 1))
                m = 3 * i * KD
                link(V.tensor_tensor(sample_cols(H), sample_cols(SQ), per_conditioning(MOD[:, m + KD:m + 2 * KD, :]), ALU.mult))
                V.tensor_tensor(sample_cols(H), sample_cols(H), per_conditioning(MOD[:, m:m + KD, :]), ALU.add).then_inc(hs_ready, 1)

            def post_norm(l, n, i):
                variance(l, n)
                begin()
                m = (3 * i + 2) * KD
                link(V.tensor_tensor(Y, Y, every_chunk(RSTD), ALU.mult))
                link(V.tensor_tensor(sample_cols(SQ), sample_cols(Y), per_conditioning(MOD[:, m:m + KD, :]), ALU.mult))
                link(V.tensor_tensor(sample_cols(X), sample_cols(X), sample_cols(SQ), ALU.add))
                for k in range(KD):
                    V.scalar_tensor_tensor(out=X[:, k, 0:NPROMPT], in0=Y[:, k, 0:NPROMPT], scalar=MOD[:, m + k, 0:1],
                                           in1=X[:, k, 0:NPROMPT], op0=ALU.mult, op1=ALU.add).then_inc(x_ready, 1)
                dve.wait_ge(x_ready, l * 24 + (8 * (i + 1) + 8))

            def ada_rows(l, a):
                dve.wait_ge(acc_ready, l * N_ADA + a + 1)
                V.tensor_copy(AR[:, :], PS[:, 4, 0:P]).then_inc(ar_ready, 1)

            def ada_columns(l, a):
                dve.wait_ge(mod_ready, l * N_ADA + a + 1)
                V.tensor_tensor(MOD[:, bass.ds(a * 4, 4), :], PS[:, 5, 0:P].rearrange("p (m c) -> p m c", c=32)[:, :, 0:NC],
                                BG[:, bass.ds(a * 4, 4)][..., None].to_broadcast([P, 4, NC]), ALU.add).then_inc(mod_free, 1)
                dve.wait_ge(mod_free, l * N_ADA + a + 2)

            def coefficients(l, parts):
                begin()
                for i in parts:
                    m = 3 * i * KD
                    gain = [BG[:, 72 + (2 * i + z) * KD:72 + (2 * i + z + 1) * KD][..., None].to_broadcast([P, KD, NC]) for z in range(2)]
                    link(V.scalar_tensor_tensor(out=MOD[:, m + KD:m + 2 * KD, :], in0=MOD[:, m + KD:m + 2 * KD, :], scalar=1.0,
                                                in1=gain[0], op0=ALU.add, op1=ALU.mult))
                    link(V.scalar_tensor_tensor(out=MOD[:, m + 2 * KD:m + 3 * KD, :], in0=MOD[:, m + 2 * KD:m + 3 * KD, :],
                                                scalar=(1.0 if i == 1 else 0.5), in1=gain[1], op0=ALU.mult, op1=ALU.mult))

            def swiglu_in(l, f):
                with loop(dve, 0, NFF // 2) as i:
                    j = i * 2
                    for jj in range(2):
                        begin()
                        dve.wait_ge(eg_ready, l * 44 + j + (22 * f + jj + 1))
                        link(V.tensor_scalar(FE[:, jj, :], FE[:, jj, :], 1.0, None, ALU.add))
                        link(V.reciprocal(FT[:, jj, :], FE[:, jj, :]))
                        link(V.tensor_tensor(FT[:, jj, :], PS[:, 2 * jj, 0:T], FT[:, jj, :], ALU.mult))
                        V.tensor_tensor(HID[:, j + jj, :], PS[:, 2 * jj + 1, 0:T], FT[:, jj, :], ALU.mult).then_inc(gu_free, 1)
                        if f == 0 and jj == 0:
                            ada_rows(l, i + N_ADA0)
                    if f == 0:
                        ada_columns(l, i + N_ADA0)
                dve.wait_ge(gu_free, l * 44 + (22 * f + 24))

            def rotate(x, heads, tt):
                n = heads * HD
                x = x.rearrange("p (h s d) -> p h s d", s=2, d=32)
                a = RT[:, 0:n].rearrange("p (h s d) -> p h s d", s=2, d=32)
                b = RT[:, 768:768 + n].rearrange("p (h s d) -> p h s d", s=2, d=32)
                cos = ROPE[:, tt, 0, :][:, None, None, :].to_broadcast([P, heads, 2, 32])
                sin = ROPE[:, tt, 1, :][:, None, :].to_broadcast([P, heads, 32])
                link(V.tensor_tensor(a, x, cos, ALU.mult))
                link(V.tensor_tensor(b[:, :, 0, :], x[:, :, 1, :], sin, ALU.mult))
                link(V.tensor_tensor(b[:, :, 1, :], x[:, :, 0, :], sin, ALU.mult))
                link(V.tensor_tensor(x[:, :, 0, :], a[:, :, 0, :], b[:, :, 0, :], ALU.subtract))
                link(V.tensor_tensor(x[:, :, 1, :], a[:, :, 1, :], b[:, :, 1, :], ALU.add))

            def reverse_scan(out, terms, more, n):
                return V.tensor_tensor_scan(out[:, ::-1], terms[:, ::-1], more[:, ::-1], 0.0, ALU.add, ALU.add)

            def choose(keys, rounds, rest):
                w = WK[:, 0:keys]
                with loop(dve, 0, rounds) as _:
                    begin()
                    link(V.max(M8, w))
                    link(V.match_replace(w, M8, w, TAKEN))
                begin()
                if rest:
                    link(V.max(M8, w))
                    link(V.memset(M8[:, rest:8], TAKEN))
                    link(V.match_replace(w, M8, w, TAKEN))

            with dve.Fori(0, DEPTH) as l:
                begin()
                dve.wait_ge(bg_ready, l + 1)
                V.tensor_copy(BG[:, :], PS[:, 7, 0:120]).then_inc(bg_free, 1)
                dve.wait_ge(bg_free, l + 2)
                for a in range(N_ADA0):
                    ada_rows(l, a)
                    ada_columns(l, a)
                coefficients(l, (0,))
                dve.sem_inc(coef_ready, 1)
                pre_norm(l, 0, 0)
                swiglu_in(l, 0)
                ada_rows(l, N_ADA - 1)
                ada_columns(l, N_ADA - 1)
                coefficients(l, (1, 2))
                dve.sem_inc(coef_ready, 1)
                post_norm(l, 1, 0)
                pre_norm(l, 2, 1)
                dve.wait_ge(p_free, l * 30 + 33)
                dve.wait_ge(bf_full, l * 16 + 16)
                begin()
                V.tensor_tensor(LF[:, 0, :, :], FREG[:, :, 0:NH], BF[:, None, :].to_broadcast([P, TT, NH]), ALU.add).then_inc(logf_arg, 1)
                dve.wait_ge(logf_exp, l + 1)
                V.scalar_tensor_tensor(out=LF[:, 0, :, :], in0=LF[:, 0, :, :], scalar=0.0, in1=LF[:, 2, :, :],
                                       op0=ALU.min, op1=ALU.subtract).then_inc(logf_ready, 1)
                dve.wait_ge(gt_copied, l + 1)
                dve.wait_ge(gn_full, l * 128 + 128)
                begin()
                link(V.memset(GX[0:48, KEYS - 1:KEYS], 0.0))
                reverse_scan(GX[0:48, 0:KEYS - 1], GS[0:48, 1:KEYS], ZERO[0:48, 1:KEYS], 0).then_inc(g_ready, 1)
                link(V.memset(RSTD[0:NH, NPROMPT - 1:NPROMPT], 0.0))
                reverse_scan(RSTD[0:NH, 0:NPROMPT - 1], VAR[0:NH, 1:NPROMPT], ZERO[0:NH, 1:NPROMPT], 0).then_inc(g_ready, 1)
                dve.wait_ge(g_stored, l * 32 + 32)
                for tt in range(TT):
                    rotate(QK[:, DSA, tt, :], 2 * NH, tt)
                    rotate(IDX[:, tt, 0:5 * HD], 5, tt)
                dve.sem_inc(rope_done, 1)
                dve.wait_ge(qk_free, l * 15 + 17)
                dve.wait_ge(stored, l * 208 + 208)
                for z in range(2):
                    link(V.tensor_copy(KI2[:, :, z * HD:(z + 1) * HD], IDX[:, :, IH * HD:(IH + 1) * HD]))
                    link(V.tensor_copy(QI2[:, :, z * HD:(z + 1) * HD], IDX[:, 2, 0:IH * HD].rearrange("p (h d) -> p h d", h=IH)))
                dve.sem_inc(dup_ready, 1)
                V.memset(QIP, 0.0).then_inc(qip_zero, 1)
                for qt in range(2):
                    begin()
                    w = IDX[:, qt, (IH + 1) * HD:]
                    dve.wait_ge(relu_ready, l * 6 + (qt + 1))
                    dve.wait_ge(qip_zero, l + 1)
                    link(V.tensor_scalar(ISC[:, 0:256], RL[:, 0:256], w[:, 0:1], None, ALU.mult))
                    for h in range(1, IH):
                        ins = V.scalar_tensor_tensor(out=ISC[:, 0:256], in0=by_parity(RL, h, IH, 256), scalar=w[:, h:h + 1],
                                                     in1=ISC[:, 0:256], op0=ALU.mult, op1=ALU.add)
                        link(ins)
                    dve.sem_inc(relu_free, 1)
                    link(V.tensor_tensor(WK[:, 0:256], ISC[:, 0:256], MASKS[:, 2, qt, :], ALU.add))
                    choose(NPROMPT, TOPK_P // 8, TOPK_P % 8)
                    V.tensor_scalar(DMB[:, qt, :], WK[:, 0:256], TAKEN / 2, NEG, ALU.is_gt, ALU.mult).then_inc(msk_ready, 1)
                    dve.wait_ge(msk_ready, l * 3 + (qt + 1))
                w = IDX[:, 2, (IH + 1) * HD:]
                begin()
                for h in range(IH):
                    dve.wait_ge(relu_ready, l * 6 + (3 + h))
                    if h == 0:
                        link(V.tensor_scalar(WK, RL[:, 0:KEYS], w[:, 0:1], None, ALU.mult))
                    else:
                        link(V.scalar_tensor_tensor(out=WK, in0=RL[:, 0:KEYS], scalar=w[:, h:h + 1], in1=WK,
                                                    op0=ALU.mult, op1=ALU.add))
                    dve.sem_inc(relu_free, 1)
                choose(KEYS, TOPK_S // 8, TOPK_S % 8)
                V.tensor_scalar(WK, WK, TAKEN / 2, NEG, ALU.is_gt, ALU.mult).then_inc(msk_ready, 1)
                dve.wait_ge(msk_ready, l * 3 + 3)
                dve.wait_ge(kidx_stored, l * 32 + 32)
                dve.sem_inc(is_done, 1)
                for it in range(6):
                    r, qt = it // 2, it % 2
                    begin()
                    dve.wait_ge(s_ready, l * 6 + (it + 1))
                    if r == FOX:
                        dve.wait_ge(gb_full, l * 16 + 16)
                    for z in range(2):
                        S = PS[:, 2 * z:2 * z + 2, :].rearrange("p b (h k) -> p (b h) k", h=2)[:, 0:NPAIR, :]
                        bias = (MASKS[:, 0, qt, :], None, DMB[:, qt, :])[r]
                        bias = GB[:, z::2, :] if r == FOX else bias[:, None, :].to_broadcast([P, NPAIR, NPROMPT])
                        link(V.scalar_tensor_tensor(out=ZP[:, z * NPAIR:(z + 1) * NPAIR, :], in0=S, scalar=SCALE, in1=bias,
                                                    op0=ALU.mult, op1=ALU.add))
                    if r == FOX:
                        link(V.tensor_tensor(ZP, ZP, MASKS[:, 1, qt, :][:, None, :].to_broadcast([P, NH, NPROMPT]), ALU.add))
                    if r == SB:
                        dve.sem_inc(z_ready, 1)
                        dve.wait_ge(e_ready, l * 6 + (it + 1))
                        link(V.scalar_tensor_tensor(out=LP, in0=ZP, scalar=0.0, in1=LP, op0=ALU.max, op1=ALU.add))
                        for h in range(NH):
                            link(reverse_scan(EP[:, h, :], LP[:, h, :], ZERO[:, 0:NPROMPT], 0))
                        V.tensor_tensor(ZP, ZP, EP, ALU.subtract).then_inc(soft_ready, 1)
                        dve.wait_ge(soft_ready, l * 6 + (it + 1))
                        dve.wait_ge(p_done, l * 6 + (it + 1))
                    else:
                        link(V.tensor_reduce(ST[:, 0:NH], ZP, AXX, ALU.max, negate=True))
                        dve.sem_inc(z_ready, 1)
                        dve.wait_ge(e_ready, l * 6 + (it + 1))
                        link(V.reciprocal(ST[:, 16:16 + NH], ST[:, 8:8 + NH]))
                        dve.sem_inc(soft_ready, 1)
                        V.tensor_tensor(EP, EP, ST[:, 16:16 + NH][..., None].to_broadcast([P, NH, NPROMPT]), ALU.mult).then_inc(p_done, 1)
                        dve.wait_ge(p_done, l * 6 + (it + 1))
                dve.wait_ge(po_copied, l * 6 + 6)
                dve.wait_ge(gexp_ready, l * 24 + 24)
                def output(b0, j):
                    b, r = b0 + j // 3, j % 3
                    dve.wait_ge(o_ready, l * NSTEP + b0 * 3 + (j + 1))
                    src = PS[:, 7, P:P + 96].rearrange("p (a c) -> p a c", a=NPAIR)
                    o = OT[:, 3 * r:3 * r + 3, bass.ds(b * NT + NPROMPT, NT)]
                    link(V.tensor_copy(o[0:64], src[0:64, :, 0:NT]))
                    V.tensor_copy(o[64:128], src[64:128, :, NT:2 * NT]).then_inc(o_free, 1)

                def output_rows(b0, j):
                    dve.wait_ge(pv_ready, l * NSTEP + b0 * 3 + (j + 3))
                    V.tensor_copy(OU[0:96, :], PS[0:96, 7, 0:P]).then_inc(ou_ready, 1)

                def queries(b0, j):
                    b, r = b0 + j // 3, j % 3
                    V.tensor_copy(QC[:, j % 2, :].rearrange("p (a c) -> p a c", a=NPAIR), QBLK[:, r, :, b, :]).then_inc(qc_ready, 1)

                def step(b0, j):
                    b, r = b0 + j // 3, j % 3
                    st = l * NSTEP + b0 * 3 + j
                    e = ES[j % 2]

                    def beside():
                        if has(b0, j + 1):
                            queries(b0, j + 1)
                        if has(b0, j - 2) and r != SB:
                            output(b0, j - 2)
                        g = G[:, b0 * 3 + j, :]
                        link(V.tensor_scalar(g, g, 1.0, None, ALU.add))
                        V.reciprocal(g, g).then_inc(gate_done, 1)
                        if has(b0, j - 2) and r == SB:
                            output(b0, j - 2)

                    begin()
                    dve.wait_ge(ss_ready, st + 1)
                    if r == FOX:
                        dve.wait_ge(bfx_full, l * (NB * 96) + b * 96 + 96)
                    if r == DSA:
                        dve.wait_ge(bdx_full, l * (NB * 96) + b * 96 + 96)
                    bias = (BSB, BFX, BDX)[r][0:96, :].rearrange("p (s k) -> p s k", s=2)
                    link(V.scalar_tensor_tensor(out=ZS[0:96, :].rearrange("p (s k) -> p s k", s=2), in0=PS[0:96, 4:6, 0:264],
                                                scalar=SCALE, in1=bias, op0=ALU.mult, op1=ALU.add))
                    if r == FOX:
                        link(V.tensor_tensor(ZS[0:96, PAST:KEYS], ZS[0:96, PAST:KEYS], MFOX[0:96, :], ALU.add))
                    if r == SB:
                        dve.sem_inc(zs_ready, 1)
                        beside()
                        dve.wait_ge(es_ready, st + 1)
                        link(V.scalar_tensor_tensor(out=LS[0:96, :], in0=ZS[0:96, :], scalar=0.0, in1=LS[0:96, :],
                                                    op0=ALU.max, op1=ALU.add))
                        link(reverse_scan(e[0:96, :], LS[0:96, :], ZERO[0:96, :], 0))
                        V.tensor_tensor(ZS[0:96, :], ZS[0:96, :], e[0:96, :], ALU.subtract).then_inc(ls_ready, 1)
                    else:
                        link(V.tensor_reduce(ST[0:96, 0:1], ZS[0:96, :], AXX, ALU.max, negate=True))
                        dve.sem_inc(zs_ready, 1)
                        dve.wait_ge(es_ready, st + 1)
                        link(V.reciprocal(ST[0:96, 16:17], ST[0:96, 8:9]))
                        dve.sem_inc(ls_ready, 1)
                        V.tensor_scalar(e[0:96, :], e[0:96, :], ST[0:96, 16:17], None, ALU.mult).then_inc(ps_ready, 1)
                        beside()
                    if has(b0, j - 1):
                        output_rows(b0, j - 1)
                    if r == SB:
                        dve.wait_ge(ps_ready, st + 1)

                begin()
                queries(0, 0)
                sweep(dve, step)
                begin()
                output(NB - 2, 4)
                output_rows(NB - 2, 5)
                output(NB - 2, 5)
                dve.wait_ge(o_free, l * 24 + 25)
                with loop(dve, 0, KD) as m:
                    begin()
                    for n in range(NBR):
                        dve.wait_ge(br_ready, l * 24 + m * 3 + (n + 1))
                        g = G[:, m + n * KD, :]
                        dst = MG[:, m, :] if n == 0 else MGT
                        V.tensor_tensor(dst, PS[:, n, 0:T], g, ALU.mult).then_inc(br_free, 1)
                        dve.wait_ge(br_free, l * 24 + m * 3 + (n + 4))
                        if n:
                            link(V.tensor_tensor(MG[:, m, :], MG[:, m, :], MGT, ALU.add))
                    dve.sem_inc(mg_ready, 1)
                post_norm(l, 3, 1)
                pre_norm(l, 4, 2)
                swiglu_in(l, 1)
                post_norm(l, 5, 2)


_INS = ["x_prompt", "x_sample", "cache_sb_k", "cache_sb_v", "cache_fox_k", "cache_fox_v", "cache_fox_logf",
        "cache_dsa_k", "cache_dsa_v", "cache_dsa_kidx", "c_prompt", "c_sample", "norm_g", "w_ada", "b_ada",
        "ffn_w_in", "ffn_w_out", "w_in", "b_forget", "w_branch", "w_out"]
_P, _S = (DEPTH, 1, NPROMPT), (DEPTH, NB, NT)
_STATE = [("sb_k", (NH, HD)), ("sb_v", (NH, HD)), ("fox_k", (NH, HD)), ("fox_v", (NH, HD)), ("fox_logf", (NH,)),
          ("dsa_k", (NH, HD)), ("dsa_v", (NH, HD)), ("dsa_kidx", (HD,))]
_OUTS = ([("o_y_p", (1, NPROMPT, D)), ("o_y_s", (NB, NT, D))]
         + [(f"o_{n}_p", _P + s) for n, s in _STATE] + [(f"o_{n}_s", _S + s) for n, s in _STATE])


def shape_constants():
    import numpy as np
    q = np.arange(NPROMPT).reshape(2, P, 1)
    k = np.arange(NPROMPT).reshape(1, 1, NPROMPT)
    masks = np.stack([np.where(k < q, 0, NEG), np.where(k <= q, 0, NEG), np.where(k // 64 <= q // 64, 0, NEG)])
    pos = np.concatenate([np.arange(NPROMPT), np.tile(PAST + np.arange(NT), NB)]).astype(np.float32)
    inv = np.float32(10000.0) ** (-np.arange(32, dtype=np.float32) / np.float32(32))
    ang = (pos[:, None] * inv[None, :]).astype(np.float32)
    rope = np.stack([np.cos(ang), np.sin(ang)], 1).reshape(TT, P, 2, 32)
    tq = np.tile(np.arange(NT), NH)[:, None]
    tk = np.arange(NT)[None, :]
    bsb = np.zeros((NH * NT, KEYS))
    bsb[:, PAST:] = np.where(tk < tq, 0, NEG)
    arrays = {
        "k_masks": masks.transpose(2, 0, 1, 3), "k_ident": np.eye(P), "k_rope": rope.transpose(1, 0, 2, 3),
        "k_bsb": bsb, "k_mfox": np.where(tk <= tq, 0, NEG),
    }
    return {n: np.ascontiguousarray(a, dtype=np.float32) for n, a in arrays.items()}


def kernel(**inputs):
    import numpy as _np
    import concourse.bacc as _bacc
    from concourse import mybir as _mybir
    from concourse.bass_utils import run_bass_kernel_spmd as _run

    nc = _bacc.Bacc("TRN2", target_bir_lowering=False, num_devices=1)
    arrays = {n: _np.ascontiguousarray(inputs[n]) for n in _INS}
    arrays.update(shape_constants())
    t = {n: nc.dram_tensor(n, a.shape, _mybir.dt.from_np(a.dtype), kind="ExternalInput").ap() for n, a in arrays.items()}
    t.update({n: nc.dram_tensor(n, s, F32, kind="ExternalOutput").ap() for n, s in _OUTS})
    program(nc, t)
    r = _run(nc, [arrays], core_ids=[0])
    return tuple(r.results[0][n] for n, _ in _OUTS)
```

```python
import concourse.bass as bass
from concourse import mybir
from contextlib import ExitStack, contextmanager

ALU = mybir.AluOpType
ACT = mybir.ActivationFunctionType
AXX = mybir.AxisListType.X
F32 = mybir.dt.float32

P = 128
D = 1024
KD = D // P
NPROMPT = 256
NB = 8
NT = 16
NSAMPLE = NB * NT
T = NPROMPT + NSAMPLE
TT = T // P
DEPTH = 2
PAST = 512
KEYS = PAST + NT
PC = PAST // P
NH = 6
HD = 64
NPAIR = NH // 2
MIX = NH * HD
NBR = 3
SB, FOX, DSA = range(NBR)
IH = 4
FF = 2816
NFF = FF // P
NC = 9
NMOD = 9
EPS = 1e-6
SCALE = HD ** -0.5
TOPK_P = NPROMPT // 4
TOPK_S = KEYS // 4
NEG = -1e30
TAKEN = -3e38

COL_QKV = [0, 3 * MIX, 6 * MIX + NH]
COL_F = 6 * MIX
COL_IDX = 9 * MIX + NH
NIDX = IH * HD + HD + IH
COL_GATE = COL_IDX + NIDX

GATES = [6, 8, 9, 16]
GATE_AT = [16, 18, 20, 21, 22, 23, 24]

N_IN, N_OUT, N_PROJ, N_GATE, N_BRANCH, N_WOUT = 11, 8, 10, 8, 4, 2
N_ADA = 18
N_ADA0 = 6
U_IN = [N_ADA0, 0]
U_OUT = [U_IN[0] + N_IN, 0]
U_PROJ = U_OUT[0] + N_OUT
U_GATE = U_PROJ + N_PROJ
U_BRANCH = U_GATE + N_GATE
U_WOUT = U_BRANCH + N_BRANCH
U_IN[1] = U_WOUT + N_WOUT
U_OUT[1] = U_IN[1] + N_IN
UNITS = U_OUT[1] + N_OUT
assert UNITS % 2 == 0

Y_BASE = [0, 2 * KD, KD]
NSTEP = NB * NBR


def program(nc, t):
    with ExitStack() as ctx:
        def sb(name, width):
            return ctx.enter_context(nc.sbuf_tensor(name, [P, width], F32))

        def sem(name):
            return ctx.enter_context(nc.semaphore(name))

        X = sb("X", KD * T)[:, :].rearrange("p (k t) -> p k t", k=KD)
        H = sb("H", KD * T)[:, :].rearrange("p (k t) -> p k t", k=KD)
        BIG = sb("BIG", 24 * T)
        QR = sb("QR", 12960)
        RING = sb("RING", 2 * 4096)
        QKT = sb("QKT", NBR * 2 * NPAIR * NPROMPT)[:, :].rearrange(
            "p (r i a t) -> p r i a t", r=NBR, i=2, a=NPAIR)
        QBLK = sb("QBLK", NBR * NPAIR * NB * 32)[:, :].rearrange(
            "p (r a b c) -> p r a b c", r=NBR, a=NPAIR, b=NB)
        OTR = sb("OT", NBR * NPAIR * T)
        OT = OTR[:, :].rearrange("p (g t) -> p g t", t=T)
        MOD = sb("MOD", NMOD * KD * NC)[:, :].rearrange("p (m c) -> p m c", c=NC)
        BGR = sb("BGR", P)
        BG = sb("BG", 120)
        MASKS = sb("MASKS", 3 * 2 * NPROMPT)[:, :].rearrange("p (r q k) -> p r q k", r=3, q=2)
        IDENT = sb("IDENT", P)
        ONES = sb("ONES", 32)
        MEAN = sb("MEAN", P)
        EPSC = sb("EPSC", 1)
        ROPE = sb("ROPE", TT * 2 * 32)[:, :].rearrange("p (t s d) -> p t s d", t=TT, s=2)
        ZERO = sb("ZERO", KEYS)
        BSB = sb("BSB", KEYS)
        MFOX = sb("MFOX", NT)
        RSTD = sb("RSTD", T)
        VAR = sb("VAR", T)
        CT = sb("CT", KD * 32)[:, :].rearrange("p (k c) -> p k c", c=32)
        AR = sb("AR", P)
        DMB = sb("DMB", 2 * NPROMPT)[:, :].rearrange("p (q k) -> p q k", q=2)
        QC = sb("QC", 2 * 96)[:, :].rearrange("p (s c) -> p s c", s=2)
        OU = sb("OU", P)
        ST = sb("ST", 64)
        LF = sb("LF", 3 * TT * NH)[:, :].rearrange("p (s t h) -> p s t h", s=3, t=TT)
        BF = sb("BF", NH)
        FREG = sb("FREG", TT * 8)[:, :].rearrange("p (t h) -> p t h", t=TT)

        def big(off, n):
            return BIG[:, off:off + n]

        def qr(off, n):
            return QR[:, off:off + n]

        HID = big(0, NFF * T).rearrange("p (j t) -> p j t", t=T)
        G = big(0, 24 * T).rearrange("p (j t) -> p j t", t=T)
        Y = qr(0, KD * T).rearrange("p (k t) -> p k t", t=T)
        SQ = qr(3072, KD * T).rearrange("p (k t) -> p k t", t=T)
        MG = qr(6144, KD * T).rearrange("p (k t) -> p k t", t=T)
        MGT = qr(9216, T)
        FE = qr(6144, 2 * T).rearrange("p (j t) -> p j t", t=T)
        FT = qr(6144 + 2 * T, 2 * T).rearrange("p (j t) -> p j t", t=T)
        ADA = qr(8192, KD * 512).rearrange("p (k w) -> p k w", w=512)
        QK = qr(0, NBR * TT * 2 * MIX).rearrange("p (r t c) -> p r t c", r=NBR, t=TT)
        VT = qr(6912, NBR * TT * MIX).rearrange("p (r t c) -> p r t c", r=NBR, t=TT)
        QX = 10368
        GS, GX, LFC = qr(QX, KEYS), qr(QX + KEYS, KEYS), qr(QX + 2 * KEYS, PC * 48)
        RT = qr(QX, 2304)
        RL, ISC, WK = qr(QX, 1024), qr(QX + 1024, KEYS), qr(QX + 1024 + KEYS, KEYS)
        M8 = ST[:, 56:64]
        IDX = OTR[:, 0:TT * NIDX].rearrange("p (t c) -> p t c", t=TT)
        o = TT * NIDX
        KI2 = OTR[:, o:o + TT * P].rearrange("p (t c) -> p t c", t=TT); o += TT * P
        KIC = OTR[:, o:o + PC * NB * HD].rearrange("p (c w) -> p c w", c=PC); o += PC * NB * HD
        assert o <= NBR * NPAIR * T
        o = 0
        QI2 = qr(o, IH * P).rearrange("p (h c) -> p h c", h=IH); o += IH * P
        KIT = qr(o, 4 * KEYS).rearrange("p (b k) -> p b k", b=4); o += 4 * KEYS
        QIP = qr(o, IH * 640).rearrange("p (h c) -> p h c", h=IH); o += IH * 640
        QIT = qr(o, 2 * NPROMPT).rearrange("p (a t) -> p a t", a=2); o += 2 * NPROMPT
        KITP = qr(o, NPROMPT); o += NPROMPT
        assert o <= 6912
        ZP, EP, LP = (qr(i * 1536, 1536).rearrange("p (h k) -> p h k", h=NH) for i in range(3))
        PTP = qr(3 * 1536, 1536).rearrange("p (h k q) -> p h k q", h=NH, k=2)
        GB = qr(QX, 1536).rearrange("p (h k) -> p h k", h=NH)
        KC = qr(0, 3840).rearrange("p (s c w) -> p s c w", s=2, c=PC + 1)
        VC = qr(3840, 3840).rearrange("p (s c w) -> p s c w", s=2, c=PC + 1)
        KT = qr(7680, NPAIR * KEYS).rearrange("p (a k) -> p a k", a=NPAIR)
        o = 7680 + NPAIR * KEYS
        ZS, ES0, ES1, LS, BFX, BDX = (qr(o + i * KEYS, KEYS) for i in range(6))
        ES = (ES0, ES1)
        PTS = qr(o + 6 * KEYS, 480).rearrange("p (c q) -> p c q", q=96)
        o += 6 * KEYS + 480
        assert o <= 12960

        def by_parity(ap, h, heads, width):
            n = (h % 2) * (heads // 2) + h // 2
            return ap[:, n * width:(n + 1) * width]

        def ring(s, k, w):
            return RING[:, s * 4096:s * 4096 + k * w].rearrange("p (k w) -> p k w", w=w)

        PS = ctx.enter_context(nc.psum_tensor("PS", [P, 8, 512], F32))

        g_s = nc.dram_tensor("scr_g_sample", (NB * NH, KEYS), F32, kind="Internal").ap()
        g_p = nc.dram_tensor("scr_g_prompt", (NH, NPROMPT), F32, kind="Internal").ap()
        m_s = nc.dram_tensor("scr_mask_sample", (NSAMPLE, KEYS), F32, kind="Internal").ap()

        in_x, in_c, in_k = sem("in_x"), sem("in_c"), sem("in_k")
        c_act, c_silu, c_ready, ct_ready = sem("c_act"), sem("c_silu"), sem("c_ready"), sem("ct_ready")
        xt_ready, xt_free, x_turned = sem("xt_ready"), sem("xt_free"), sem("x_turned")
        settled = sem("settled")
        vch, ach = sem("vector_chain"), sem("scalar_chain")
        slot_full = [sem("slot_full0"), sem("slot_full1")]
        bg_full, bg_ready, bg_free = sem("bg_full"), sem("bg_ready"), sem("bg_free")
        acc_ready, ar_ready, ada_full = sem("acc_ready"), sem("ar_ready"), sem("ada_full")
        mod_ready, mod_free, coef_ready = sem("mod_ready"), sem("mod_free"), sem("coef_ready")
        sq_ready, sums_ready, sums_copied, ms_ready, rstd_ready = sem("sq_ready"), sem("sums_ready"), sem("sums_copied"), sem("ms_ready"), sem("rstd_ready")
        xc_ready, ys_ready = sem("xc_ready"), sem("ys_ready")
        h_ready, hs_ready, x_ready = sem("h_ready"), sem("hs_ready"), sem("x_ready")
        gu_ready, sig_ready, gu_free, half_used = sem("gu_ready"), sem("sig_ready"), sem("gu_free"), sem("half_used")
        y_ready, y_free = sem("y_ready"), sem("y_free")
        p_ready, p_free = sem("p_ready"), sem("p_free")
        rope_done, logf_exp, logf_ready = sem("rope_done"), sem("logf_exp"), sem("logf_ready")
        logf_arg = sem("logf_arg")
        stored, nf_stored, kidx_stored = sem("stored"), sem("nf_stored"), sem("kidx_stored")
        qk_ready, qk_free = sem("qk_ready"), sem("qk_free")
        bf_full, gc_full, gn_full = sem("bf_full"), sem("gc_full"), sem("gn_full")
        gt_ready, gt_copied, g_ready, g_stored, gb_full = sem("gt_ready"), sem("gt_copied"), sem("g_ready"), sem("g_stored"), sem("gb_full")
        ki_full, dup_ready = sem("ki_full"), sem("dup_ready")
        it_ready, it_free, qip_zero = sem("it_ready"), sem("it_free"), sem("qip_zero")
        is_ready, relu_ready, relu_free, is_done = sem("is_ready"), sem("relu_ready"), sem("relu_free"), sem("is_done")
        msk_ready, msk_stored = sem("msk_ready"), sem("msk_stored")
        s_ready, z_ready, e_ready = sem("ps_ready"), sem("pz_ready"), sem("pe_ready")
        p_done, pt_ready, pt_copied = sem("p_probs_ready"), sem("ppt_ready"), sem("ppt_copied")
        po_ready, po_copied = sem("ppo_ready"), sem("ppo_copied")
        k_full = [sem("k_full0"), sem("k_full1")]
        v_full = [sem("v_full0"), sem("v_full1")]
        k_used, o_ready, o_free = sem("k_used"), sem("o_ready"), sem("o_free")
        pv_ready, ou_ready = sem("pv_ready"), sem("ou_ready")
        kt_ready, kt_free = sem("kt_ready"), sem("kt_free")
        qc_ready, ss_ready, zs_ready, es_ready = sem("qc_ready"), sem("ss_ready"), sem("zs_ready"), sem("es_ready")
        ps_ready = sem("sprobs_ready")
        st_ready, st_copied = sem("st_ready"), sem("st_copied")
        bfx_full, bdx_full = sem("bfx_full"), sem("bdx_full")
        gate_ready, gate_taken = sem("gate_ready"), sem("gate_taken")
        br_ready, br_free, mg_ready = sem("br_ready"), sem("br_free"), sem("mg_ready")
        out_stored = sem("out_stored")

        block = ctx.enter_context(nc.Block())

        def settle(eng):
            eng.sem_inc(settled, 1)

        @contextmanager
        def loop(eng, start, end):
            settle(eng)
            with eng.Fori(start, end) as i:
                yield i

        def chained(eng, chain):
            n = [0]

            def begin():
                settle(eng)
                eng.sem_clear(chain)
                n[0] = 0

            def link(ins):
                n[0] += 1
                ins.then_inc(chain, 1)
                eng.wait_ge(chain, n[0])
            return begin, link

        def sample_cols(ap):
            return ap[:, :, NPROMPT:T].rearrange("p k (b t) -> p k b t", b=NB)

        @contextmanager
        def by_two(eng, start, end):
            with loop(eng, start // 2, end // 2) as half:
                yield half * 2

        def sweep(eng, step):
            step(0, 0)
            step(0, 1)
            with by_two(eng, 0, NB - 2) as b0:
                for j in range(2, 8):
                    step(b0, j)
            for j in range(2, 6):
                step(NB - 2, j)

        def has(b0, j):
            return not isinstance(b0, int) or 0 <= b0 * NBR + j < NSTEP

        @block.sync
        def _(sp):
            sp.dma_start(qr(0, 2048).rearrange("p (t d) -> p t d", t=2),
                         t["x_prompt"].rearrange("o (t p) d -> p (o t) d", p=P)).then_inc(in_x, 16)
            sp.dma_start(qr(2048, 1024), t["x_sample"].rearrange("b t d -> (b t) d")).then_inc(in_x, 16)
            sp.dma_start(BIG[0:1, 0:D], t["c_prompt"]).then_inc(in_c, 16)
            sp.dma_start(BIG[1:NC, 0:D], t["c_sample"]).then_inc(in_c, 16)
            sp.dma_start(MASKS, t["k_masks"]).then_inc(in_k, 16)
            sp.dma_start(IDENT[:, :], t["k_ident"]).then_inc(in_k, 16)
            sp.dma_start(ROPE, t["k_rope"]).then_inc(in_k, 16)
            sp.dma_start(BSB[0:96, :], t["k_bsb"]).then_inc(in_k, 16)
            sp.dma_start(MFOX[0:96, :], t["k_mfox"]).then_inc(in_k, 16)

            def load(u, parts):
                s = u % 2
                for dst, src in parts:
                    sp.dma_start(dst, src).then_inc(slot_full[s], 16)

            def ffn_in(l, f, u, i):
                w = t["ffn_w_in"][l, f].rearrange("(k p) n -> p k n", p=P)
                d = ring(u % 2, KD, 512)
                return [(d[:, :, 0:256], w[:, :, bass.ds(i * 256, 256)]),
                        (d[:, :, 256:512], w[:, :, bass.ds(i * 256 + FF, 256)])]

            def ffn_out(l, f, u, mp, half):
                w = t["ffn_w_out"][l, f].rearrange("(k p) n -> p k n", p=P)
                d = ring(u % 2, NFF // 2, 256)
                k0 = half * (NFF // 2)
                return [(d[:, a:b, :], w[:, k0 + a:k0 + b, bass.ds(mp * 256, 256)]) for a, b in ((0, 6), (6, 11))]

            def by_k(u, w, col, width, k=KD):
                d = ring(u % 2, k, width)
                h = k // 2
                return [(d[:, a:b, :], w[:, a:b, bass.ds(col, width)]) for a, b in ((0, h), (h, k))]

            def swiglu_weights(l, f, before, beside=None):
                u = U_IN[f]
                for i in range(2):
                    before[i]()
                    load(u + i, ffn_in(l, f, u + i, i))
                if beside:
                    beside(0)
                with by_two(sp, 2, 10) as i:
                    for j in range(2):
                        if beside:
                            beside(i + (j - 1))
                        sp.wait_ge(gu_ready, l * 44 + i * 2 + (22 * f + 2 * j - 2))
                        load(u + j, ffn_in(l, f, u + j, i + j))
                if beside:
                    beside(9)
                sp.wait_ge(gu_ready, l * 44 + (22 * f + 18))
                load(u + 10, ffn_in(l, f, u + 10, 10))
                u = U_OUT[f]
                if beside:
                    beside(10)
                sp.wait_ge(gu_ready, l * 44 + (22 * f + 20))
                load(u, ffn_out(l, f, u, 0, 0))
                if beside:
                    beside(11)
                sp.wait_ge(gu_ready, l * 44 + (22 * f + 22))
                load(u + 1, ffn_out(l, f, u + 1, 0, 1))
                with loop(sp, 1, 4) as mp:
                    sp.wait_ge(half_used, l * 8 + mp + 4 * f)
                    load(u, ffn_out(l, f, u, mp, 0))
                    sp.wait_ge(y_ready, l * 24 + mp * 2 + Y_BASE[f])
                    load(u + 1, ffn_out(l, f, u + 1, mp, 1))

            with sp.Fori(0, DEPTH) as l:
                sp.wait_ge(bg_free, l + 1)
                sp.dma_start(BGR[0:72, :], t["b_ada"][l].rearrange("(m p) -> m p", p=P)).then_inc(bg_full, 16)
                sp.dma_start(BGR[72:120, :], t["norm_g"][l].rearrange("n (k p) -> (n k) p", p=P)).then_inc(bg_full, 16)
                sp.dma_start(BF[:, :], t["b_forget"][bass.ds(l, 1), :].to_broadcast([P, NH])).then_inc(bf_full, 16)
                w = t["w_ada"][l].rearrange("(k p) n -> p k n", p=P)
                sp.wait_ge(y_free, l * 24 + 2)
                for i in range(2):
                    load(i, by_k(i, w, i * 512, 512))
                for i in range(2, N_ADA0):
                    sp.wait_ge(acc_ready, l * N_ADA + (i - 1))
                    load(i, by_k(i, w, i * 512, 512))

                def ada(a):
                    sp.wait_ge(acc_ready, l * N_ADA + a + N_ADA0)
                    for k in range(0, KD, 4):
                        sp.dma_start(ADA[:, k:k + 4, :], w_ada[:, k:k + 4, bass.ds(a * 512 + N_ADA0 * 512, 512)]).then_inc(ada_full, 16)
                w_ada = w
                swiglu_weights(l, 0, [lambda: sp.wait_ge(acc_ready, l * N_ADA + 5),
                                      lambda: sp.wait_ge(acc_ready, l * N_ADA + 6)], ada)
                w = t["w_in"][l].rearrange("(k p) n -> p k n", p=P)
                for i in range(N_PROJ):
                    u = U_PROJ + i
                    if i == 0:
                        sp.wait_ge(half_used, l * 8 + 4)
                    elif i == 1:
                        sp.wait_ge(y_ready, l * 24 + 8)
                    else:
                        sp.wait_ge(p_ready, l * 30 + 3 * (i - 1))
                    if i < 9:
                        load(u, by_k(u, w, COL_QKV[i // 3] + (i % 3) * MIX, MIX))
                    else:
                        d = ring(u % 2, KD, NIDX + NH)
                        load(u, [(d[:, :, 0:NIDX], w[:, :, COL_IDX:COL_IDX + NIDX]),
                                 (d[:, :, NIDX:NIDX + NH], w[:, :, COL_F:COL_F + NH])])
                for c in range(PC):
                    sp.dma_start(LFC[:, c * 48:c * 48 + 48].rearrange("p (b h) -> p b h", b=NB),
                                 t["cache_fox_logf"][l][:, c * P:c * P + P, :].rearrange("b p h -> p b h")).then_inc(gc_full, 16)
                for c in range(PC):
                    sp.dma_start(KIC[:, c, :].rearrange("p (b d) -> p b d", b=NB),
                                 t["cache_dsa_kidx"][l][:, c * P:c * P + P, :].rearrange("b p d -> p b d")).then_inc(ki_full, 16)
                for g in range(2):
                    sp.wait_ge(p_ready, l * 30 + 27 + 3 * g)
                    load(U_GATE + g, by_k(U_GATE + g, w, COL_GATE + g * MIX, MIX))
                sp.wait_ge(nf_stored, l * 16 + 16)
                for b in range(NB):
                    sp.dma_start(GS[b * NH:(b + 1) * NH, PAST:KEYS],
                                 t["o_fox_logf_s"][l, b].rearrange("t h -> h t"),
                                 allow_slow_non_contiguous=True).then_inc(gn_full, 16)
                sp.wait_ge(g_ready, l * 2 + 1)
                sp.dma_start(g_s, GX[0:48, :]).then_inc(g_stored, 16)
                sp.wait_ge(g_ready, l * 2 + 2)
                sp.dma_start(g_p, RSTD[0:NH, 0:NPROMPT]).then_inc(g_stored, 16)
                def gates(g):
                    u = U_GATE + g
                    sp.wait_ge(gate_ready, l * 24 + 3 * (g - 1))
                    load(u, by_k(u, w, COL_GATE + g * MIX, MIX))

                for g in range(2, 7):
                    gates(g)
                sp.wait_ge(g_stored, l * 32 + 32)
                sp.wait_ge(is_done, l + 1)
                sp.dma_start(GB, g_p.rearrange("(o h) k -> o h k", o=1).to_broadcast([P, NH, NPROMPT])).then_inc(gb_full, 16)
                sp.wait_ge(msk_ready, l * 3 + 3)
                sp.dma_start(m_s, WK).then_inc(msk_stored, 16)
                gates(7)
                sp.wait_ge(stored, l * 208 + 208)
                settle(sp)
                sp.wait_ge(po_copied, l * 6 + 6)
                sp.wait_ge(msk_stored, l * 16 + 16)
                settle(sp)
                def load_keys(b0, j):
                    b, r = b0 + j // 3, j % 3
                    st = l * NSTEP + b0 * 3 + j
                    ck = t[("cache_sb_k", "cache_fox_k", "cache_dsa_k")[r]]
                    nk = t[("o_sb_k_s", "o_fox_k_s", "o_dsa_k_s")[r]]
                    sp.wait_ge(k_used, st + 1)
                    settle(sp)
                    sp.dma_start(KC[:, j % 2, 0:PC, :],
                                 ck[l, b].rearrange("(c p) h d -> p c (h d)", p=P)).then_inc(k_full[j % 2], 16)
                    sp.dma_start(KC[0:NT, j % 2, PC, :], nk[l, b].rearrange("t h d -> t (h d)")).then_inc(k_full[j % 2], 16)
                    if r != SB:
                        sp.wait_ge(zs_ready, st)
                        settle(sp)
                    for h in range(NH):
                        if r == FOX:
                            sp.dma_start(BFX[h * NT:(h + 1) * NT, :],
                                         g_s[bass.ds(b * NH + h, 1), :].to_broadcast([NT, KEYS])).then_inc(bfx_full, 16)
                        if r == DSA:
                            sp.dma_start(BDX[h * NT:(h + 1) * NT, :],
                                         m_s[bass.ds(b * NT, NT), :]).then_inc(bdx_full, 16)

                def load_step(b0, j):
                    b, r = b0 + j // 3, j % 3
                    if has(b0, j + 1):
                        load_keys(b0, j + 1)
                    cv = t[("cache_sb_v", "cache_fox_v", "cache_dsa_v")[r]]
                    nv = t[("o_sb_v_s", "o_fox_v_s", "o_dsa_v_s")[r]]
                    sp.wait_ge(pv_ready, l * NSTEP + b0 * 3 + (j + 1))
                    settle(sp)
                    sp.dma_start(VC[:, j % 2, 0:PC, :],
                                 cv[l, b].rearrange("(c p) h d -> p c (h d)", p=P)).then_inc(v_full[j % 2], 16)
                    sp.dma_start(VC[0:NT, j % 2, PC, :], nv[l, b].rearrange("t h d -> t (h d)")).then_inc(v_full[j % 2], 16)

                load_keys(0, 0)
                sweep(sp, load_step)
                w = t["w_branch"][l].rearrange("n (k p) d -> p (n k) d", p=P)
                for i in range(N_BRANCH):
                    u = U_BRANCH + i
                    if i < 2:
                        sp.wait_ge(gate_ready, l * 24 + 21 + 3 * i)
                    else:
                        sp.wait_ge(br_ready, l * 24 + 6 * (i - 1))
                    load(u, by_k(u, w, i * 256, 256, k=9))
                w = t["w_out"][l].rearrange("(k p) n -> p k n", p=P)
                for i in range(N_WOUT):
                    u = U_WOUT + i
                    sp.wait_ge(br_ready, l * 24 + 18 + 6 * i)
                    load(u, by_k(u, w, i * 512, 512))
                swiglu_weights(l, 1, [lambda: sp.wait_ge(y_ready, l * 24 + Y_BASE[2] + 4),
                                      lambda: sp.wait_ge(y_ready, l * 24 + Y_BASE[2] + 8)])

        @block.tensor
        def _(pe):
            def full(l, u0, more=0):
                pe.wait_ge(slot_full[u0 % 2], l * (16 * UNITS) + more * 32 + 32 * (u0 // 2 + 1))

            pe.wait_ge(in_x, 32)
            pe.wait_ge(in_k, 80)
            for g in range(6):
                pe.wait_ge(xt_free, g + 1)
                for j in range(4):
                    k, tt = 4 * (g % 2) + j, g // 2
                    mm = pe.transpose(PS[:, g % 2, j * P:(j + 1) * P],
                                      qr(tt * 1024 + k * P, P), IDENT[:, :])
                mm.then_inc(xt_ready, 1)
            pe.wait_ge(c_ready, 1)
            for k in range(KD):
                mm = pe.transpose(PS[:, 2, k * NC:(k + 1) * NC], BIG[0:NC, 3 * D + k * P:3 * D + (k + 1) * P], IDENT[0:NC, 0:NC])
            mm.then_inc(ct_ready, 1)
            pe.wait_ge(x_turned, 1)
            pe.wait_ge(c_silu, 1)

            def mean_square(l, n):
                for k in range(KD):
                    j = k % 4
                    pe.wait_ge(sq_ready, l * 48 + (8 * n + k + 1))
                    mm = pe.matmul(PS[32 * j:32 * j + 32, 6, 0:T], ONES[:, :], SQ[:, k, :], start=(k < 4), stop=(k >= 4))
                mm.then_inc(sums_ready, 1)
                pe.wait_ge(sums_copied, l * 6 + (n + 1))
                pe.matmul(PS[:, 6, 0:T], MEAN[:, :], VAR[:, :], start=True, stop=True).then_inc(ms_ready, 1)

            def h_is_ready(l, i, k):
                pe.wait_ge(h_ready, l * 24 + (8 * i + k + 1))

            def ada_unit(l, a, w):
                for k in range(KD):
                    for j in range(4):
                        mm = pe.matmul(PS[32 * j:32 * j + 32, 4, 0:P], CT[:, k, :], w[:, k, j * P:(j + 1) * P],
                                       start=(k == 0), stop=(k == KD - 1))
                mm.then_inc(acc_ready, 1)

            def ada_turned(l, a):
                pe.wait_ge(ar_ready, l * N_ADA + a + 1)
                pe.wait_ge(mod_free, l * N_ADA + a + 1)
                pe.transpose(PS[:, 5, 0:P], AR[:, :], IDENT[:, :]).then_inc(mod_ready, 1)

            def swiglu_in(l, f):
                u = U_IN[f]

                def unit(j, i, first=False):
                    full(l, u + j, i)
                    w = ring((u + j) % 2, KD, 512)
                    for jj in range(2):
                        pe.wait_ge(gu_free, l * 44 + i * 4 + (22 * f + 2 * j + jj + 1))
                        for part in range(2):
                            for k in range(KD):
                                if first and jj == 0 and part == 0:
                                    h_is_ready(l, 2 * f, k)
                                mm = pe.matmul(PS[:, 2 * jj + part, 0:T],
                                               w[:, k, part * 256 + jj * P:part * 256 + (jj + 1) * P], H[:, k, :],
                                               start=(k == 0), stop=(k == KD - 1))
                        mm.then_inc(gu_ready, 1)
                        if f == 0 and jj == 0:
                            pe.wait_ge(ada_full, l * 384 + i * 64 + (32 * j + 32))
                            ada_unit(l, i * 2 + (N_ADA0 + j), ADA)
                    if f == 0:
                        ada_turned(l, i * 2 + (N_ADA0 + j))
                unit(0, 0, first=True)
                unit(1, 0)
                with loop(pe, 1, 5) as i:
                    unit(0, i)
                    unit(1, i)
                full(l, u + 10)
                w = ring((u + 10) % 2, KD, 512)
                for jj in range(2):
                    pe.wait_ge(gu_free, l * 44 + (22 * f + 20 + jj + 1))
                    for part in range(2):
                        for k in range(KD):
                            mm = pe.matmul(PS[:, 2 * jj + part, 0:T],
                                           w[:, k, part * 256 + jj * P:part * 256 + (jj + 1) * P], H[:, k, :],
                                           start=(k == 0), stop=(k == KD - 1))
                    mm.then_inc(gu_ready, 1)
                    if f == 0 and jj == 0:
                        pe.wait_ge(ada_full, l * 384 + 352)
                        ada_unit(l, N_ADA0 + 10, ADA)
                if f == 0:
                    ada_turned(l, N_ADA0 + 10)

            def swiglu_out(l, f):
                u = U_OUT[f]
                pe.wait_ge(gu_free, l * 44 + (22 * f + 24))
                with loop(pe, 0, 4) as mp:
                    for half in range(2):
                        full(l, u + half, mp)
                        w = ring((u + half) % 2, NFF // 2, 256)
                        for m in range(2):
                            if half == 0:
                                pe.wait_ge(y_free, l * 24 + mp * 2 + (Y_BASE[f] + m + 1))
                            for k in range(NFF // 2):
                                mm = pe.matmul(PS[:, m, 0:T], w[:, k, m * P:(m + 1) * P],
                                               HID[:, half * (NFF // 2) + k, :],
                                               start=(half == 0 and k == 0), stop=(half == 1 and k == NFF // 2 - 1))
                            if half == 1:
                                mm.then_inc(y_ready, 1)
                        if half == 0:
                            mm.then_inc(half_used, 1)

            with pe.Fori(0, DEPTH) as l:
                mean_square(l, 0)
                pe.wait_ge(bg_full, l * 32 + 32)
                pe.transpose(PS[:, 7, 0:120], BGR[0:120, :], IDENT[0:120, 0:120]).then_inc(bg_ready, 1)
                for a in range(N_ADA0):
                    full(l, a)
                    ada_unit(l, a, ring(a % 2, KD, 512))
                    ada_turned(l, a)
                swiglu_in(l, 0)
                swiglu_out(l, 0)
                pe.wait_ge(ada_full, l * 384 + 384)
                ada_unit(l, N_ADA - 1, ADA)
                mean_square(l, 1)
                ada_turned(l, N_ADA - 1)
                mean_square(l, 2)
                for i in range(N_PROJ):
                    full(l, U_PROJ + i)
                    width = MIX if i < 9 else NIDX + NH
                    w = ring((U_PROJ + i) % 2, KD, width)
                    for tt in range(TT):
                        pe.wait_ge(p_free, l * 30 + (3 * i + tt + 1))
                        for k in range(KD):
                            if i == 0 and tt == 0:
                                h_is_ready(l, 1, k)
                            mm = pe.matmul(PS[:, tt, 0:width], H[:, k, tt * P:(tt + 1) * P], w[:, k, :],
                                           start=(k == 0), stop=(k == KD - 1))
                        mm.then_inc(p_ready, 1)
                pe.wait_ge(p_free, l * 30 + 30 + 3)
                pe.wait_ge(gc_full, l * 64 + 64)
                pe.wait_ge(logf_ready, l + 1)
                settle(pe)
                for c in range(PC):
                    pe.transpose(PS[0:48, 5, c * P:(c + 1) * P], LFC[:, c * 48:c * 48 + 48], IDENT[:, :])
                for tt in range(2):
                    mm = pe.transpose(PS[0:NH, 6, tt * P:(tt + 1) * P], LF[:, 0, tt, :], IDENT[:, :])
                mm.then_inc(gt_ready, 1)
                def gate_tile(n, bank):
                    u = U_GATE + n // 3
                    if n % 3 == 0:
                        full(l, u)
                    if n >= 2 and bank < 4:
                        pe.wait_ge(gate_taken, l * 24 + n - 1)
                    w = ring(u % 2, KD, MIX)
                    for k in range(KD):
                        mm = pe.matmul(PS[:, bank, 0:T], w[:, k, (n % 3) * P:(n % 3 + 1) * P], H[:, k, :],
                                       start=(k == 0), stop=(k == KD - 1))
                    mm.then_inc(gate_ready, 1)

                for n in range(GATES[0]):
                    gate_tile(n, n % 2)
                pe.wait_ge(rope_done, l + 1)
                n = 0
                for r in range(NBR):
                    for tt in range(TT):
                        for i in range(2 if tt < 2 else 1):
                            pe.wait_ge(qk_free, l * 15 + (n + 1))
                            for a in range(NPAIR):
                                mm = pe.transpose(PS[:, 3 + n % 2, a * P:(a + 1) * P],
                                                  QK[:, r, tt, i * MIX + a * P:i * MIX + (a + 1) * P], IDENT[:, :])
                            mm.then_inc(qk_ready, 1)
                            n += 1
                pe.wait_ge(dup_ready, l + 1)
                pe.wait_ge(gt_copied, l + 1)
                for tt in range(2):
                    pe.wait_ge(it_free, l * 8 + (tt + 1))
                    for a in range(2):
                        pe.transpose(PS[:, 5 + tt, a * P:(a + 1) * P], IDX[:, tt, a * P:(a + 1) * P], IDENT[:, :])
                    pe.transpose(PS[:, 5 + tt, 2 * P:3 * P], KI2[:, tt, :], IDENT[:, :]).then_inc(it_ready, 1)
                pe.wait_ge(it_free, l * 8 + 3)
                for h in range(IH):
                    mm = pe.transpose(PS[:, 5, h * P:(h + 1) * P], QI2[:, h, :], IDENT[:, :])
                mm.then_inc(it_ready, 1)
                pe.wait_ge(it_free, l * 8 + 4)
                pe.transpose(PS[:, 6, 0:P], KI2[:, 2, :], IDENT[:, :]).then_inc(it_ready, 1)
                pe.wait_ge(ki_full, l * 64 + 64)
                for bp in range(4):
                    pe.wait_ge(it_free, l * 8 + (5 + bp))
                    for c in range(PC):
                        mm = pe.transpose(PS[:, 5 + bp % 2, c * P:(c + 1) * P], KIC[:, c, bp * P:(bp + 1) * P], IDENT[:, :])
                    mm.then_inc(it_ready, 1)
                pe.wait_ge(qk_free, l * 15 + 17)
                pe.wait_ge(gate_taken, l * 24 + GATES[0])
                pe.wait_ge(it_free, l * 8 + 4)
                for qt in range(2):
                    for h in range(IH):
                        s = slice(64 * (h % 2), 64 * (h % 2) + 64)
                        mm = pe.matmul(PS[:, 2 * qt + h % 2, (h // 2) * 256:(h // 2) * 256 + 256],
                                       QIT[s, h // 2, qt * P:(qt + 1) * P], KITP[s, :], start=True, stop=True)
                    mm.then_inc(is_ready, 1)
                pe.wait_ge(it_free, l * 8 + 10)
                for h in range(IH):
                    if h >= 2:
                        pe.wait_ge(relu_ready, l * 6 + (h + 1))
                    for half in range(2):
                        for bp in range(4):
                            mm = pe.matmul(PS[:, 4 + 2 * (h % 2) + half, 0:264], QIP[:, h, bp * P:(bp + 1) * P],
                                           KIT[:, bp, half * 264:(half + 1) * 264], start=(bp == 0), stop=(bp == 3))
                    mm.then_inc(is_ready, 1)
                    if h in (1, 2):
                        pe.wait_ge(relu_ready, l * 6 + 1)
                        for n in range(GATES[h - 1], GATES[h]):
                            gate_tile(n, n % 2)
                pe.wait_ge(relu_ready, l * 6 + 6)
                for n in range(GATES[2], GATES[3]):
                    gate_tile(n, n % 2)
                pe.wait_ge(gate_taken, l * 24 + GATES[3])
                def prompt_scores(it):
                    r, qt = it // 2, it % 2
                    if it:
                        pe.wait_ge(z_ready, l * 6 + it)
                    for h in range(NH):
                        s = slice(64 * (h % 2), 64 * (h % 2) + 64)
                        mm = pe.matmul(PS[:, 2 * (h % 2) + h // 4, (h // 2 % 2) * 256:(h // 2 % 2) * 256 + 256],
                                       QKT[s, r, 0, h // 2, qt * P:(qt + 1) * P], QKT[s, r, 1, h // 2, :],
                                       start=True, stop=True)
                    mm.then_inc(s_ready, 1)

                prompt_scores(0)
                for it in range(6):
                    r, qt = it // 2, it % 2
                    if it < 5:
                        prompt_scores(it + 1)
                    for n in range(GATE_AT[it], GATE_AT[it + 1]):
                        gate_tile(n, 4 + n - GATE_AT[it])
                    pe.wait_ge(gate_taken, l * 24 + GATE_AT[it + 1])
                    pe.wait_ge(p_done, l * 6 + (it + 1))
                    for g in range(3):
                        n = 3 * it + g
                        if n >= 2:
                            pe.wait_ge(pt_copied, l * 18 + (n - 1))
                        for j in range(4):
                            mm = pe.transpose(PS[:, 5 + n % 2, j * P:(j + 1) * P],
                                              EP[:, 2 * g + j // 2, (j % 2) * P:(j % 2 + 1) * P], IDENT[:, :])
                        mm.then_inc(pt_ready, 1)
                    if it:
                        pe.wait_ge(po_copied, l * 6 + it)
                    pe.wait_ge(pt_copied, l * 18 + (3 * it + 3))
                    for h in range(NH):
                        for kt in range(2):
                            mm = pe.matmul(PS[64 * (h % 2):64 * (h % 2) + 64, 7, (h // 2) * P:(h // 2 + 1) * P],
                                           VT[:, r, kt, h * HD:(h + 1) * HD],
                                           PTP[:, (h % 2) * NPAIR + h // 2, kt, :],
                                           start=(kt == 0), stop=(kt == 1))
                    mm.then_inc(po_ready, 1)
                pe.wait_ge(po_copied, l * 6 + 6)

                def turn(b0, j):
                    s = j % 2
                    pe.wait_ge(k_full[s], l * (NSTEP * 16) + b0 * 48 + 32 * (j // 2 + 1))
                    pe.wait_ge(kt_free, l * NSTEP + b0 * 3 + (j + 1))
                    for a in range(NPAIR):
                        for c in range(PC):
                            pe.transpose(PS[:, a, c * P:(c + 1) * P], KC[:, s, c, a * P:(a + 1) * P], IDENT[:, :])
                    for a in range(NPAIR):
                        mm = pe.transpose(PS[:, 3, a * NT:(a + 1) * NT], KC[0:NT, s, PC, a * P:(a + 1) * P], IDENT[0:NT, 0:NT])
                    mm.then_inc(kt_ready, 1)

                def output(b0, j):
                    pe.wait_ge(ou_ready, l * NSTEP + b0 * 3 + (j + 2))
                    settle(pe)
                    pe.transpose(PS[:, 7, P:P + 96], OU[0:96, :], IDENT[0:96, 0:96]).then_inc(o_ready, 1)

                def probs_and_values(b0, j):
                    st = l * NSTEP + b0 * 3 + j
                    pe.wait_ge(ps_ready, st + 1)
                    for c in range(PC):
                        pe.transpose(PS[:, 6, c * 96:(c + 1) * 96], ES[j % 2][0:96, c * P:(c + 1) * P], IDENT[0:96, 0:96])
                    pe.transpose(PS[0:NT, 6, 384:480], ES[j % 2][0:96, PAST:KEYS], IDENT[0:96, 0:96]).then_inc(st_ready, 1)
                    pe.wait_ge(v_full[j % 2], l * (NSTEP * 16) + b0 * 48 + 32 * (j // 2 + 1))
                    pe.wait_ge(ou_ready, st + 1)
                    pe.wait_ge(o_free, st + 1)
                    pe.wait_ge(st_copied, st + 1)
                    for c in range(PC + 1):
                        n = P if c < PC else NT
                        for a in range(NPAIR):
                            mm = pe.matmul(PS[32 * a:32 * a + 32, 7, 0:P], PTS[0:n, c, a * 32:(a + 1) * 32],
                                           VC[0:n, j % 2, c, a * P:(a + 1) * P], start=(c == 0), stop=(c == PC))
                    mm.then_inc(pv_ready, 1)

                def step(b0, j):
                    st = l * NSTEP + b0 * 3 + j
                    pe.wait_ge(kt_free, st + 2)
                    pe.wait_ge(qc_ready, st + 1)
                    pe.wait_ge(zs_ready, st + 2)
                    for half in range(2):
                        for a in range(NPAIR):
                            mm = pe.matmul(PS[32 * a:32 * a + 32, 4 + half, 0:264], QC[:, j % 2, a * 32:(a + 1) * 32],
                                           KT[:, a, half * 264:(half + 1) * 264], start=True, stop=True)
                    mm.then_inc(ss_ready, 1)
                    if has(b0, j + 1):
                        turn(b0, j + 1)
                    if has(b0, j - 2):
                        output(b0, j - 2)
                    if has(b0, j - 1):
                        probs_and_values(b0, j - 1)

                turn(0, 0)
                sweep(pe, step)
                output(NB - 2, 4)
                probs_and_values(NB - 2, 5)
                output(NB - 2, 5)
                pe.wait_ge(o_free, l * 24 + 24 + 1)
                for i in range(N_BRANCH):
                    full(l, U_BRANCH + i)
                    w = ring((U_BRANCH + i) % 2, 9, 256)
                    for m in range(2):
                        for n in range(NBR):
                            pe.wait_ge(br_free, l * 24 + (6 * i + 3 * m + n + 1))
                            for k in range(NPAIR):
                                mm = pe.matmul(PS[:, n, 0:T], w[:, 3 * n + k, m * P:(m + 1) * P], OT[:, 3 * n + k, :],
                                               start=(k == 0), stop=(k == NPAIR - 1))
                            mm.then_inc(br_ready, 1)
                pe.wait_ge(mg_ready, l * 8 + 8)
                for i in range(N_WOUT):
                    full(l, U_WOUT + i)
                    w = ring((U_WOUT + i) % 2, KD, 512)
                    for m in range(4):
                        pe.wait_ge(y_free, l * 24 + (Y_BASE[2] + 4 * i + m + 1))
                        for k in range(KD):
                            mm = pe.matmul(PS[:, m % 2, 0:T], w[:, k, m * P:(m + 1) * P], MG[:, k, :],
                                           start=(k == 0), stop=(k == KD - 1))
                        mm.then_inc(y_ready, 1)
                mean_square(l, 3)
                mean_square(l, 4)
                swiglu_in(l, 1)
                swiglu_out(l, 1)
                mean_square(l, 5)
            pe.wait_ge(x_ready, 8 + 48)
            for g in range(6):
                pe.wait_ge(xt_free, 6 + g + 1)
                for j in range(4):
                    k, tt = 4 * (g % 2) + j, g // 2
                    mm = pe.transpose(PS[:, g % 2, j * P:(j + 1) * P], X[:, k, tt * P:(tt + 1) * P], IDENT[:, :])
                mm.then_inc(xt_ready, 1)

        @block.scalar
        def _(act):
            begin, link = chained(act, ach)
            A = nc.scalar.activation
            act.wait_ge(in_c, 32)
            A(BIG[0:NC, D:2 * D], BIG[0:NC, 0:D], ACT.Sigmoid).then_inc(c_act, 1)
            for g in range(6):
                act.wait_ge(xt_ready, g + 1)
                ins = A(X[:, 4 * (g % 2):4 * (g % 2) + 4, (g // 2) * P:(g // 2 + 1) * P],
                        PS[:, g % 2, :].rearrange("p (k t) -> p k t", k=4), ACT.Copy)
                ins.then_inc(xt_free, 1)
            act.wait_ge(xt_free, 2 + 6)
            act.sem_inc(x_turned, 1)

            def prompt_coefficient(l, i, k):
                A(H[:, k, 0:NPROMPT], X[:, k, 0:NPROMPT], ACT.Identity, scale=MOD[:, (3 * i + 1) * KD + k, 0:1]).then_inc(xc_ready, 1)

            def squares_of_x(l, i):
                if i:
                    act.wait_ge(coef_ready, l * 2 + 2)
                for k in range(KD):
                    act.wait_ge(x_ready, l * 24 + (8 * i + k + 1))
                    A(SQ[:, k, :], X[:, k, :], ACT.Square).then_inc(sq_ready, 1)
                    if i:
                        prompt_coefficient(l, i, k)

            def rstd(l, n):
                begin()
                act.wait_ge(ms_ready, l * 6 + (n + 1))
                link(A(VAR[:, :], PS[:, 6, 0:T], ACT.Ln, scale=1.0 / D, bias=EPSC[:, :]))
                A(RSTD[:, :], VAR[:, :], ACT.Exp, scale=-0.5).then_inc(rstd_ready, 1)

            def shift_prompt(l, i):
                for k in range(KD):
                    act.wait_ge(hs_ready, l * 24 + (8 * i + k + 1))
                    A(H[:, k, 0:NPROMPT], H[:, k, 0:NPROMPT], ACT.Identity, bias=MOD[:, 3 * i * KD + k, 0:1]).then_inc(h_ready, 1)

            def swiglu_in(l, f):
                with by_two(act, 0, 22) as j:
                    for jj in range(2):
                        act.wait_ge(gu_free, l * 44 + j + (22 * f + jj + 1))
                        act.wait_ge(gu_ready, l * 44 + j + (22 * f + jj + 1))
                        A(FE[:, jj, :], PS[:, 2 * jj, 0:T], ACT.Sigmoid).then_inc(sig_ready, 1)

            def take_y(l, i, base):
                for m in range(KD):
                    act.wait_ge(y_ready, l * 24 + (base + m + 1))
                    A(SQ[:, m, :], PS[:, m % 2, 0:T], ACT.Square).then_inc(sq_ready, 1)
                    A(Y[:, m, 0:NPROMPT], PS[:, m % 2, 0:NPROMPT], ACT.Identity, scale=MOD[:, (3 * i + 2) * KD + m, 0:1])
                    A(Y[:, m, NPROMPT:T], PS[:, m % 2, NPROMPT:T], ACT.Copy).then_inc(y_free, 1)

            with act.Fori(0, DEPTH) as l:
                squares_of_x(l, 0)
                rstd(l, 0)
                act.wait_ge(coef_ready, l * 2 + 1)
                for k in range(KD):
                    prompt_coefficient(l, 0, k)
                shift_prompt(l, 0)
                swiglu_in(l, 0)
                take_y(l, 0, Y_BASE[0])
                rstd(l, 1)
                squares_of_x(l, 1)
                rstd(l, 2)
                shift_prompt(l, 1)
                for i in range(N_PROJ):
                    for tt in range(TT):
                        act.wait_ge(p_ready, l * 30 + (3 * i + tt + 1))
                        if i < 9:
                            dst = VT[:, i // 3, tt, :] if i % 3 == 2 else QK[:, i // 3, tt, (i % 3) * MIX:(i % 3 + 1) * MIX]
                            A(dst, PS[:, tt, 0:MIX], ACT.Copy).then_inc(p_free, 1)
                        else:
                            begin()
                            link(A(IDX[:, tt, :], PS[:, tt, 0:NIDX], ACT.Copy))
                            A(FREG[:, tt, 0:NH], PS[:, tt, NIDX:NIDX + NH], ACT.Copy).then_inc(p_free, 1)
                act.wait_ge(logf_arg, l + 1)
                begin()
                link(A(LF[:, 1, :, :], LF[:, 0, :, :], ACT.Abs))
                link(A(LF[:, 1, :, :], LF[:, 1, :, :], ACT.Exp, scale=-1.0))
                A(LF[:, 2, :, :], LF[:, 1, :, :], ACT.Ln, bias=1.0).then_inc(logf_exp, 1)
                act.wait_ge(logf_ready, l + 1)
                act.dma_start(t["o_fox_logf_s"][l].rearrange("b t h -> (b t) h"), LF[:, 0, 2, :]).then_inc(nf_stored, 16)
                act.dma_start(t["o_fox_logf_p"][l].rearrange("o (t p) h -> p (o t) h", p=P), LF[:, 0, 0:2, :]).then_inc(stored, 16)
                act.wait_ge(gt_ready, l + 1)
                begin()
                link(A(GS[0:48, 0:PAST], PS[0:48, 5, :], ACT.Copy))
                A(VAR[0:NH, 0:NPROMPT], PS[0:NH, 6, 0:NPROMPT], ACT.Copy).then_inc(gt_copied, 1)
                def take_gate(n, bank):
                    act.wait_ge(gate_ready, l * 24 + (n + 1))
                    A(G[:, n, :], PS[:, bank, 0:T], ACT.Sigmoid).then_inc(gate_taken, 1)

                act.wait_ge(p_free, l * 30 + 33)
                for name, r, src in (("sb_k", SB, QK), ("sb_v", SB, VT), ("fox_k", FOX, QK), ("fox_v", FOX, VT),
                                     ("dsa_v", DSA, VT), ("dsa_k", DSA, QK)):
                    if name == "dsa_k":
                        for n in range(GATES[0]):
                            take_gate(n, n % 2)
                        act.wait_ge(rope_done, l + 1)
                    cols = slice(0, MIX) if src is VT else slice(MIX, 2 * MIX)
                    act.dma_start(t[f"o_{name}_p"][l].rearrange("o (t p) h d -> p (o t) (h d)", p=P),
                                  src[:, r, 0:2, cols]).then_inc(stored, 16)
                    act.dma_start(t[f"o_{name}_s"][l].rearrange("b t h d -> (b t) (h d)"), src[:, r, 2, cols]).then_inc(stored, 16)
                act.dma_start(t["o_dsa_kidx_p"][l].rearrange("o (t p) d -> p (o t) d", p=P), IDX[:, 0:2, IH * HD:IH * HD + HD]).then_inc(kidx_stored, 16)
                act.dma_start(t["o_dsa_kidx_s"][l].rearrange("b t d -> (b t) d"), IDX[:, 2, IH * HD:IH * HD + HD]).then_inc(kidx_stored, 16)
                n = 0
                for r in range(NBR):
                    for tt in range(TT):
                        for i in range(2 if tt < 2 else 1):
                            act.wait_ge(qk_ready, l * 15 + (n + 1))
                            src = PS[:, 3 + n % 2, 0:MIX].rearrange("p (a t) -> p a t", a=NPAIR)
                            if tt < 2:
                                A(QKT[:, r, i, :, tt * P:(tt + 1) * P], src, ACT.Copy).then_inc(qk_free, 1)
                            else:
                                src = src.rearrange("p a (b t) -> p a b t", b=NB)
                                begin()
                                link(A(QBLK[0:64, r, :, :, 0:NT], src[0:64], ACT.Copy))
                                A(QBLK[64:128, r, :, :, NT:2 * NT], src[64:128], ACT.Copy).then_inc(qk_free, 1)
                            n += 1
                act.wait_ge(qip_zero, l + 1)
                for tt in range(2):
                    act.wait_ge(it_ready, l * 8 + (tt + 1))
                    begin()
                    link(A(QIT[:, :, tt * P:(tt + 1) * P], PS[:, 5 + tt, 0:2 * P].rearrange("p (a t) -> p a t", a=2), ACT.Copy))
                    A(KITP[:, tt * P:(tt + 1) * P], PS[:, 5 + tt, 2 * P:3 * P], ACT.Copy).then_inc(it_free, 1)
                act.wait_ge(it_ready, l * 8 + 3)
                begin()
                for par in range(2):
                    s = slice(64 * par, 64 * par + 64)
                    for h in range(IH):
                        dst = QIP[s, h, :].rearrange("p (i c) -> p i c", c=160)[:, :, NT * par:NT * par + NT]
                        src = PS[s, 5, h * P:(h + 1) * P].rearrange("p (i z t) -> p i z t", z=2, t=NT)[:, :, par, :]
                        ins = A(dst, src, ACT.Copy)
                        if par == 0 or h < IH - 1:
                            link(ins)
                ins.then_inc(it_free, 1)
                act.wait_ge(it_ready, l * 8 + 4)
                begin()
                src = PS[:, 6, 0:P].rearrange("p (i z t) -> p i z t", z=2, t=NT)
                link(A(KIT[0:64, :, PAST:KEYS], src[0:64, :, 0, :], ACT.Copy))
                A(KIT[64:128, :, PAST:KEYS], src[64:128, :, 1, :], ACT.Copy).then_inc(it_free, 1)
                for bp in range(4):
                    act.wait_ge(it_ready, l * 8 + (5 + bp))
                    A(KIT[:, bp, 0:PAST], PS[:, 5 + bp % 2, :], ACT.Copy).then_inc(it_free, 1)
                for n in range(6):
                    act.wait_ge(is_ready, l * 6 + (n + 1))
                    act.wait_ge(relu_free, l * 6 + (n + 1))
                    if n < 2:
                        A(RL.rearrange("p (h k) -> p h k", h=IH), PS[:, 2 * n:2 * n + 2, :].rearrange("p b (h k) -> p (b h) k", h=2),
                          ACT.Relu, scale=1 / 16).then_inc(relu_ready, 1)
                    else:
                        A(RL[:, 0:KEYS].rearrange("p (s k) -> p s k", s=2), PS[:, 4 + 2 * (n % 2):6 + 2 * (n % 2), 0:264],
                          ACT.Relu, scale=1 / 16).then_inc(relu_ready, 1)
                    if n in (1, 2):
                        for g in range(GATES[n - 1], GATES[n]):
                            take_gate(g, g % 2)
                for n in range(GATES[2], GATES[3]):
                    take_gate(n, n % 2)
                for it in range(6):
                    r = it // 2
                    begin()
                    act.wait_ge(z_ready, l * 6 + (it + 1))
                    if r == SB:
                        link(A(LP, ZP, ACT.Sigmoid, scale=-1.0))
                        A(EP, ZP, ACT.Sigmoid).then_inc(e_ready, 1)
                    else:
                        for h in range(NH):
                            ins = A(EP[:, h, :], ZP[:, h, :], ACT.Exp, bias=ST[:, h:h + 1], accum_out=ST[:, 8 + h:9 + h])
                            if h < NH - 1:
                                link(ins)
                        ins.then_inc(e_ready, 1)
                    for n in range(GATE_AT[it], GATE_AT[it + 1]):
                        take_gate(n, 4 + n - GATE_AT[it])
                    for g in range(3):
                        act.wait_ge(pt_ready, l * 18 + (3 * it + g + 1))
                        A(PTP[:, 2 * g:2 * g + 2, :, :], PS[:, 5 + (3 * it + g) % 2, :].rearrange("p (h k q) -> p h k q", h=2, k=2),
                          ACT.Copy).then_inc(pt_copied, 1)
                    act.wait_ge(po_ready, l * 6 + (it + 1))
                    A(OT[:, 3 * r:3 * r + 3, (it % 2) * P:(it % 2 + 1) * P],
                      PS[:, 7, 0:MIX].rearrange("p (a q) -> p a q", a=NPAIR), ACT.Copy).then_inc(po_copied, 1)
                def turned_keys(b0, j):
                    act.wait_ge(kt_ready, l * NSTEP + b0 * 3 + (j + 1))
                    act.sem_inc(k_used, 1)
                    link(A(KT[:, :, 0:PAST], PS[:, 0:NPAIR, :], ACT.Copy))
                    A(KT[:, :, PAST:KEYS], PS[:, 3, 0:NPAIR * NT].rearrange("p (a t) -> p a t", a=NPAIR), ACT.Copy).then_inc(kt_free, 1)

                def step(b0, j):
                    st = l * NSTEP + b0 * 3 + j
                    e = ES[j % 2]
                    begin()
                    if has(b0, j + 1):
                        turned_keys(b0, j + 1)
                    act.wait_ge(zs_ready, st + 3)
                    if j % 3 == SB:
                        link(A(LS[0:96, :], ZS[0:96, :], ACT.Sigmoid, scale=-1.0))
                        A(e[0:96, :], ZS[0:96, :], ACT.Sigmoid).then_inc(es_ready, 1)
                    else:
                        A(e[0:96, :], ZS[0:96, :], ACT.Exp, bias=ST[0:96, 0:1], accum_out=ST[0:96, 8:9]).then_inc(es_ready, 1)

                begin()
                turned_keys(0, 0)
                sweep(act, step)
                take_y(l, 1, Y_BASE[2])
                rstd(l, 3)
                squares_of_x(l, 2)
                rstd(l, 4)
                shift_prompt(l, 2)
                swiglu_in(l, 1)
                take_y(l, 2, Y_BASE[1])
                rstd(l, 5)
            for g in range(6):
                act.wait_ge(xt_ready, 6 + g + 1)
                k0, tt = 4 * (g % 2), g // 2
                A(qr(tt * 1024 + k0 * P, 512), PS[:, g % 2, :], ACT.Copy).then_inc(xt_free, 1)
            act.wait_ge(xt_free, 2 + 12)
            act.dma_start(t["o_y_p"].rearrange("o (t p) d -> p (o t) d", p=P), qr(0, 2048).rearrange("p (t d) -> p t d", t=2)).then_inc(out_stored, 16)
            act.dma_start(t["o_y_s"].rearrange("b t d -> (b t) d"), qr(2048, 1024)).then_inc(out_stored, 16)
            act.wait_ge(out_stored, 32)

        @block.vector
        def _(dve):
            begin, link = chained(dve, vch)
            V = nc.vector
            for s, n in ((xt_free, 2), (gu_free, 2), (y_free, 2), (mod_free, 1), (bg_free, 1), (p_free, 3), (qk_free, 2),
                         (it_free, 2), (relu_free, 1), (o_free, 1), (kt_free, 1), (pv_ready, 2), (ou_ready, 1), (br_free, 3),
                         (k_used, 2), (zs_ready, 2)):
                dve.sem_inc(s, n)
            begin()
            link(V.memset(ONES[:, :], 1.0))
            link(V.memset(MEAN[:, :], 1 / 32))
            link(V.memset(EPSC[:, :], EPS))
            link(V.memset(ZERO[:, :], 0.0))
            link(V.memset(QBLK, 0.0))
            link(V.memset(CT, 0.0))
            dve.wait_ge(c_act, 1)
            c, e, g = (BIG[0:NC, i * D:(i + 1) * D] for i in (0, 1, 3))
            V.tensor_tensor(g, c, e, ALU.mult).then_inc(c_ready, 1)
            dve.wait_ge(ct_ready, 1)
            link(V.tensor_copy(CT[:, :, 0:NC], PS[:, 2, 0:KD * NC].rearrange("p (k c) -> p k c", c=NC)))
            dve.wait_ge(x_turned, 1)
            dve.sem_inc(x_ready, KD)
            dve.sem_inc(c_silu, 1)

            def sums(l, n):
                dve.wait_ge(sums_ready, l * 6 + (n + 1))
                V.tensor_copy(VAR[:, :], PS[:, 6, 0:T]).then_inc(sums_copied, 1)

            def per_sample(m):
                return MOD[:, m:m + KD, 1:NC][..., None].to_broadcast([P, KD, NB, NT])

            def pre_norm(l, n, i):
                begin()
                m = 3 * i * KD
                link(V.tensor_tensor(sample_cols(H), sample_cols(X), per_sample(m + KD), ALU.mult))
                if n:
                    sums(l, n)
                dve.wait_ge(xc_ready, l * 24 + (8 * i + 8))
                dve.wait_ge(rstd_ready, l * 6 + (n + 1))
                settle(dve)
                begin()
                for k in range(KD + 1):
                    if k < KD:
                        V.tensor_tensor(H[:, k, :], H[:, k, :], RSTD[:, :], ALU.mult).then_inc(vch, 1)
                    if k:
                        dve.wait_ge(vch, k)
                        hs = H[:, k - 1, NPROMPT:T].rearrange("p (b t) -> p b t", b=NB)
                        V.tensor_tensor(hs, hs, per_sample(m)[:, k - 1], ALU.add).then_inc(hs_ready, 1)

            def scale_y(l, i, base):
                for k in range(KD):
                    dve.wait_ge(y_free, l * 24 + (base + k + 1 + 2))
                    ys = Y[:, k, NPROMPT:T].rearrange("p (b t) -> p b t", b=NB)
                    V.tensor_tensor(ys, ys, per_sample((3 * i + 2) * KD)[:, k], ALU.mult).then_inc(ys_ready, 1)

            def post_norm(l, n, i):
                dve.wait_ge(rstd_ready, l * 6 + (n + 1))
                dve.wait_ge(ys_ready, l * 24 + (8 * i + 8))
                begin()
                for k in range(KD + 1):
                    if k < KD:
                        V.tensor_tensor(Y[:, k, :], Y[:, k, :], RSTD[:, :], ALU.mult).then_inc(vch, 1)
                    if k:
                        dve.wait_ge(vch, k)
                        V.tensor_tensor(X[:, k - 1, :], X[:, k - 1, :], Y[:, k - 1, :], ALU.add).then_inc(x_ready, 1)
                dve.wait_ge(x_ready, l * 24 + (8 * (i + 1) + 8))

            def ada_rows(l, a):
                dve.wait_ge(acc_ready, l * N_ADA + a + 1)
                V.tensor_copy(AR[:, :], PS[:, 4, 0:P]).then_inc(ar_ready, 1)

            def ada_columns(l, a):
                dve.wait_ge(mod_ready, l * N_ADA + a + 1)
                V.tensor_tensor(MOD[:, bass.ds(a * 4, 4), :], PS[:, 5, 0:P].rearrange("p (m c) -> p m c", c=32)[:, :, 0:NC],
                                BG[:, bass.ds(a * 4, 4)][..., None].to_broadcast([P, 4, NC]), ALU.add).then_inc(mod_free, 1)
                dve.wait_ge(mod_free, l * N_ADA + a + 2)

            def coefficients(l, parts):
                begin()
                for i in parts:
                    m = 3 * i * KD
                    gain = [BG[:, 72 + (2 * i + z) * KD:72 + (2 * i + z + 1) * KD][..., None].to_broadcast([P, KD, NC]) for z in range(2)]
                    link(V.scalar_tensor_tensor(out=MOD[:, m + KD:m + 2 * KD, :], in0=MOD[:, m + KD:m + 2 * KD, :], scalar=1.0,
                                                in1=gain[0], op0=ALU.add, op1=ALU.mult))
                    link(V.scalar_tensor_tensor(out=MOD[:, m + 2 * KD:m + 3 * KD, :], in0=MOD[:, m + 2 * KD:m + 3 * KD, :],
                                                scalar=(1.0 if i == 1 else 0.5), in1=gain[1], op0=ALU.mult, op1=ALU.mult))

            def swiglu_in(l, f):
                with loop(dve, 0, NFF // 2) as i:
                    j = i * 2
                    for jj in range(2):
                        begin()
                        dve.wait_ge(sig_ready, l * 44 + j + (22 * f + jj + 1))
                        link(V.tensor_tensor(FT[:, jj, :], PS[:, 2 * jj, 0:T], FE[:, jj, :], ALU.mult))
                        V.tensor_tensor(HID[:, j + jj, :], PS[:, 2 * jj + 1, 0:T], FT[:, jj, :], ALU.mult).then_inc(gu_free, 1)
                        if f == 0 and jj == 0:
                            ada_rows(l, i + N_ADA0)
                    if f == 0:
                        ada_columns(l, i + N_ADA0)
                dve.wait_ge(gu_free, l * 44 + (22 * f + 24))

            def rotate(x, heads, tt):
                n = heads * HD
                x = x.rearrange("p (h s d) -> p h s d", s=2, d=32)
                a = RT[:, 0:n].rearrange("p (h s d) -> p h s d", s=2, d=32)
                b = RT[:, 768:768 + n].rearrange("p (h s d) -> p h s d", s=2, d=32)
                cos = ROPE[:, tt, 0, :][:, None, None, :].to_broadcast([P, heads, 2, 32])
                sin = ROPE[:, tt, 1, :][:, None, :].to_broadcast([P, heads, 32])
                link(V.tensor_tensor(a, x, cos, ALU.mult))
                link(V.tensor_tensor(b[:, :, 0, :], x[:, :, 1, :], sin, ALU.mult))
                link(V.tensor_tensor(b[:, :, 1, :], x[:, :, 0, :], sin, ALU.mult))
                link(V.tensor_tensor(x[:, :, 0, :], a[:, :, 0, :], b[:, :, 0, :], ALU.subtract))
                link(V.tensor_tensor(x[:, :, 1, :], a[:, :, 1, :], b[:, :, 1, :], ALU.add))

            def reverse_product(out, factors, zero):
                return V.tensor_tensor_scan(out[:, ::-1], factors[:, ::-1], zero[:, ::-1], 1.0, ALU.mult, ALU.add)

            def reverse_sum(out, terms, zero):
                return V.tensor_tensor_scan(out[:, ::-1], terms[:, ::-1], zero[:, ::-1], 0.0, ALU.add, ALU.add)

            def choose(keys, rounds, rest):
                w = WK[:, 0:keys]
                with loop(dve, 0, rounds) as _:
                    begin()
                    link(V.max(M8, w))
                    link(V.match_replace(w, M8, w, TAKEN))
                begin()
                if rest:
                    link(V.max(M8, w))
                    link(V.memset(M8[:, rest:8], TAKEN))
                    link(V.match_replace(w, M8, w, TAKEN))

            with dve.Fori(0, DEPTH) as l:
                sums(l, 0)
                begin()
                dve.wait_ge(bg_ready, l + 1)
                V.tensor_copy(BG[:, :], PS[:, 7, 0:120]).then_inc(bg_free, 1)
                dve.wait_ge(bg_free, l + 2)
                for a in range(N_ADA0):
                    ada_rows(l, a)
                    ada_columns(l, a)
                coefficients(l, (0,))
                dve.sem_inc(coef_ready, 1)
                pre_norm(l, 0, 0)
                swiglu_in(l, 0)
                scale_y(l, 0, Y_BASE[0])
                ada_rows(l, N_ADA - 1)
                sums(l, 1)
                ada_columns(l, N_ADA - 1)
                coefficients(l, (1, 2))
                dve.sem_inc(coef_ready, 1)
                post_norm(l, 1, 0)
                pre_norm(l, 2, 1)
                dve.wait_ge(p_free, l * 30 + 33)
                dve.wait_ge(bf_full, l * 16 + 16)
                begin()
                V.tensor_tensor(LF[:, 0, :, :], FREG[:, :, 0:NH], BF[:, None, :].to_broadcast([P, TT, NH]), ALU.add).then_inc(logf_arg, 1)
                dve.wait_ge(logf_exp, l + 1)
                V.scalar_tensor_tensor(out=LF[:, 0, :, :], in0=LF[:, 0, :, :], scalar=0.0, in1=LF[:, 2, :, :],
                                       op0=ALU.min, op1=ALU.subtract).then_inc(logf_ready, 1)
                dve.wait_ge(gt_copied, l + 1)
                dve.wait_ge(gn_full, l * 128 + 128)
                begin()
                link(V.memset(GX[0:48, KEYS - 1:KEYS], 0.0))
                reverse_sum(GX[0:48, 0:KEYS - 1], GS[0:48, 1:KEYS], ZERO[0:48, 1:KEYS]).then_inc(g_ready, 1)
                link(V.memset(RSTD[0:NH, NPROMPT - 1:NPROMPT], 0.0))
                reverse_sum(RSTD[0:NH, 0:NPROMPT - 1], VAR[0:NH, 1:NPROMPT], ZERO[0:NH, 1:NPROMPT]).then_inc(g_ready, 1)
                dve.wait_ge(g_stored, l * 32 + 32)
                for tt in range(TT):
                    rotate(QK[:, DSA, tt, :], 2 * NH, tt)
                    rotate(IDX[:, tt, 0:5 * HD], 5, tt)
                dve.sem_inc(rope_done, 1)
                dve.wait_ge(qk_free, l * 15 + 17)
                dve.wait_ge(stored, l * 208 + 208)
                for z in range(2):
                    link(V.tensor_copy(KI2[:, :, z * HD:(z + 1) * HD], IDX[:, :, IH * HD:(IH + 1) * HD]))
                    link(V.tensor_copy(QI2[:, :, z * HD:(z + 1) * HD], IDX[:, 2, 0:IH * HD].rearrange("p (h d) -> p h d", h=IH)))
                dve.sem_inc(dup_ready, 1)
                V.memset(QIP, 0.0).then_inc(qip_zero, 1)
                for qt in range(2):
                    begin()
                    w = IDX[:, qt, (IH + 1) * HD:]
                    dve.wait_ge(relu_ready, l * 6 + (qt + 1))
                    dve.wait_ge(qip_zero, l + 1)
                    link(V.tensor_scalar(ISC[:, 0:256], RL[:, 0:256], w[:, 0:1], None, ALU.mult))
                    for h in range(1, IH):
                        ins = V.scalar_tensor_tensor(out=ISC[:, 0:256], in0=by_parity(RL, h, IH, 256), scalar=w[:, h:h + 1],
                                                     in1=ISC[:, 0:256], op0=ALU.mult, op1=ALU.add)
                        link(ins)
                    dve.sem_inc(relu_free, 1)
                    link(V.tensor_tensor(WK[:, 0:256], ISC[:, 0:256], MASKS[:, 2, qt, :], ALU.add))
                    choose(NPROMPT, TOPK_P // 8, TOPK_P % 8)
                    V.tensor_scalar(DMB[:, qt, :], WK[:, 0:256], TAKEN / 2, NEG, ALU.is_gt, ALU.mult).then_inc(msk_ready, 1)
                    dve.wait_ge(msk_ready, l * 3 + (qt + 1))
                w = IDX[:, 2, (IH + 1) * HD:]
                begin()
                for h in range(IH):
                    dve.wait_ge(relu_ready, l * 6 + (3 + h))
                    if h == 0:
                        link(V.tensor_scalar(WK, RL[:, 0:KEYS], w[:, 0:1], None, ALU.mult))
                    else:
                        link(V.scalar_tensor_tensor(out=WK, in0=RL[:, 0:KEYS], scalar=w[:, h:h + 1], in1=WK,
                                                    op0=ALU.mult, op1=ALU.add))
                    dve.sem_inc(relu_free, 1)
                choose(KEYS, TOPK_S // 8, TOPK_S % 8)
                V.tensor_scalar(WK, WK, TAKEN / 2, NEG, ALU.is_gt, ALU.mult).then_inc(msk_ready, 1)
                dve.wait_ge(msk_ready, l * 3 + 3)
                dve.wait_ge(kidx_stored, l * 32 + 32)
                dve.sem_inc(is_done, 1)
                for it in range(6):
                    r, qt = it // 2, it % 2
                    begin()
                    dve.wait_ge(s_ready, l * 6 + (it + 1))
                    if r == FOX:
                        dve.wait_ge(gb_full, l * 16 + 16)
                    for z in range(2):
                        S = PS[:, 2 * z:2 * z + 2, :].rearrange("p b (h k) -> p (b h) k", h=2)[:, 0:NPAIR, :]
                        bias = (MASKS[:, 0, qt, :], None, DMB[:, qt, :])[r]
                        bias = GB[:, z::2, :] if r == FOX else bias[:, None, :].to_broadcast([P, NPAIR, NPROMPT])
                        link(V.scalar_tensor_tensor(out=ZP[:, z * NPAIR:(z + 1) * NPAIR, :], in0=S, scalar=SCALE, in1=bias,
                                                    op0=ALU.mult, op1=ALU.add))
                    if r == FOX:
                        link(V.tensor_tensor(ZP, ZP, MASKS[:, 1, qt, :][:, None, :].to_broadcast([P, NH, NPROMPT]), ALU.add))
                    if r == SB:
                        dve.sem_inc(z_ready, 1)
                        dve.wait_ge(e_ready, l * 6 + (it + 1))
                        for h in range(NH):
                            link(reverse_product(ZP[:, h, 0:NPROMPT - 1], LP[:, h, 1:NPROMPT], ZERO[:, 1:NPROMPT]))
                        V.tensor_tensor(EP[:, :, 0:NPROMPT - 1], EP[:, :, 0:NPROMPT - 1], ZP[:, :, 0:NPROMPT - 1],
                                        ALU.mult).then_inc(p_done, 1)
                        dve.wait_ge(p_done, l * 6 + (it + 1))
                    else:
                        link(V.tensor_reduce(ST[:, 0:NH], ZP, AXX, ALU.max, negate=True))
                        dve.sem_inc(z_ready, 1)
                        dve.wait_ge(e_ready, l * 6 + (it + 1))
                        link(V.reciprocal(ST[:, 16:16 + NH], ST[:, 8:8 + NH]))
                        V.tensor_tensor(EP, EP, ST[:, 16:16 + NH][..., None].to_broadcast([P, NH, NPROMPT]), ALU.mult).then_inc(p_done, 1)
                        dve.wait_ge(p_done, l * 6 + (it + 1))
                dve.wait_ge(po_copied, l * 6 + 6)
                dve.wait_ge(gate_taken, l * 24 + 24)
                def output(b0, j):
                    b, r = b0 + j // 3, j % 3
                    dve.wait_ge(o_ready, l * NSTEP + b0 * 3 + (j + 1))
                    src = PS[:, 7, P:P + 96].rearrange("p (a c) -> p a c", a=NPAIR)
                    o = OT[:, 3 * r:3 * r + 3, bass.ds(b * NT + NPROMPT, NT)]
                    V.tensor_copy(o[0:64], src[0:64, :, 0:NT])
                    V.tensor_copy(o[64:128], src[64:128, :, NT:2 * NT]).then_inc(o_free, 1)

                def turned_probs(b0, j):
                    dve.wait_ge(st_ready, l * NSTEP + b0 * 3 + (j + 1))
                    V.tensor_copy(PTS[:, 0:PC, :], PS[:, 6, 0:384].rearrange("p (c q) -> p c q", q=96))
                    V.tensor_copy(PTS[0:NT, PC, :], PS[0:NT, 6, 384:480]).then_inc(st_copied, 1)

                def output_rows(b0, j):
                    dve.wait_ge(pv_ready, l * NSTEP + b0 * 3 + (j + 3))
                    V.tensor_copy(OU[0:96, :], PS[0:96, 7, 0:P]).then_inc(ou_ready, 1)

                def queries(b0, j):
                    b, r = b0 + j // 3, j % 3
                    V.tensor_copy(QC[:, j % 2, :].rearrange("p (a c) -> p a c", a=NPAIR), QBLK[:, r, :, b, :]).then_inc(qc_ready, 1)

                def step(b0, j):
                    b, r = b0 + j // 3, j % 3
                    st = l * NSTEP + b0 * 3 + j
                    e = ES[j % 2]

                    begin()
                    dve.wait_ge(ss_ready, st + 1)
                    if r == FOX:
                        dve.wait_ge(bfx_full, l * (NB * 96) + b * 96 + 96)
                    if r == DSA:
                        dve.wait_ge(bdx_full, l * (NB * 96) + b * 96 + 96)
                    bias = (BSB, BFX, BDX)[r][0:96, :].rearrange("p (s k) -> p s k", s=2)
                    link(V.scalar_tensor_tensor(out=ZS[0:96, :].rearrange("p (s k) -> p s k", s=2), in0=PS[0:96, 4:6, 0:264],
                                                scalar=SCALE, in1=bias, op0=ALU.mult, op1=ALU.add))
                    if r == FOX:
                        link(V.tensor_tensor(ZS[0:96, PAST:KEYS], ZS[0:96, PAST:KEYS], MFOX[0:96, :], ALU.add))
                    if r != SB:
                        link(V.tensor_reduce(ST[0:96, 0:1], ZS[0:96, :], AXX, ALU.max, negate=True))
                    dve.sem_inc(zs_ready, 1)
                    if has(b0, j + 1):
                        queries(b0, j + 1)
                    if has(b0, j - 2):
                        output(b0, j - 2)
                    if has(b0, j - 1):
                        turned_probs(b0, j - 1)
                    dve.wait_ge(es_ready, st + 1)
                    if r == SB:
                        link(reverse_product(ZS[0:96, 0:KEYS - 1], LS[0:96, 1:KEYS], ZERO[0:96, 1:KEYS]))
                        V.tensor_tensor(e[0:96, 0:KEYS - 1], e[0:96, 0:KEYS - 1], ZS[0:96, 0:KEYS - 1], ALU.mult).then_inc(ps_ready, 1)
                    else:
                        link(V.reciprocal(ST[0:96, 16:17], ST[0:96, 8:9]))
                        V.tensor_scalar(e[0:96, :], e[0:96, :], ST[0:96, 16:17], None, ALU.mult).then_inc(ps_ready, 1)
                    if has(b0, j - 1):
                        output_rows(b0, j - 1)
                    dve.wait_ge(ps_ready, st + 1)

                begin()
                queries(0, 0)
                sweep(dve, step)
                output(NB - 2, 4)
                turned_probs(NB - 2, 5)
                output_rows(NB - 2, 5)
                output(NB - 2, 5)
                dve.wait_ge(o_free, l * 24 + 25)
                with loop(dve, 0, KD) as m:
                    begin()
                    for n in range(NBR):
                        dve.wait_ge(br_ready, l * 24 + m * 3 + (n + 1))
                        g = G[:, m + n * KD, :]
                        dst = MG[:, m, :] if n == 0 else MGT
                        V.tensor_tensor(dst, PS[:, n, 0:T], g, ALU.mult).then_inc(br_free, 1)
                        dve.wait_ge(br_free, l * 24 + m * 3 + (n + 4))
                        if n:
                            link(V.tensor_tensor(MG[:, m, :], MG[:, m, :], MGT, ALU.add))
                    dve.sem_inc(mg_ready, 1)
                scale_y(l, 1, Y_BASE[2])
                sums(l, 3)
                post_norm(l, 3, 1)
                pre_norm(l, 4, 2)
                swiglu_in(l, 1)
                scale_y(l, 2, Y_BASE[1])
                sums(l, 5)
                post_norm(l, 5, 2)


_INS = ["x_prompt", "x_sample", "cache_sb_k", "cache_sb_v", "cache_fox_k", "cache_fox_v", "cache_fox_logf",
        "cache_dsa_k", "cache_dsa_v", "cache_dsa_kidx", "c_prompt", "c_sample", "norm_g", "w_ada", "b_ada",
        "ffn_w_in", "ffn_w_out", "w_in", "b_forget", "w_branch", "w_out"]
_P, _S = (DEPTH, 1, NPROMPT), (DEPTH, NB, NT)
_STATE = [("sb_k", (NH, HD)), ("sb_v", (NH, HD)), ("fox_k", (NH, HD)), ("fox_v", (NH, HD)), ("fox_logf", (NH,)),
          ("dsa_k", (NH, HD)), ("dsa_v", (NH, HD)), ("dsa_kidx", (HD,))]
_OUTS = ([("o_y_p", (1, NPROMPT, D)), ("o_y_s", (NB, NT, D))]
         + [(f"o_{n}_p", _P + s) for n, s in _STATE] + [(f"o_{n}_s", _S + s) for n, s in _STATE])


def shape_constants():
    import numpy as np
    q = np.arange(NPROMPT).reshape(2, P, 1)
    k = np.arange(NPROMPT).reshape(1, 1, NPROMPT)
    masks = np.stack([np.where(k < q, 0, NEG), np.where(k <= q, 0, NEG), np.where(k // 64 <= q // 64, 0, NEG)])
    pos = np.concatenate([np.arange(NPROMPT), np.tile(PAST + np.arange(NT), NB)]).astype(np.float32)
    inv = np.float32(10000.0) ** (-np.arange(32, dtype=np.float32) / np.float32(32))
    ang = (pos[:, None] * inv[None, :]).astype(np.float32)
    rope = np.stack([np.cos(ang), np.sin(ang)], 1).reshape(TT, P, 2, 32)
    tq = np.tile(np.arange(NT), NH)[:, None]
    tk = np.arange(NT)[None, :]
    bsb = np.zeros((NH * NT, KEYS))
    bsb[:, PAST:] = np.where(tk < tq, 0, NEG)
    arrays = {
        "k_masks": masks.transpose(2, 0, 1, 3), "k_ident": np.eye(P), "k_rope": rope.transpose(1, 0, 2, 3),
        "k_bsb": bsb, "k_mfox": np.where(tk <= tq, 0, NEG),
    }
    return {n: np.ascontiguousarray(a, dtype=np.float32) for n, a in arrays.items()}


def kernel(**inputs):
    import numpy as _np
    import concourse.bacc as _bacc
    from concourse import mybir as _mybir
    from concourse.bass_utils import run_bass_kernel_spmd as _run

    nc = _bacc.Bacc("TRN2", target_bir_lowering=False, num_devices=1)
    arrays = {n: _np.ascontiguousarray(inputs[n]) for n in _INS}
    arrays.update(shape_constants())
    t = {n: nc.dram_tensor(n, a.shape, _mybir.dt.from_np(a.dtype), kind="ExternalInput").ap() for n, a in arrays.items()}
    t.update({n: nc.dram_tensor(n, s, F32, kind="ExternalOutput").ap() for n, s in _OUTS})
    program(nc, t)
    r = _run(nc, [arrays], core_ids=[0])
    return tuple(r.results[0][n] for n, _ in _OUTS)
```
